# Optimizing a Trainium2 kernel written in Bass

```python
import jax, jax.numpy as jnp
from jax import lax
import numpy as np

D_MODEL = 1024
BATCH = 1
SEQ = 1024
DEPTH = 2
DEC_BATCH = 8
DEC_SEQ = 1
PAST_LEN = 1024
PAGE_SIZE = 128

GROUP_W = D_MODEL // 4
EPS = 1e-6
NEG_BIG = -1e30
LRU_W = GROUP_W
LRU_BLOCKS = 4
LRU_BD = LRU_W // LRU_BLOCKS
CONV_W = 4
LRU_C = 8.0
ATT_HEADS = 4
ATT_KV_HEADS = 2
ATT_GROUPS = ATT_HEADS // ATT_KV_HEADS
HEAD_DIM = GROUP_W // ATT_HEADS
ROT_DIM = HEAD_DIM // 4
ROPE_THETA = 500000.0
WINDOW = 128
HG_HEADS = 4
HG_DK = GROUP_W // HG_HEADS
HG_DV = GROUP_W // HG_HEADS
ML_HEADS = 4
ML_D = GROUP_W // ML_HEADS
CHUNK = 64
D_FF = 4 * D_MODEL
PLE_DIM = 256

IN_SIZES = (LRU_W, LRU_W,
            ATT_HEADS * HEAD_DIM, ATT_KV_HEADS * HEAD_DIM, ATT_KV_HEADS * HEAD_DIM,
            GROUP_W, GROUP_W, GROUP_W, GROUP_W,
            GROUP_W, GROUP_W, GROUP_W, GROUP_W, ML_HEADS, ML_HEADS)
D_IN = sum(IN_SIZES)
SPLIT_IDX = tuple(int(v) for v in np.cumsum(IN_SIZES)[:-1])

kernel_name = 'hybrid_rglru_swa_hgrn2_mlstm_step'

F32 = jnp.float32

def _rmsnorm(x, g):
    xf = x.astype(F32)
    y = xf * lax.rsqrt(jnp.mean(xf * xf, axis=-1, keepdims=True) + EPS)
    return (y * g.astype(F32)).astype(x.dtype)

def _rope(x, pos):
    half = ROT_DIM // 2
    inv = jnp.power(ROPE_THETA, -jnp.arange(half, dtype=F32) * (2.0 / ROT_DIM))
    ang = pos.astype(F32)[:, None] * inv[None, :]
    cos = jnp.cos(ang)[None, :, None, :]
    sin = jnp.sin(ang)[None, :, None, :]
    xf = x.astype(F32)
    x1, x2, rest = xf[..., :half], xf[..., half:ROT_DIM], xf[..., ROT_DIM:]
    return jnp.concatenate([x1 * cos - x2 * sin, x2 * cos + x1 * sin, rest], axis=-1).astype(x.dtype)

def _lin_comb(left, right):
    a1, b1 = left
    a2, b2 = right
    return a1 * a2, a2 * b1 + b2

def _rglru(xa, ga, h0, conv0, conv_w, conv_b, wr, br, wi, bi, lam):
    bsz, t, _ = xa.shape
    xp = jnp.concatenate([conv0.astype(xa.dtype), xa], axis=1)
    xc = conv_b
    for j in range(CONV_W):
        xc = xc + xp[:, j:j + t] * conv_w[j]
    xh = xc.reshape(bsz, t, LRU_BLOCKS, LRU_BD)
    r = jax.nn.sigmoid(jnp.einsum('bthi,hij->bthj', xh, wr).reshape(bsz, t, LRU_W) + br)
    ig = jax.nn.sigmoid(jnp.einsum('bthi,hij->bthj', xh, wi).reshape(bsz, t, LRU_W) + bi)
    log_a = -LRU_C * r.astype(F32) * jax.nn.softplus(-lam.astype(F32))
    a = jnp.exp(log_a)
    bx = jnp.sqrt(-jnp.expm1(2.0 * log_a)) * (ig * xc).astype(F32)
    a_cum, b_cum = lax.associative_scan(_lin_comb, (a, bx), axis=1)
    h = a_cum * h0.astype(F32)[:, None, :] + b_cum
    y = h.astype(xa.dtype) * jax.nn.gelu(ga)
    return y, h[:, -1].astype(h0.dtype), xp[:, -(CONV_W - 1):]

def _sink_softmax(s, sinks):
    sk = jnp.broadcast_to(sinks.astype(F32).reshape(ATT_KV_HEADS, ATT_GROUPS, 1, 1), s.shape[:-1] + (1,))
    return jax.nn.softmax(jnp.concatenate([s, sk], axis=-1), axis=-1)[..., :-1]

def _swa_prompt(q, k, v, sinks):
    bsz, t = q.shape[:2]
    nb = t // WINDOW
    qb = q.reshape(bsz, nb, WINDOW, ATT_KV_HEADS, ATT_GROUPS, HEAD_DIM)

    def band(a):
        ap = jnp.pad(a, ((0, 0), (WINDOW, 0), (0, 0), (0, 0))).reshape(bsz, nb + 1, WINDOW, ATT_KV_HEADS, HEAD_DIM)
        return jnp.concatenate([ap[:, :-1], ap[:, 1:]], axis=2)

    kb, vb = band(k), band(v)
    s = jnp.einsum('bnqkgd,bnskd->bnkgqs', qb, kb).astype(F32) * (HEAD_DIM ** -0.5)
    qi = jnp.arange(WINDOW)[:, None]
    kj = jnp.arange(2 * WINDOW)[None, :]
    rel = qi + WINDOW - kj
    kpos = jnp.arange(nb)[:, None, None] * WINDOW - WINDOW + kj[None]
    mask = (rel >= 0)[None] & (rel < WINDOW)[None] & (kpos >= 0)
    s = jnp.where(mask[None, :, None, None], s, NEG_BIG)
    pr = _sink_softmax(s, sinks).astype(v.dtype)
    o = jnp.einsum('bnkgqs,bnskd->bnqkgd', pr, vb)
    return o.reshape(bsz, t, ATT_HEADS * HEAD_DIM)

def _swa_sample(q, k, v, kbuf, vbuf, sinks, pos):
    bsz, t = q.shape[:2]
    wb = kbuf.shape[1]
    kk = jnp.concatenate([kbuf.astype(k.dtype), k], axis=1)
    vv = jnp.concatenate([vbuf.astype(v.dtype), v], axis=1)
    qg = q.reshape(bsz, t, ATT_KV_HEADS, ATT_GROUPS, HEAD_DIM)
    s = jnp.einsum('btkgd,bskd->bkgts', qg, kk).astype(F32) * (HEAD_DIM ** -0.5)
    kpos = pos[0] - wb + jnp.arange(wb + t)
    rel = pos[:, None] - kpos[None, :]
    mask = (rel >= 0) & (rel < WINDOW)
    s = jnp.where(mask, s, NEG_BIG)
    pr = _sink_softmax(s, sinks).astype(v.dtype)
    o = jnp.einsum('bkgts,bskd->btkgd', pr, vv).reshape(bsz, t, ATT_HEADS * HEAD_DIM)
    return o, kk[:, t:], vv[:, t:]

def _chunked_scan(step, carry, xs):
    t = xs[0].shape[1]
    l = CHUNK if t % CHUNK == 0 else t
    nc = t // l

    def to_chunks(a):
        return jnp.moveaxis(a.reshape((a.shape[0], nc, l) + a.shape[2:]), 1, 0)

    carry, ys = lax.scan(step, carry, tuple(to_chunks(a) for a in xs))
    ys = jnp.moveaxis(ys, 0, 1)
    return ys.reshape((ys.shape[0], t) + ys.shape[3:]), carry

def _hgrn2_chunk(s0, inp):
    q, k, logf, v = inp
    l = q.shape[1]
    qf, kf, vf = q.astype(F32), k.astype(F32), v.astype(F32)
    b = jnp.cumsum(logf.astype(F32), axis=1)
    causal = jnp.tril(jnp.ones((l, l), dtype=bool))
    diff = b[:, :, None] - b[:, None, :]
    decay = jnp.exp(jnp.where(causal[None, :, :, None, None], diff, NEG_BIG))
    att = jnp.einsum('bthd,bshd,btshd->btsh', qf, kf, decay)
    s0f = s0.astype(F32)
    o = jnp.einsum('bthd,bhde->bthe', qf * jnp.exp(b), s0f) + jnp.einsum('btsh,bshe->bthe', att, vf)
    b_end = b[:, -1]
    s_new = jnp.exp(b_end)[..., None] * s0f + jnp.einsum('bshd,bshe->bhde', kf * jnp.exp(b_end[:, None] - b), vf)
    return s_new.astype(s0.dtype), o.astype(q.dtype)

def _hgrn2(cq, cf, ci, cg, lb, s0, norm_g):
    bsz, t, _ = cq.shape
    q = jax.nn.silu(cq).reshape(bsz, t, HG_HEADS, HG_DK)
    lbf = lb.astype(F32).reshape(HG_HEADS, HG_DK)
    f = lbf + (1.0 - lbf) * jax.nn.sigmoid(cf.astype(F32).reshape(bsz, t, HG_HEADS, HG_DK))
    logf = jnp.log(f)
    k = 1.0 - f
    v = ci.reshape(bsz, t, HG_HEADS, HG_DV)
    o, s_new = _chunked_scan(_hgrn2_chunk, s0, (q, k, logf, v))
    o = _rmsnorm(o, norm_g).reshape(bsz, t, GROUP_W) * jax.nn.silu(cg)
    return o, s_new

def _mlstm_chunk(carry, inp):
    c0, n0, m0 = carry
    q, k, v, ig, logf = inp
    l = q.shape[1]
    qf, kf, vf = q.astype(F32), k.astype(F32), v.astype(F32)
    c0f, n0f, m0f = c0.astype(F32), n0.astype(F32), m0.astype(F32)
    causal = jnp.tril(jnp.ones((l, l), dtype=bool))
    fcum = jnp.cumsum(logf, axis=1)
    a_inter = fcum + m0f[:, None, :]
    dmat = fcum[:, :, None, :] - fcum[:, None, :, :] + ig[:, None, :, :]
    dmat = jnp.where(causal[None, :, :, None], dmat, NEG_BIG)
    m_t = jnp.maximum(a_inter, jnp.max(dmat, axis=2))
    wmat = jnp.exp(dmat - m_t[:, :, None, :])
    s = jnp.einsum('bthd,bshd->btsh', qf, kf) * wmat
    inter = jnp.exp(a_inter - m_t)
    num = inter[..., None] * jnp.einsum('bthd,bhde->bthe', qf, c0f) + jnp.einsum('btsh,bshe->bthe', s, vf)
    den = inter * jnp.einsum('bthd,bhd->bth', qf, n0f) + jnp.sum(s, axis=2)
    h = num / jnp.maximum(jnp.abs(den), jnp.exp(-m_t))[..., None]
    g_end = fcum[:, -1:, :] - fcum + ig
    f_end = fcum[:, -1] + m0f
    m_new = jnp.maximum(f_end, jnp.max(g_end, axis=1))
    w_end = jnp.exp(g_end - m_new[:, None])
    decay0 = jnp.exp(f_end - m_new)
    c_new = decay0[..., None, None] * c0f + jnp.einsum('bsh,bshd,bshe->bhde', w_end, kf, vf)
    n_new = decay0[..., None] * n0f + jnp.einsum('bsh,bshd->bhd', w_end, kf)
    return (c_new.astype(c0.dtype), n_new.astype(n0.dtype), m_new.astype(m0.dtype)), h.astype(q.dtype)

def _mlstm(dq, dk, dv, do, di, df, ib, fb, c0, n0, m0, norm_g):
    bsz, t, _ = dq.shape
    shp = (bsz, t, ML_HEADS, ML_D)
    q = dq.reshape(shp)
    k = dk.reshape(shp) * (ML_D ** -0.5)
    v = dv.reshape(shp)
    ig = (di + ib).astype(F32)
    logf = jax.nn.log_sigmoid((df + fb).astype(F32))
    hh, (c_new, n_new, m_new) = _chunked_scan(_mlstm_chunk, (c0, n0, m0), (q, k, v, ig, logf))
    y = _rmsnorm(hh, norm_g).reshape(bsz, t, GROUP_W) * jax.nn.sigmoid(do)
    return y, c_new, n_new, m_new

def _layer(h, p_l, lst, w, lb, pos, wbuf, prompt):
    bsz, t, _ = h.shape
    h0, conv0, kbuf, vbuf, s0, c0, n0, m0 = lst
    u = _rmsnorm(h, w['norm1_g']) @ w['w_in']
    (a_x, a_g, b_q, b_k, b_v, c_q, c_f, c_i, c_g,
     d_q, d_k, d_v, d_o, d_i, d_f) = jnp.split(u, SPLIT_IDX, axis=-1)
    y_a, h_new, conv_new = _rglru(a_x, a_g, h0, conv0, w['conv_w'], w['conv_b'], w['lru_wr'],
                                  w['lru_br'], w['lru_wi'], w['lru_bi'], w['lru_lam'])
    q = _rope(_rmsnorm(b_q.reshape(bsz, t, ATT_HEADS, HEAD_DIM), w['q_norm_g']), pos)
    k = _rope(_rmsnorm(b_k.reshape(bsz, t, ATT_KV_HEADS, HEAD_DIM), w['k_norm_g']), pos)
    v = b_v.reshape(bsz, t, ATT_KV_HEADS, HEAD_DIM)
    if prompt:
        y_b = _swa_prompt(q, k, v, w['attn_sinks'])
        k_new, v_new = k[:, t - wbuf:], v[:, t - wbuf:]
    else:
        y_b, k_new, v_new = _swa_sample(q, k, v, kbuf, vbuf, w['attn_sinks'], pos)
    y_c, s_new = _hgrn2(c_q, c_f, c_i, c_g, lb, s0, w['hgrn_norm_g'])
    y_d, c_new, n_new, m_new = _mlstm(d_q, d_k, d_v, d_o, d_i, d_f, w['mlstm_ib'], w['mlstm_fb'],
                                      c0, n0, m0, w['mlstm_norm_g'])
    h = h + jnp.concatenate([y_a, y_b, y_c, y_d], axis=-1) @ w['w_out']
    f = _rmsnorm(h, w['norm2_g']) @ w['w_up']
    h = h + jnp.square(jax.nn.relu(f)) @ w['w_down']
    h = h + jax.nn.sigmoid(h @ w['w_ple_gate']) * (p_l @ w['w_ple_proj'])
    return h, (h_new, conv_new, k_new, v_new, s_new, c_new, n_new, m_new)

def _run_group(x, p, st, wts, lbs, pos, wbuf, prompt):
    bsz = x.shape[0]
    dt = x.dtype
    h = x
    outs = [[] for _ in range(8)]
    for l in range(DEPTH):
        if prompt:
            lst = (jnp.zeros((bsz, LRU_W), dt), jnp.zeros((bsz, CONV_W - 1, LRU_W), dt), None, None,
                   jnp.zeros((bsz, HG_HEADS, HG_DK, HG_DV), dt), jnp.zeros((bsz, ML_HEADS, ML_D, ML_D), dt),
                   jnp.zeros((bsz, ML_HEADS, ML_D), dt), jnp.zeros((bsz, ML_HEADS), dt))
        else:
            lst = tuple(s[l] for s in st)
        lw = {name: arr[l] for name, arr in wts.items()}
        h, new = _layer(h, p[l], lst, lw, lbs[l], pos, wbuf, prompt)
        for o, n in zip(outs, new):
            o.append(n)
    return h, tuple(jnp.stack(o) for o in outs)

def setup_inputs(seed: int = 0) -> dict:
    key = jax.random.key(seed)
    ks = iter(jax.random.split(key, 48))

    def nrm(shape, scale):
        return scale * jax.random.normal(next(ks), shape, jnp.float32)

    wbuf = min(WINDOW, PAST_LEN)
    lam_u = jax.random.uniform(next(ks), (DEPTH, LRU_W), jnp.float32, 0.9, 0.999)
    return {
        'x_prompt': nrm((BATCH, SEQ, D_MODEL), 1.0),
        'x_sample': nrm((DEC_BATCH, DEC_SEQ, D_MODEL), 1.0),
        'p_prompt': nrm((DEPTH, BATCH, SEQ, PLE_DIM), 1.0),
        'p_sample': nrm((DEPTH, DEC_BATCH, DEC_SEQ, PLE_DIM), 1.0),
        'state_rglru_h': nrm((DEPTH, DEC_BATCH, LRU_W), 0.5),
        'state_rglru_conv': nrm((DEPTH, DEC_BATCH, CONV_W - 1, LRU_W), 1.0),
        'cache_swa_k': nrm((DEPTH, DEC_BATCH, wbuf, ATT_KV_HEADS, HEAD_DIM), 1.0),
        'cache_swa_v': nrm((DEPTH, DEC_BATCH, wbuf, ATT_KV_HEADS, HEAD_DIM), 1.0),
        'state_hgrn_s': nrm((DEPTH, DEC_BATCH, HG_HEADS, HG_DK, HG_DV), 0.5),
        'state_mlstm_c': nrm((DEPTH, DEC_BATCH, ML_HEADS, ML_D, ML_D), 0.3),
        'state_mlstm_n': nrm((DEPTH, DEC_BATCH, ML_HEADS, ML_D), 0.3),
        'state_mlstm_m': nrm((DEPTH, DEC_BATCH, ML_HEADS), 1.0),
        'norm1_g': 1.0 + nrm((DEPTH, D_MODEL), 0.05),
        'w_in': nrm((DEPTH, D_MODEL, D_IN), D_MODEL ** -0.5),
        'conv_w': nrm((DEPTH, CONV_W, LRU_W), CONV_W ** -0.5),
        'conv_b': nrm((DEPTH, LRU_W), 0.02),
        'lru_wr': nrm((DEPTH, LRU_BLOCKS, LRU_BD, LRU_BD), LRU_BD ** -0.5),
        'lru_br': nrm((DEPTH, LRU_W), 0.02),
        'lru_wi': nrm((DEPTH, LRU_BLOCKS, LRU_BD, LRU_BD), LRU_BD ** -0.5),
        'lru_bi': nrm((DEPTH, LRU_W), 0.02),
        'lru_lam': jnp.log(lam_u) - jnp.log1p(-lam_u),
        'q_norm_g': 1.0 + nrm((DEPTH, HEAD_DIM), 0.05),
        'k_norm_g': 1.0 + nrm((DEPTH, HEAD_DIM), 0.05),
        'attn_sinks': nrm((DEPTH, ATT_HEADS), 0.5),
        'hgrn_gamma': nrm((DEPTH, HG_HEADS * HG_DK), 1.0),
        'hgrn_norm_g': 1.0 + nrm((DEPTH, HG_DV), 0.05),
        'mlstm_ib': nrm((DEPTH, ML_HEADS), 0.1),
        'mlstm_fb': jnp.linspace(3.0, 6.0, ML_HEADS, dtype=jnp.float32)[None] + nrm((DEPTH, ML_HEADS), 0.1),
        'mlstm_norm_g': 1.0 + nrm((DEPTH, ML_D), 0.05),
        'w_out': nrm((DEPTH, D_MODEL, D_MODEL), D_MODEL ** -0.5),
        'norm2_g': 1.0 + nrm((DEPTH, D_MODEL), 0.05),
        'w_up': nrm((DEPTH, D_MODEL, D_FF), D_MODEL ** -0.5),
        'w_down': nrm((DEPTH, D_FF, D_MODEL), D_FF ** -0.5),
        'w_ple_gate': nrm((DEPTH, D_MODEL, D_MODEL), D_MODEL ** -0.5),
        'w_ple_proj': nrm((DEPTH, PLE_DIM, D_MODEL), PLE_DIM ** -0.5),
    }

def reference(x_prompt, x_sample, p_prompt, p_sample, state_rglru_h, state_rglru_conv, cache_swa_k,
              cache_swa_v, state_hgrn_s, state_mlstm_c, state_mlstm_n, state_mlstm_m, norm1_g, w_in,
              conv_w, conv_b, lru_wr, lru_br, lru_wi, lru_bi, lru_lam, q_norm_g, k_norm_g, attn_sinks,
              hgrn_gamma, hgrn_norm_g, mlstm_ib, mlstm_fb, mlstm_norm_g, w_out, norm2_g, w_up, w_down,
              w_ple_gate, w_ple_proj):
    wts = {'norm1_g': norm1_g, 'w_in': w_in, 'conv_w': conv_w, 'conv_b': conv_b, 'lru_wr': lru_wr,
           'lru_br': lru_br, 'lru_wi': lru_wi, 'lru_bi': lru_bi, 'lru_lam': lru_lam,
           'q_norm_g': q_norm_g, 'k_norm_g': k_norm_g, 'attn_sinks': attn_sinks,
           'hgrn_norm_g': hgrn_norm_g, 'mlstm_ib': mlstm_ib, 'mlstm_fb': mlstm_fb,
           'mlstm_norm_g': mlstm_norm_g, 'w_out': w_out, 'norm2_g': norm2_g, 'w_up': w_up,
           'w_down': w_down, 'w_ple_gate': w_ple_gate, 'w_ple_proj': w_ple_proj}
    pf = jax.nn.softmax(hgrn_gamma.astype(F32), axis=0)
    lbs = jnp.cumsum(pf, axis=0) - pf[:1]
    wbuf = cache_swa_k.shape[2]
    pos_p = jnp.arange(x_prompt.shape[1])
    pos_s = PAST_LEN + jnp.arange(x_sample.shape[1])
    y_prompt, st_p = _run_group(x_prompt, p_prompt, None, wts, lbs, pos_p, wbuf, True)
    st_in = (state_rglru_h, state_rglru_conv, cache_swa_k, cache_swa_v, state_hgrn_s,
             state_mlstm_c, state_mlstm_n, state_mlstm_m)
    y_sample, st_s = _run_group(x_sample, p_sample, st_in, wts, lbs, pos_s, wbuf, False)
    (p_h, p_conv, p_k, p_v, p_s, p_c, p_n, p_m) = st_p
    (s_h, s_conv, s_k, s_v, s_s, s_c, s_n, s_m) = st_s
    return (y_prompt, y_sample, p_h, p_conv, p_k, p_v, p_s, p_c, p_n, p_m,
            s_h, s_conv, s_k, s_v, s_s, s_c, s_n, s_m)


_drawn_inputs = setup_inputs


def setup_inputs(seed=0):
    import zlib

    import numpy as np

    out = dict(_drawn_inputs(seed))
    spreads = {}
    factors = {'lru_br': 8.0,
     'lru_bi': 7.545,
     'q_norm_g': 8.0,
     'attn_sinks': 31.423,
     'hgrn_norm_g': 3.28,
     'mlstm_norm_g': 3.583}
    for name, (base, spread) in spreads.items():
        noise = np.random.default_rng([zlib.crc32(name.encode()), seed]).standard_normal(out[name].shape)
        drawn = base * np.exp(spread * noise) if base else spread * noise
        out[name] = __import__('jax').numpy.asarray(drawn.astype(out[name].dtype))
    for name, factor in factors.items():
        out[name] = (out[name] * factor).astype(out[name].dtype)
    return out
```

```python
from contextlib import ExitStack

import numpy as np

import concourse.bass as bass
from concourse import mybir

ALU = mybir.AluOpType
ACT = mybir.ActivationFunctionType
AX_X = mybir.AxisListType.X
F32 = mybir.dt.float32
F32R = mybir.dt.float32r
U32 = mybir.dt.uint32

P = 128
LAYERS, SEQ, DEC, D, D_FF, PLE = 2, 1024, 8, 1024, 4096, 256
T = SEQ + DEC
TT = T // 3
KT = D // P
CH = 128
NC = SEQ // CH
NLEV = 7
NEG = -1e30
EPS = 1e-6
FF_TILES = 4
FF_STEPS = D_FF // (P * FF_TILES)
WIN = ['gates', 'ax0', 'ax1', 'ag0', 'ag1', 'q0', 'q1', 'k', 'bv', 'ci0', 'ci1', 'dv0', 'dv1',
       'dq0', 'dq1', 'cq0', 'cq1', 'cf0', 'cf1', 'cg0', 'cg1', 'dk0', 'dk1', 'do0', 'do1']
JOB = {name: j for j, name in enumerate(WIN)}
SLOT = dict(ax0=10, ax1=11, ag0=12, ag1=13, q0=14, q1=15, k=16, bv=17, ci0=18, ci1=19, dv0=4, dv1=5,
            dq0=10, dq1=11, cq0=0, cq1=1, cf0=2, cf1=3, cg0=6, cg1=7, dk0=16, dk1=17, do0=18, do1=19)
VT_COL = dict(bv=0, ci0=128, ci1=256, dv0=384, dv1=512)
N_WIN, N_OUT, N_FF, N_PLE = len(WIN), KT, FF_STEPS * 8, KT + 2
N_JOBS = N_WIN + N_OUT + N_FF + N_PLE

LEV_AT = [(0, 128), (0, 192), (2, 0), (2, 64), (2, 128), (2, 192), (0, 0)]

C_ID, C_ONE, C_BLK, C_ROT, C_MD, C_MP, C_MC, C_EYE, C_LEV = 0, 128, 256, 384, 512, 640, 768, 896, 960
C_SEL = C_LEV + NLEV * 64
N_CONST = C_SEL + 2 * P
_sizes = dict(g1=8, g2=8, cw=8, cb=2, br=2, bi=2, lam=2, qg=1, kg=1, hg=1, mg=1, gam=4, lm=1, sink=4,
              sinkc=1, ib=1, fb=1, wr=256, wi=256, conv=48, h0=16, n0=16, m0=8)
PC, N_PAR = {}, 0
for _n, _s in _sizes.items():
    PC[_n] = N_PAR
    N_PAR += _s
_sizes = dict(convp=6, convs=48, hp=2, hs=16, np=2, ns=16, mp=1, ms=8)
OC, N_SO = {}, 0
for _n, _s in _sizes.items():
    OC[_n] = N_SO
    N_SO += _s

ORDER = [('job', 0), ('rows', 0)] + [('job', j) for j in range(1, 5)] + [('conv', 0)]
ORDER += [('job', j) for j in range(5, 9)] + [('gate', 0), ('lru', 0), ('rope', 0), ('vt', 0)]
_fill = [[('job', 9)], [('job', 10)], [('vt', 1)], [('job', 11), ('vt', 2)], [('job', 12)], [('job', 13), ('vt', 3)],
         [('job', 14)], [('vt', 4)]]
for _c in range(NC):
    ORDER += [('attn', _c)] + _fill[_c]
ORDER += [('sattn', 0)] + [('job', j) for j in range(15, 21)] + [('hprep', 0)]
for _c in range(NC):
    ORDER += [('hchunk', _c)] + ([('job', 21 + _c // 4)] if _c % 4 == 3 else [])
ORDER += [('hsample', 0), ('job', 23), ('job', 24), ('hnorm', 0), ('mprep', 0)]
ORDER += [('mchunk', _c) for _c in range(NC)] + [('msample', 0), ('mnorm', 0)]


def build(nc, x_in, consts, rope_in, par_in, w_in, p_in, kc_in, vc_in, hs_in, cs_in,
          y_out, so_out, kv_out, kc_out, vc_out, hp_out, cp_out, hs_out, cs_out):
    with ExitStack() as ctx:
        def sem(name):
            s = ctx.enter_context(nc.semaphore(name))
            sems.append(s)
            return s

        def sb(name, shape, dt=F32, stack=ctx):
            return stack.enter_context(nc.sbuf_tensor(name, shape, dt))

        sems = []
        h_saved = nc.dram_tensor("h_saved", (P, KT, T), F32, kind="Internal").ap()
        pj = ctx.enter_context(nc.psum_tensor("pj", [P, 3, 512], F32))
        pm = ctx.enter_context(nc.psum_tensor("pm", [P, 5, 512], F32))

        res = sb("res", [P, KT, T])
        n_hi, n_lo = sb("n_hi", [P, KT, T], F32R), sb("n_lo", [P, KT, T], F32R)
        w_raw = sb("w_raw", [P, 2, KT * P])
        w_hi, w_lo = sb("w_hi", [P, 2, KT * P], F32R), sb("w_lo", [P, 2, KT * P], F32R)
        cst, par, so = sb("cst", [P, N_CONST]), sb("par", [P, N_PAR]), sb("so", [P, N_SO])
        ex2, qe = sb("ex2", [P, 2, 2, CH]), sb("qe", [P, 2, CH])
        ktok, att = sb("ktok", [P, 2, CH]), sb("att", [P, 4, CH])
        h_st, c_st = sb("h_st", [P, 2, P]), sb("c_st", [P, 2, P])
        n_st = h_st
        v_smp = sb("v_smp", [P, 4, DEC])
        bw = sb("bw", [P, NC, 2, 4])
        tiny = sb("tiny", [P, 48])
        with ExitStack() as mixer:
            ext = sb("ext", [P, 12, T], stack=mixer)
            vt = sb("vt", [P, NC, 640], stack=mixer)
        with ExitStack() as ff:
            hid_hi = sb("hid_hi", [P, FF_TILES, T], F32R, ff)
            hid_lo = sb("hid_lo", [P, FF_TILES, T], F32R, ff)
            relu = sb("relu", [P, 2, T], stack=ff)
            hsq = sb("hsq", [P, 2, T], stack=ff)
        with ExitStack() as ple:
            ple_hi, ple_lo = sb("ple_hi", [P, 2, T], F32R, ple), sb("ple_lo", [P, 2, T], F32R, ple)
            ple_raw = sb("ple_raw", [P, 2, T], stack=ple)
            ple_proj = sb("ple_proj", [P, 4, T], stack=ple)
            ple_sig = sb("ple_sig", [P, T], stack=ple)

        def slot(a, n=1):
            t = res[:, a:a + n, :] if a < KT else ext[:, a - KT:a - KT + n, :]
            return t if n > 1 else t[:, 0, :]

        def flat(a, n=1):
            return (res[:, a:a + n, :] if a < KT else ext[:, a - KT:a - KT + n, :]).rearrange("p a t -> p (a t)")

        def pc(name, i=0, n=1):
            return par[:, PC[name] + i:PC[name] + i + n]

        def oc(name, i=0, n=1):
            return so[:, OC[name] + i:OC[name] + i + n]

        ident, ones, blk = cst[:, 0:P], cst[:, C_ONE:C_ONE + P], cst[:, C_BLK:C_BLK + P]
        rot, mask_d = cst[:, C_ROT:C_ROT + P], cst[:, C_MD:C_MD + P]
        eye, sel = cst[:, C_EYE:C_EYE + 64], cst[:, C_SEL:C_SEL + 2 * P]
        three = "p (a t) -> p a t"
        pm3 = pm[:, 0:3, 0:TT]
        S0 = SEQ

        w_ld = [sem("w_ld0"), sem("w_ld1")]
        hi_made, lo_made = sem("hi_made"), sem("lo_made")
        mm = [sem(f"mm{t}") for t in range(3)]
        ev = [sem(f"ev{t}") for t in range(3)]
        cst_ld, par_ld, rope_ld, h_ld, h_out = (sem(n) for n in ("cst_ld", "par_ld", "rope_ld", "h_ld", "h_out"))
        smp_ld, st_ld, ple_ld = sem("smp_ld"), sem("st_ld"), sem("ple_ld")
        mix_mm, mix_ev = sem("mix_mm"), sem("mix_ev")
        nrm_sq, nrm_mm, nrm_rs, nrm_n = (sem("nrm_" + n) for n in ("sq", "mm", "rs", "n"))
        nrm_hi, nrm_lo = sem("nrm_hi"), sem("nrm_lo")
        rows_a, rows_v, rows_t, rows_c = (sem("rows_" + n) for n in "avtc")
        conv_v, lru_a, lru_v = sem("conv_v"), sem("lru_a"), sem("lru_v")
        rope_a, rope_v = sem("rope_a"), sem("rope_v")
        vt_t, vt_c = sem("vt_t"), sem("vt_c")
        at_s, at_m, at_e, at_p, at_t, at_c, at_o, at_w = (sem("at_" + n) for n in
                                                          ("s", "m", "e", "p", "t", "c", "o", "w"))
        sa_v, sa_t, sa_a, sa_x = sem("sa_v"), sem("sa_t"), sem("sa_a"), sem("sa_x")
        hp_v, hp_a = sem("hp_v"), sem("hp_a")
        hc_sub, hc_exp, hc_kq, hc_lt, hc_lv, hc_tt, hc_tc, hc_ot, hc_oc, hc_sv = (
            sem("hc_" + n) for n in ("sub", "exp", "kq", "lt", "lv", "tt", "tc", "ot", "oc", "sv"))
        ss_v, ss_t, ss_a = sem("ss_v"), sem("ss_t"), sem("ss_a")
        nm_a, nm_v = sem("nm_a"), sem("nm_v")
        mp_a = sem("mp_a")
        mc_t, mc_w, mc_s, mc_tt, mc_k, mc_q, mc_nt, mc_d, mc_h, mc_sv = (
            sem("mc_" + n) for n in ("t", "w", "s", "tt", "k", "q", "nt", "d", "h", "sv"))
        y_hi, y_lo = sem("y_hi"), sem("y_lo")
        ff_r, ff_q, ff_h, ff_l = sem("ff_r"), sem("ff_q"), sem("ff_h"), sem("ff_l")
        ph, pl, pg, pv = sem("ph"), sem("pl"), sem("pg"), sem("pv")
        kv_st, so_st, smp_st, mix_st = sem("kv_st"), sem("so_st"), sem("smp_st"), sem("mix_st")
        ch_a, ch_v, ch_g = sem("ch_a"), sem("ch_v"), sem("ch_g")
        clearable = sems[:]
        clearable.remove(cst_ld)
        arrived, go, left = sem("arrived"), sem("go"), sem("left")
        y_st = sem("y_st")

        def linker(eng, s):
            n = [0]

            def link(ins):
                n[0] += 1
                ins.then_inc(s, 1)
                eng.wait_ge(s, n[0])
            return link

        def layer_end(eng):
            eng.drain().then_inc(arrived, 1)
            eng.wait_ge(go, 1)
            eng.sem_inc(left, 1)

        sm_tmp, st_slot = (18, 7), (19, 6)

        block = ctx.enter_context(nc.Block())

        @block.sync
        def _(sp):
            sp.dma_start(cst[:], consts).then_inc(cst_ld, 16)
            sp.dma_start(res[:], x_in).then_inc(y_st, 16)
            sp.wait_ge(y_st, 16)

            with sp.Fori(0, LAYERS) as l:
                def load(j, wait):
                    if wait:
                        sp.wait_ge(hi_made, j - 1)
                        sp.wait_ge(lo_made, j - 1)
                    sp.dma_start(w_raw[:, j % 2, :], w_in[l, j]).then_inc(w_ld[j % 2], 16)

                sp.dma_start(par[:], par_in[l]).then_inc(par_ld, 16)
                load(0, False)
                load(1, False)
                sp.dma_start(h_saved, res[:]).then_inc(h_out, 16)
                sp.dma_start(slot(18, 2), rope_in).then_inc(rope_ld, 16)
                for j in range(2, N_WIN + N_OUT):
                    load(j, True)
                with sp.Fori(0, FF_STEPS) as i:
                    for q in range(8):
                        j0 = N_WIN + N_OUT + q
                        sp.wait_ge(hi_made, i * 8 + (j0 - 1))
                        sp.wait_ge(lo_made, i * 8 + (j0 - 1))
                        sp.dma_start(w_raw[:, j0 % 2, :], w_in[l, i * 8 + j0]).then_inc(w_ld[j0 % 2], 16)
                for j in range(N_WIN + N_OUT + N_FF, N_JOBS):
                    load(j, True)
                sp.wait_ge(arrived, 4)
                for s in clearable + [arrived]:
                    sp.sem_clear(s)
                sp.sem_inc(go, 4)
                sp.wait_ge(left, 4)
                sp.sem_clear(left)
                sp.sem_clear(go)
            sp.dma_start(y_out, res[:]).then_inc(y_st, 16)
            sp.wait_ge(y_st, 32)

        @block.tensor
        def _(pe):
            def unit(par_j, k0, nk, hi, lo, u, first_waits=None, vals=None):
                for t in range(3):
                    if vals is not None:
                        pe.wait_ge(ev[t], vals)
                    elif u:
                        pe.wait_ge(ev[t], u)
                    cols = slice(t * TT, (t + 1) * TT)
                    for k in range(nk):
                        if first_waits is not None and t == 0:
                            first_waits(k)
                        ws = slice((k0 + k) * P, (k0 + k + 1) * P)
                        wh, wl = w_hi[:, par_j, ws], w_lo[:, par_j, ws]
                        pe.matmul(pj[:, t, 0:TT], wh, hi[:, k, cols], start=(k == 0), stop=False)
                        pe.matmul(pj[:, t, 0:TT], wh, lo[:, k, cols], start=False, stop=False)
                        last = pe.matmul(pj[:, t, 0:TT], wl, hi[:, k, cols], start=False, stop=(k == nk - 1))
                    last.then_inc(mm[t], 1)

            def mix(n, lhs, rhs):
                if n > 1:
                    pe.wait_ge(mix_ev, n - 1)
                for t in range(3):
                    last = pe.matmul(pm[:, t, 0:TT], lhs, rhs[:, t * TT:(t + 1) * TT], start=True, stop=True)
                last.then_inc(mix_mm, 1)

            def norm(i):
                pe.wait_ge(cst_ld, 16)
                if i:
                    pe.wait_ge(mix_ev, 19)
                for k in range(KT):
                    pe.wait_ge(nrm_sq, KT * i + k + 1)
                    for t in range(3):
                        last = pe.matmul(pm[:, t, 0:TT], ones, ext[:, k % 2, t * TT:(t + 1) * TT],
                                         start=(k == 0), stop=(k == KT - 1))
                    last.then_inc(nrm_mm, 1)

            def job(j):
                pe.wait_ge(lo_made, j + 1)
                unit(j % 2, 0, KT, n_hi, n_lo, j,
                     (lambda k: pe.wait_ge(nrm_lo, k + 1)) if j == 0 else None)

            def rows(_):
                pe.wait_ge(rows_v, 9)
                for c in range(NC):
                    pe.matmul(pm[:, 3, c * 8:c * 8 + 4], slot(6)[0:4, c * CH:(c + 1) * CH], ident[0:4, 0:4],
                              is_transpose=True, start=True, stop=True)
                    last = pe.matmul(pm[:, 4, c * 8:c * 8 + 4], slot(6)[32:36, c * CH:(c + 1) * CH],
                                     ident[32:36, 32:36], is_transpose=True, start=True, stop=True)
                last.then_inc(rows_t, 1)

            def gate(_):
                pe.wait_ge(conv_v, 1)
                for n, (w, j) in enumerate((('wr', 0), ('wr', 1), ('wi', 0), ('wi', 1))):
                    if n == 0:
                        pe.wait_ge(nrm_rs, 1)
                    mix_first = n + 1
                    mix(mix_first, pc(w, j * P, P), slot(j))

            def rope(_):
                for n in range(3):
                    pe.wait_ge(rope_a, n + 1)
                    mix(5 + n, blk, slot(n))
                for n in range(3):
                    pe.wait_ge(rope_v, n + 1)
                    mix(8 + n, rot, slot(14 + n))

            def vtrans(v):
                src = slot(SLOT[list(VT_COL)[v]])
                pe.wait_ge(ev[2], JOB[list(VT_COL)[v]] + 1)
                if v == 0:
                    pe.wait_ge(rows_c, 2)
                if attn_before[v]:
                    pe.wait_ge(at_o, attn_before[v])
                for h in range(2):
                    if 2 * v + h >= 1:
                        pe.wait_ge(vt_c, 2 * v + h)
                    for q in range(4):
                        c = 4 * h + q
                        last = pe.transpose(pm[:, 4, q * P:(q + 1) * P], src[:, c * CH:(c + 1) * CH], ident)
                    last.then_inc(vt_t, 1)

            def attn(c):
                if c == 0:
                    pe.wait_ge(mix_ev, 10)
                    pe.wait_ge(rope_v, 6)
                    pe.wait_ge(vt_c, 2)
                lo_k = 0 if c else CH
                if c:
                    pe.wait_ge(at_m, c)
                for j in range(2):
                    for hh in range(2):
                        r = slice(64 * hh, 64 * hh + 64)
                        last = pe.matmul(pm[:, hh, j * 256 + lo_k:j * 256 + 256], slot(14 + j)[r, c * CH:(c + 1) * CH],
                                         slot(16)[r, (c - 1) * CH + lo_k:(c + 1) * CH], start=True, stop=True)
                last.then_inc(at_s, 1)
                pe.wait_ge(at_p, c + 1)
                if c:
                    pe.wait_ge(at_c, c)
                sc = flat(0)[:, 0:1024].rearrange("p (i s) -> p i s", i=4)
                for i in range(4):
                    for h in range(0 if c else 1, 2):
                        last = pe.transpose(pm[:, 2 + i // 2, (i % 2 * 2 + h) * P:(i % 2 * 2 + h + 1) * P],
                                            sc[:, i, h * CH:(h + 1) * CH], ident)
                last.then_inc(at_t, 1)
                pe.wait_ge(at_c, c + 1)
                pt = flat(2)[:, 0:1024].rearrange("p (i h t) -> p i h t", i=4, h=2)
                pe.wait_ge(vt_c, vt_before[c])
                if c:
                    pe.wait_ge(at_o, c)
                for j in range(2):
                    for hh in range(2):
                        for h in range(0 if c else 1, 2):
                            last = pe.matmul(pm[64 * hh:64 * hh + 64, 4, j * CH:(j + 1) * CH],
                                             vt[:, c - 1 + h, 64 * hh:64 * hh + 64], pt[:, 2 * hh + j, h, :],
                                             start=(h == (0 if c else 1)), stop=(h == 1))
                last.then_inc(at_w, 1)

            vt_before, attn_before, n, m = {}, {}, 0, 0
            for what, i in ORDER:
                if what == 'vt':
                    n, attn_before[i] = n + 2, m
                if what == 'attn':
                    vt_before[i], m = n, m + 1

            def sattn(_):
                pe.wait_ge(at_o, NC)
                pe.wait_ge(sa_v, 1)
                pe.wait_ge(vt_c, 10)
                for b in range(DEC):
                    last = pe.matmul(pm[0:1, b // 4, (b % 4) * P:(b % 4 + 1) * P], slot(17)[:, S0 + b:S0 + b + 1],
                                     ident, start=True, stop=True)
                last.then_inc(sa_t, 1)
                kc = flat(6)[:, 0:1024].rearrange("p (b s) -> p b s", b=DEC)
                qb = flat(0)[:, 0:32].rearrange("p (b i) -> p b i", b=DEC)
                for b in range(DEC):
                    last = pe.matmul(pm[0:4, 2 + b // 4, (b % 4) * P:(b % 4 + 1) * P], qb[:, b, :], kc[:, b, :],
                                     start=True, stop=True)
                last.then_inc(sa_t, 1)
                pe.wait_ge(sa_v, 2)
                pr = flat(2)[0:4, 0:1024].rearrange("p (b s) -> p b s", b=DEC)
                for b in range(DEC):
                    last = pe.transpose(pm[:, 4, b * 4:b * 4 + 4], pr[:, b, :], ident[0:4, 0:4])
                last.then_inc(sa_t, 1)
                pe.wait_ge(sa_v, 3)
                pe.wait_ge(sa_a, 1)
                vc = flat(7)[:, 0:1024].rearrange("p (b d) -> p b d", b=DEC)
                for b in range(DEC):
                    last = pe.matmul(pm[:, 4, 64 + b * 4:64 + b * 4 + 4], vc[:, b, :], flat(3)[:, b * 4:b * 4 + 4],
                                     start=True, stop=True)
                last.then_inc(sa_t, 1)

            def hchunk(c):
                el = flat(18, 2)[:, 0:NLEV * 256].rearrange("p (l j t) -> p l j t", l=NLEV, j=2)
                if c == 0:
                    pe.wait_ge(sa_v, 4)
                    pe.wait_ge(hp_v, 1)
                else:
                    pe.wait_ge(hc_lv, 8 * c)
                q, k = slot(0, 2), slot(4, 2)
                cc = slice(c * CH, (c + 1) * CH)
                for j in range(2):
                    for hh in range(2):
                        r = slice(64 * hh, 64 * hh + 64)
                        pe.matmul(pm[:, hh, j * 256:j * 256 + 128], k[r, j, cc], q[r, j, cc], start=True, stop=True)
                pe.wait_ge(hc_kq, c + 1)
                for l in range(NLEV):
                    bank, at, half = LEV_AT[l][0], LEV_AT[l][1], 1 << l
                    if l == 2 and c:
                        pe.wait_ge(hc_oc, c)
                        pe.wait_ge(hc_sv, c)
                    if l == 6:
                        pe.wait_ge(hc_lv, 8 * c + 3)
                    for j in range(2):
                        for hh in range(2):
                            r = slice(64 * hh, 64 * hh + 64)
                            rhs = el[r, l, j, :].rearrange("p (n two b) -> p n two b", two=2, b=half)[:, :, 1, :]
                            out = pm[:, bank + hh, j * 256 + at:j * 256 + at + 64]
                            last = pe.matmul(out.rearrange("p (n b) -> p n b", b=half), el[r, l, j, :], rhs,
                                             start=True, stop=True)
                    if l in (1, 5, 6):
                        last.then_inc(hc_lt, 1)
                if c:
                    pe.wait_ge(hc_tc, c)
                for j in range(2):
                    last = pe.transpose(pm[:, 4, j * P:(j + 1) * P], ex2[:, 1, j, :], ident)
                last.then_inc(hc_tt, 1)
                pe.wait_ge(hc_lv, 8 * (c + 1))
                for j in range(2):
                    pe.matmul(pm[:, 2, j * CH:(j + 1) * CH], h_st[:, j, :], qe[:, j, :], start=True, stop=False,
                              skip_group_check=True)
                    for hh in range(2):
                        v0 = 128 + (2 * j + hh) * 64
                        last = pe.matmul(pm[64 * hh:64 * hh + 64, 2, j * CH:(j + 1) * CH], vt[:, c, v0:v0 + 64],
                                         att[:, 2 * hh + j, :], start=False, stop=(hh == 1), skip_group_check=True)
                last.then_inc(hc_ot, 1)
                pe.wait_ge(hc_tc, c + 1)
                for j in range(2):
                    last = pe.matmul(pm[:, 3, j * P:(j + 1) * P], ktok[:, j, :], vt[:, c, 128 + j * P:128 + (j + 1) * P],
                                     start=True, stop=True)
                last.then_inc(hc_ot, 1)

            def sample(g, prev):
                for j in range(2):
                    pe.wait_ge(ss_v, 5 * g + 2 * j + 1)
                    pe.matmul(pm[:, j, :], blk, flat(sm_tmp[g])[:, 0:512], start=True, stop=True).then_inc(ss_t, 1)
                    pe.wait_ge(ss_v, 5 * g + 2 * j + 2)
                    pe.matmul(pm[:, 2 + j, :], blk, flat(sm_tmp[g])[:, 512:1024], start=True,
                              stop=True).then_inc(ss_t, 1)

            def hsample(_):
                pe.wait_ge(hc_oc, NC)
                pe.wait_ge(hc_sv, NC)
                sample(0, 0)

            def gnorm(g, n0):
                for j in range(2):
                    pe.wait_ge(nm_a, 2 * g + j + 1)
                    if j == 0:
                        pe.wait_ge(ss_v, 5 * g + 5)
                    mix(n0 + j, blk, slot(2 + j))

            def mprep(_):
                pe.wait_ge(nm_v, 1)
                for j in range(2):
                    mix(13 + j, sel[0:4, j * P:(j + 1) * P], slot(9)[0:4, :])
                for j in range(2):
                    mix(15 + j, sel[32:36, j * P:(j + 1) * P],
                        slot(8)[32:36, :])
                pe.wait_ge(mix_ev, 16)
                for j in range(2):
                    last = pe.matmul(pm[:, 3, j * 8:j * 8 + 8],
                                     sel[0:4, j * P:(j + 1) * P],
                                     slot(8)[0:4, S0:S0 + 8], start=True, stop=True)
                last.then_inc(mix_mm, 1)

            def mchunk(c):
                cc = slice(c * CH, (c + 1) * CH)
                q, k = slot(10, 2), slot(16, 2)
                if c == 0:
                    pe.wait_ge(mix_ev, 17)
                else:
                    pe.wait_ge(mc_w, c)
                    pe.wait_ge(mc_s, c)
                    pe.wait_ge(mc_k, c)
                    pe.wait_ge(mc_h, c)
                    pe.wait_ge(mc_sv, c)
                pe.matmul(pm[:, 0, :], ident, mask_d.unsqueeze(1).to_broadcast([P, 4, CH]), start=True, stop=False,
                          skip_group_check=True)
                for i in range(4):
                    head = 2 * (i % 2) + i // 2
                    last = pe.matmul(pm[:, 0, i * CH:(i + 1) * CH], ident[0:4, head:head + 1].to_broadcast([4, P]),
                                     slot(8)[0:4, cc], start=False, stop=(i == 3), skip_group_check=True)
                last.then_inc(mc_t, 1)
                for j in range(2):
                    for hh in range(2):
                        r = slice(64 * hh, 64 * hh + 64)
                        last = pe.matmul(pm[:, 1 + hh, j * CH:(j + 1) * CH], k[r, j, cc], q[r, j, cc],
                                         start=True, stop=True)
                last.then_inc(mc_t, 1)
                for j in range(2):
                    last = pe.transpose(pm[:, 4, j * P:(j + 1) * P], k[:, j, cc], ident)
                last.then_inc(mc_tt, 1)
                pe.wait_ge(mc_q, c + 1)
                pe.wait_ge(mc_s, c + 1)
                for n, st in enumerate((c_st, n_st)):
                    for j in range(2):
                        at = (2 * n + j) * CH
                        pe.matmul(pm[:, 3, at:at + CH], st[:, j, :], qe[:, j, :], start=True, stop=False,
                                  skip_group_check=True)
                        for hh in range(2):
                            v0 = 384 + (2 * j + hh) * 64
                            lhs = ones[:, 0:64] if n else vt[:, c, v0:v0 + 64]
                            last = pe.matmul(pm[64 * hh:64 * hh + 64, 3, at:at + CH], lhs, att[:, 2 * hh + j, :],
                                             start=False, stop=(hh == 1), skip_group_check=True)
                last.then_inc(mc_nt, 1)
                pe.wait_ge(mc_k, c + 1)
                for j in range(2):
                    pe.matmul(pm[:, 1, 256 + j * P:256 + (j + 1) * P], ktok[:, j, :],
                              vt[:, c, 384 + j * P:384 + (j + 1) * P], start=True, stop=True)
                    last = pe.matmul(pm[:, 2, 256 + 2 * j:258 + 2 * j], ktok[:, j, :], ones[:, 0:2],
                                     start=True, stop=True)
                last.then_inc(mc_nt, 1)

            def msample(_):
                pe.wait_ge(mc_h, NC)
                pe.wait_ge(mc_sv, NC)
                sample(1, 0)
                pe.wait_ge(ss_v, 10)
                for j in range(2):
                    last = pe.matmul(pm[:, 4, 384 + j * 8:392 + j * 8], blk, tiny[:, 16 + j * 8:24 + j * 8],
                                     start=True, stop=True)
                last.then_inc(ss_t, 1)

            steps = dict(job=job, rows=rows, conv=lambda _: None, gate=gate, lru=lambda _: None, rope=rope,
                         vt=vtrans, attn=attn, sattn=sattn, hprep=lambda _: None, hchunk=hchunk, hsample=hsample,
                         hnorm=lambda _: gnorm(0, 11), mprep=mprep, mchunk=mchunk, msample=msample,
                         mnorm=lambda _: gnorm(1, 18))
            with pe.Fori(0, LAYERS) as l:
                norm(0)
                for what, i in ORDER:
                    steps[what](i)
                for j in range(N_WIN, N_WIN + N_OUT):
                    pe.wait_ge(lo_made, j + 1)
                    unit(j % 2, 0, KT, n_hi, n_lo, j,
                         (lambda k: pe.wait_ge(y_lo, k + 1)) if j == N_WIN else None)
                norm(1)
                with pe.Fori(0, FF_STEPS) as i:
                    U0 = N_WIN + N_OUT
                    for q in range(4):
                        pe.wait_ge(lo_made, i * 8 + (U0 + q + 1))
                        unit((U0 + q) % 2, 0, KT, n_hi, n_lo, 0,
                             (lambda k: pe.wait_ge(nrm_lo, KT + k + 1)) if q == 0 else None,
                             vals=i * 12 + (U0 + q))
                    for q in range(4, 8):
                        pe.wait_ge(lo_made, i * 8 + (U0 + q + 1))
                        for m in range(2):
                            unit((U0 + q) % 2, 4 * m, 4, hid_hi, hid_lo, 0,
                                 (lambda k: pe.wait_ge(ff_l, i * 4 + (k + 1))) if q == 4 and m == 0 else None,
                                 vals=i * 12 + (U0 + 4 + (q - 4) * 2 + m))
                u = N_WIN + N_OUT + 12 * FF_STEPS
                j = N_WIN + N_OUT + N_FF
                for half in range(2):
                    pe.wait_ge(lo_made, j + 1)
                    for m in range(4):
                        unit(j % 2, 2 * m, 2, ple_hi, ple_lo, u,
                             (lambda k: pe.wait_ge(pl, k + 1)) if half == 0 and m == 0 else None)
                        u += 1
                    j += 1
                    for m in range(4):
                        pe.wait_ge(lo_made, j + 1)
                        unit(j % 2, 0, KT, n_hi, n_lo, u,
                             (lambda k: pe.wait_ge(pl, 2 + k + 1)) if half == 0 and m == 0 else None)
                        u += 1
                        j += 1
                layer_end(pe)


        @block.scalar
        def _(act):
            link = linker(act, ch_a)

            def split_hi(j, done=None):
                act.wait_ge(w_ld[j % 2], 16 * (j // 2 + 1))
                if done:
                    act.wait_ge(mm[2], done)
                act.activation(w_hi[:, j % 2, :], w_raw[:, j % 2, :], ACT.Copy).then_inc(hi_made, 1)

            def take(dst, func, n, rows=slice(0, P), out_rows=None, **kw):
                for t in range(3):
                    act.wait_ge(mm[t], n)
                    o = dst[out_rows or rows, t * TT:(t + 1) * TT]
                    act.activation(o, pj[rows, t, 0:TT], func, **kw).then_inc(ev[t], 1)

            def norm(i):
                for k in range(KT):
                    if k >= 2:
                        act.wait_ge(nrm_mm, KT * i + k - 1)
                    act.activation(ext[:, k % 2, :], res[:, k, :], ACT.Square).then_inc(nrm_sq, 1)
                act.wait_ge(nrm_mm, KT * (i + 1))
                act.activation(ext[:, 2, :].rearrange(three, a=3), pm3, ACT.Sqrt, bias=EPS,
                               scale=1.0 / D).then_inc(nrm_rs, 1)
                for k in range(KT):
                    act.wait_ge(nrm_n, KT * i + k + 1)
                    act.activation(n_hi[:, k, :], ext[:, 3 + k % 2, :], ACT.Copy).then_inc(nrm_hi, 1)

            kind = dict(cq0=ACT.Silu, cq1=ACT.Silu, cg0=ACT.Silu, cg1=ACT.Silu, cf0=ACT.Sigmoid, cf1=ACT.Sigmoid,
                        do0=ACT.Sigmoid, do1=ACT.Sigmoid)

            def job(j):
                name = WIN[j]
                split_hi(j + 1, j if j >= 1 else None)
                if name == 'gates':
                    for t in range(3):
                        act.wait_ge(mm[t], 1)
                        act.activation(slot(8)[0:4, t * TT:(t + 1) * TT], pj[0:4, t, 0:TT], ACT.Copy)
                        act.activation(slot(9)[0:4, t * TT:(t + 1) * TT], pj[32:36, t, 0:TT],
                                       ACT.Copy).then_inc(ev[t], 1)
                    return
                if name in ('ci0', 'ci1'):
                    act.wait_ge(rope_v, 6)
                if name in ('dv0', 'dv1', 'dq0', 'dq1'):
                    act.wait_ge(lru_v, 2)
                    act.wait_ge(rope_v, 6)
                if name in ('cq0', 'cf0'):
                    act.wait_ge(sa_v, 4)
                    act.wait_ge(sa_t, 4)
                if name == 'cg0':
                    act.wait_ge(smp_st, 32)
                if name == 'dk0':
                    act.wait_ge(kv_st, 32)
                    act.wait_ge(sa_v, 4)
                if name == 'do0':
                    act.wait_ge(ss_v, 5)
                    act.wait_ge(ss_t, 4)
                    act.wait_ge(mix_st, 32)
                kw = dict(scale=0.125) if name in ('dk0', 'dk1') else {}
                take(slot(SLOT[name]), kind.get(name, ACT.Copy), j + 1, **kw)
                if name in ('ci0', 'ci1', 'dv0', 'dv1'):
                    act.wait_ge(ev[2], j + 1)
                    i = ('ci0', 'ci1', 'dv0', 'dv1').index(name)
                    act.activation(v_smp[:, i, :], slot(SLOT[name])[:, S0:T], ACT.Copy).then_inc(hp_a, 1)

            def rows(_):
                z = slot(9)[0:4, :]
                act.wait_ge(rows_v, 1)
                link(act.activation(slot(2)[0:4, :], z, ACT.Abs))
                act.activation(slot(2)[0:4, :], slot(2)[0:4, :], ACT.Exp, scale=-1.0).then_inc(rows_a, 1)
                act.wait_ge(rows_v, 2)
                act.activation(slot(5)[0:4, :], slot(3)[0:4, :], ACT.Ln).then_inc(rows_a, 1)
                act.wait_ge(rows_v, 5)
                act.activation(slot(6)[32:36, 0:SEQ], slot(2)[0:4, 0:SEQ], ACT.Exp).then_inc(rows_a, 1)
                act.activation(slot(9)[0:4, :], slot(9)[0:4, :], ACT.Exp).then_inc(rows_a, 1)
                act.activation(slot(8)[32:36, :], slot(5)[0:4, :], ACT.Exp, scale=-1.0).then_inc(rows_a, 1)
                act.activation(slot(8)[0:4, S0:T], slot(8)[0:4, S0:T], ACT.Exp).then_inc(rows_a, 1)
                act.wait_ge(rows_t, 1)
                act.activation(bw[:, :, 0, :], pm[:, 3, 0:64].rearrange("p (c e) -> p c e", c=NC)[:, :, 0:4],
                               ACT.Copy).then_inc(rows_c, 1)
                act.activation(bw[:, :, 1, :], pm[:, 4, 0:64].rearrange("p (c e) -> p c e", c=NC)[:, :, 0:4],
                               ACT.Copy).then_inc(rows_c, 1)
                link(act.activation(tiny[:, 0:2], pc('lam', 0, 2), ACT.Abs))
                act.activation(tiny[:, 2:4], tiny[:, 0:2], ACT.Exp, scale=-1.0).then_inc(rows_a, 1)
                act.wait_ge(rows_v, 10)
                act.activation(tiny[:, 6:8], tiny[:, 4:6], ACT.Ln).then_inc(rows_a, 1)
                act.wait_ge(rows_v, 11)
                act.activation(tiny[:, 16:20], tiny[:, 12:16], ACT.Exp).then_inc(rows_a, 1)

            def gate(_):
                for n in range(4):
                    act.wait_ge(mix_mm, n + 1)
                    b = pc('br' if n < 2 else 'bi', n % 2)
                    act.activation(slot(2 + n).rearrange(three, a=3), pm3, ACT.Sigmoid, bias=b).then_inc(mix_ev, 1)
                act.wait_ge(mix_ev, 4)
                act.wait_ge(rows_v, 12)
                for j in range(2):
                    act.activation(slot(2 + j), slot(2 + j), ACT.Tanh, scale=tiny[:, 10 + j:11 + j]).then_inc(lru_a, 1)
                act.wait_ge(lru_a, 2)
                for j in range(2):
                    act.activation(slot(6 + j), slot(2 + j), ACT.Sqrt).then_inc(lru_a, 1)
                act.wait_ge(ev[2], 5)
                for j in range(2):
                    act.activation(slot(12 + j), slot(12 + j), ACT.Gelu_apprx_tanh).then_inc(lru_a, 1)

            def rope(_):
                act.wait_ge(lru_v, 2)
                act.wait_ge(ev[2], JOB['k'] + 1)
                for n in range(3):
                    act.activation(slot(n), slot(14 + n), ACT.Square).then_inc(rope_a, 1)
                for n in range(3):
                    act.wait_ge(mix_mm, 5 + n)
                    act.activation(slot(3 + n).rearrange(three, a=3), pm3, ACT.Sqrt, bias=EPS,
                                   scale=1.0 / 64).then_inc(mix_ev, 1)

            def vtrans(v):
                col = VT_COL[list(VT_COL)[v]]
                for h in range(2):
                    act.wait_ge(vt_t, 2 * v + h + 1)
                    act.activation(vt[:, 4 * h:4 * h + 4, col:col + P],
                                   pm[:, 4, :].rearrange("p (c d) -> p c d", c=4), ACT.Copy).then_inc(vt_c, 1)

            def attn(c):
                if c == 0:
                    act.wait_ge(rope_v, 6)
                    act.dma_start(kv_out[l][:, 0, :], slot(16)[:, SEQ - CH:SEQ]).then_inc(kv_st, 16)
                    act.wait_ge(ev[2], JOB['bv'] + 1)
                    act.dma_start(kv_out[l][:, 1, :], slot(17)[:, SEQ - CH:SEQ]).then_inc(kv_st, 16)
                    act.wait_ge(lru_v, 2)
                    kc = flat(6)[:, 0:1024].rearrange("p (b s) -> p b s", b=DEC)
                    vc = flat(7)[:, 0:1024].rearrange("p (b d) -> p b d", b=DEC)
                    act.dma_start(kc[:, :, 1:P], kc_in[l]).then_inc(smp_ld, 16)
                    act.dma_start(vc[1:P, :, :], vc_in[l]).then_inc(smp_ld, 16)
                sc = flat(0)[:, 0:1024].rearrange("p (i s) -> p i s", i=4)
                lo_k = 0 if c else CH
                act.wait_ge(at_m, c + 1)
                for i in range(4):
                    act.activation(sc[:, i, lo_k:], sc[:, i, lo_k:], ACT.Exp, bias=tiny[:, 24 + i:25 + i],
                                   accum_out=tiny[:, 28 + i:29 + i])
                act.activation(tiny[:, 32:36], tiny[:, 32:36], ACT.Exp).then_inc(at_e, 1)
                act.wait_ge(at_t, c + 1)
                act.activation(flat(2)[:, 0:1024].rearrange("p (a s) -> p a s", a=2)
                               if c else flat(2)[:, 0:1024].rearrange("p (i h t) -> p i h t", i=4, h=2)[:, :, 1, :],
                               pm[:, 2:4, :] if c else
                               pm[:, 2:4, :].rearrange("p a (i h t) -> p (a i) h t", i=2, h=2)[:, :, 1, :],
                               ACT.Copy).then_inc(at_c, 1)
                act.wait_ge(at_w, c + 1)
                act.activation(slot(14, 2)[:, :, c * CH:(c + 1) * CH],
                               pm[:, 4, 0:256].rearrange("p (j t) -> p j t", j=2), ACT.Copy).then_inc(at_o, 1)

            def sattn(_):
                vc = flat(7)[:, 0:1024].rearrange("p (b d) -> p b d", b=DEC)
                act.wait_ge(sa_t, 1)
                act.activation(vc[0:1, :, :].rearrange("p (a b) d -> p a (b d)", a=2), pm[0:1, 0:2, :],
                               ACT.Copy).then_inc(sa_a, 1)
                act.wait_ge(sa_x, 1)
                act.activation(flat(2)[0:4, 0:1024], flat(2)[0:4, 0:1024], ACT.Exp).then_inc(sa_a, 1)
                act.activation(tiny[0:4, 8:16], tiny[0:4, 8:16], ACT.Exp).then_inc(sa_a, 1)
                act.wait_ge(sa_t, 4)
                act.wait_ge(sa_a, 1)
                act.dma_start(kc_out[l], flat(6)[:, 0:1024].rearrange("p (b s) -> p b s", b=DEC)).then_inc(smp_st, 16)
                act.dma_start(vc_out[l], vc).then_inc(smp_st, 16)

            def hprep(_):
                act.wait_ge(hp_v, 1)
                for j in range(2):
                    act.activation(slot(2 + j), slot(2 + j), ACT.Ln).then_inc(hp_a, 1)

            def hchunk(c):
                el = flat(18, 2)[:, 0:NLEV * 256]
                act.wait_ge(hc_sub, c + 1)
                act.activation(el, el, ACT.Exp).then_inc(hc_exp, 1)
                act.activation(ex2[:], ex2[:], ACT.Exp).then_inc(hc_exp, 1)
                act.wait_ge(hc_tt, c + 1)
                act.activation(ktok[:], pm[:, 4, 0:256].rearrange("p (j t) -> p j t", j=2), ACT.Copy).then_inc(hc_tc, 1)
                act.wait_ge(hc_ot, 2 * c + 1)
                act.activation(slot(0, 2)[:, :, c * CH:(c + 1) * CH],
                               pm[:, 2, 0:256].rearrange("p (j t) -> p j t", j=2), ACT.Copy).then_inc(hc_oc, 1)

            def hsample(_):
                act.wait_ge(hc_sv, NC)
                act.dma_start(flat(19)[:, 0:1024], hs_in[l]).then_inc(st_ld, 16)
                act.activation(tiny[:, 0:16].rearrange("p (j b) -> p j b", j=2), slot(2, 2)[:, :, S0:T],
                               ACT.Exp).then_inc(ss_a, 1)
                act.dma_start(hp_out[l], h_st[:]).then_inc(mix_st, 16)
                act.wait_ge(ss_v, 5)
                act.dma_start(hs_out[l], flat(19)[:, 0:1024]).then_inc(mix_st, 16)

            def gnorm(g, n0, o):
                act.wait_ge(ss_v, 5 if g == 0 else 11)
                act.wait_ge(hc_oc, NC)
                for j in range(2):
                    act.activation(slot(2 + j), slot(o + j), ACT.Square).then_inc(nm_a, 1)
                for j in range(2):
                    act.wait_ge(mix_mm, n0 + j)
                    act.activation(slot(4 + j).rearrange(three, a=3), pm3, ACT.Sqrt, bias=EPS,
                                   scale=1.0 / 64).then_inc(mix_ev, 1)

            def mprep(_):
                act.wait_ge(nm_v, 1)
                act.dma_start(flat(6)[:, 0:1024], cs_in[l]).then_inc(st_ld, 16)
                for n in range(4):
                    act.wait_ge(mix_mm, 13 + n)
                    act.activation(slot(2 + n).rearrange(three, a=3), pm3, ACT.Copy).then_inc(mix_ev, 1)
                act.wait_ge(mix_mm, 17)
                act.activation(tiny[:, 0:16], pm[:, 3, 0:16], ACT.Copy).then_inc(mix_ev, 1)

            def mchunk(c):
                w = ex2[:].rearrange("p a j t -> p (a j) t")
                act.wait_ge(mc_t, 2 * c + 1)
                if c == 0:
                    act.wait_ge(mc_d, 1)
                for i in range(4):
                    head = 2 * (i % 2) + i // 2
                    last = act.activation(w[:, i, :], pm[:, 0, i * CH:(i + 1) * CH], ACT.Exp, bias=bw[:, c, 0, head:head + 1])
                last.then_inc(mc_w, 1)
                act.wait_ge(mc_nt, 2 * c + 1)
                act.activation(ktmp, pm[:, 3, 256:512].rearrange("p (j t) -> p j t", j=2), ACT.Abs).then_inc(mc_d, 1)

            ktmp = vt[:, 0:2, 0:CH]

            def msample(_):
                act.wait_ge(mc_sv, NC)
                act.dma_start(cp_out[l], c_st[:]).then_inc(mix_st, 16)
                act.wait_ge(ss_t, 9)
                act.activation(tiny[:, 32:48], pm[:, 4, 384:400], ACT.Abs).then_inc(ss_a, 1)
                act.dma_start(cs_out[l], flat(6)[:, 0:1024]).then_inc(mix_st, 16)

            steps = dict(job=job, rows=rows, conv=lambda _: None, gate=gate, lru=lambda _: None, rope=rope,
                         vt=vtrans, attn=attn, sattn=sattn, hprep=hprep, hchunk=hchunk, hsample=hsample,
                         hnorm=lambda _: gnorm(0, 11, 0), mprep=mprep, mchunk=mchunk, msample=msample,
                         mnorm=lambda _: gnorm(1, 18, 10))
            with act.Fori(0, LAYERS) as l:
                act.wait_ge(par_ld, 16)
                split_hi(0)
                norm(0)
                act.wait_ge(h_out, 16)
                for what, i in ORDER:
                    steps[what](i)
                act.wait_ge(mm[2], N_WIN)
                for k, s in enumerate((12, 13, 14, 15, 0, 1, 10, 11)):
                    if k == 0:
                        act.wait_ge(lru_v, 2)
                        act.wait_ge(sa_v, 4)
                        act.wait_ge(nm_v, 1)
                    if k == 6:
                        act.wait_ge(nm_v, 2)
                    act.activation(n_hi[:, k, :], slot(s), ACT.Copy).then_inc(y_hi, 1)
                act.wait_ge(y_lo, KT)
                act.wait_ge(y_hi, KT)
                act.wait_ge(mix_st, 64)
                act.dma_start(res[:], h_saved).then_inc(h_ld, 16)
                act.dma_start(so_out[l], so[:]).then_inc(so_st, 16)
                for j in range(N_WIN, N_WIN + N_OUT):
                    split_hi(j + 1, j)
                act.wait_ge(ev[2], N_WIN + N_OUT)
                norm(1)
                with act.Fori(0, FF_STEPS) as i:
                    for q in range(8):
                        j = N_WIN + N_OUT + q + 1
                        done = N_WIN + N_OUT + (q if q < 5 else 4 + (q - 4) * 2)
                        n_ld = (i * 4 + (j // 2 + 1)) * 16
                        act.wait_ge(w_ld[j % 2], n_ld)
                        act.wait_ge(mm[2], i * 12 + done)
                        act.activation(w_hi[:, j % 2, :], w_raw[:, j % 2, :], ACT.Copy).then_inc(hi_made, 1)
                        if q < 4:
                            for t in range(3):
                                act.wait_ge(mm[t], i * 12 + (N_WIN + N_OUT + q + 1))
                                act.activation(relu[:, q % 2, t * TT:(t + 1) * TT], pj[:, t, 0:TT],
                                               ACT.Relu).then_inc(ev[t], 1)
                            act.wait_ge(ff_q, i * 4 + (q + 1))
                            act.activation(hid_hi[:, q, :], hsq[:, q % 2, :], ACT.Copy).then_inc(ff_h, 1)
                act.wait_ge(mm[2], N_WIN + N_OUT + 12 * FF_STEPS)
                act.wait_ge(ff_l, 4 * FF_STEPS)
                act.dma_start(ple_raw[:], p_in[l]).then_inc(ple_ld, 16)
                act.wait_ge(ple_ld, 16)
                for k in range(2):
                    act.activation(ple_hi[:, k, :], ple_raw[:, k, :], ACT.Copy).then_inc(ph, 1)
                act.wait_ge(ev[2], N_WIN + N_OUT + 12 * FF_STEPS)
                for k in range(KT):
                    act.activation(n_hi[:, k, :], res[:, k, :], ACT.Copy).then_inc(ph, 1)
                u = N_WIN + N_OUT + 12 * FF_STEPS
                j = N_WIN + N_OUT + N_FF
                for half in range(2):
                    split_hi(j + 1, u)
                    for m in range(4):
                        if half:
                            act.wait_ge(pv, 4 * half)
                        u += 1
                        take(ple_proj[:, m, :], ACT.Copy, u)
                    j += 1
                    for m in range(4):
                        if j + 1 < N_JOBS:
                            split_hi(j + 1, u)
                        u += 1
                        if 4 * half + m:
                            act.wait_ge(pv, 4 * half + m)
                        take(ple_sig, ACT.Sigmoid, u)
                        j += 1
                act.wait_ge(pv, KT)
                act.wait_ge(so_st, 16)
                layer_end(act)

        @block.gpsimd
        def _(pool):
            def split_lo(j, done=None):
                pool.wait_ge(hi_made, j + 1)
                if done:
                    pool.wait_ge(mm[2], done)
                pool.tensor_tensor(w_lo[:, j % 2, :], w_raw[:, j % 2, :], w_hi[:, j % 2, :].bitcast(F32),
                                   ALU.subtract).then_inc(lo_made, 1)

            def norm(i):
                for k in range(KT):
                    pool.wait_ge(nrm_hi, KT * i + k + 1)
                    pool.tensor_tensor(n_lo[:, k, :], ext[:, 3 + k % 2, :], n_hi[:, k, :].bitcast(F32),
                                       ALU.subtract).then_inc(nrm_lo, 1)

            with pool.Fori(0, LAYERS) as l:
                split_lo(0)
                norm(0)
                for j in range(1, N_WIN + 1):
                    split_lo(j, j - 1 if j >= 2 else None)
                for k, s in enumerate((12, 13, 14, 15, 0, 1, 10, 11)):
                    pool.wait_ge(y_hi, k + 1)
                    pool.tensor_tensor(n_lo[:, k, :], slot(s), n_hi[:, k, :].bitcast(F32),
                                       ALU.subtract).then_inc(y_lo, 1)
                for j in range(N_WIN + 1, N_WIN + N_OUT + 1):
                    split_lo(j, j - 1)
                norm(1)
                with pool.Fori(0, FF_STEPS) as i:
                    for q in range(8):
                        j = N_WIN + N_OUT + q + 1
                        done = N_WIN + N_OUT + (q if q < 5 else 4 + (q - 4) * 2)
                        pool.wait_ge(hi_made, i * 8 + (j + 1))
                        pool.wait_ge(mm[2], i * 12 + done)
                        pool.tensor_tensor(w_lo[:, j % 2, :], w_raw[:, j % 2, :], w_hi[:, j % 2, :].bitcast(F32),
                                           ALU.subtract).then_inc(lo_made, 1)
                        if q < 4:
                            pool.wait_ge(ff_h, i * 4 + (q + 1))
                            pool.tensor_tensor(hid_lo[:, q, :], hsq[:, q % 2, :], hid_hi[:, q, :].bitcast(F32),
                                               ALU.subtract).then_inc(ff_l, 1)
                for k in range(2):
                    pool.wait_ge(ph, k + 1)
                    pool.tensor_tensor(ple_lo[:, k, :], ple_raw[:, k, :], ple_hi[:, k, :].bitcast(F32),
                                       ALU.subtract).then_inc(pl, 1)
                for k in range(KT):
                    pool.wait_ge(ph, 2 + k + 1)
                    pool.tensor_tensor(n_lo[:, k, :], res[:, k, :], n_hi[:, k, :].bitcast(F32),
                                       ALU.subtract).then_inc(pl, 1)
                u = N_WIN + N_OUT + 12 * FF_STEPS
                j = N_WIN + N_OUT + N_FF
                for half in range(2):
                    split_lo(j + 1, u)
                    u += 4
                    j += 1
                    for m in range(4):
                        if j + 1 < N_JOBS:
                            split_lo(j + 1, u)
                        u += 1
                        j += 1
                layer_end(pool)

        @block.vector
        def _(dve):
            link = linker(dve, ch_v)

            def tt(o, a, b, op):
                return dve.tensor_tensor(o, a, b, op)

            def norm(i):
                dve.wait_ge(nrm_rs, i + 1)
                rs = ext[:, 2, :]
                link(dve.reciprocal(rs, rs))
                for k in range(KT):
                    if k >= 2:
                        dve.wait_ge(nrm_lo, KT * i + k - 1)
                    dve.scalar_tensor_tensor(ext[:, 3 + k % 2, :], res[:, k, :], pc('g1' if i == 0 else 'g2', k), rs,
                                             ALU.mult, ALU.mult).then_inc(nrm_n, 1)

            def rows(_):
                z, ig = slot(9)[0:4, :], slot(8)[0:4, :]
                t1, t2, ln, f = slot(2)[0:4, :], slot(3)[0:4, :], slot(5)[0:4, :], slot(4)[0:4, :]
                for t in range(3):
                    dve.wait_ge(ev[t], 1)
                dve.wait_ge(h_out, 16)
                link(dve.memset(so[:], 0.0))
                link(dve.tensor_scalar(ig, ig, pc('ib')[0:4], None, ALU.add))
                dve.tensor_scalar(z, z, pc('fb')[0:4], None, ALU.add).then_inc(rows_v, 1)
                dve.wait_ge(rows_a, 1)
                dve.tensor_scalar(t2, t1, 1.0, None, ALU.add).then_inc(rows_v, 1)
                dve.wait_ge(rows_a, 2)
                link(dve.tensor_scalar(t2, t2, -1.0, 1e-30, ALU.add, ALU.max))
                link(dve.reciprocal(t2, t2))
                link(tt(t2, t2, t1, ALU.mult))
                link(tt(ln, ln, t2, ALU.mult))
                link(dve.scalar_tensor_tensor(z, z, 0.0, ln, ALU.min, ALU.subtract))
                one = flat(7)[0:4, 0:CH]
                link(dve.memset(flat(7)[0:P, 0:CH], 1.0))
                for c in range(NC):
                    last = dve.tensor_tensor_scan(f[:, c * CH:(c + 1) * CH], one, z[:, c * CH:(c + 1) * CH], 0.0,
                                                  ALU.mult, ALU.add)
                link(last)
                m = ln
                link(dve.tensor_tensor_scan(m[:, 0:SEQ], z[:, 0:SEQ], ig[:, 0:SEQ], 0.0, ALU.add, ALU.max))
                link(tt(f[:, SEQ:T], z[:, SEQ:T], pc('m0', 0, 8)[0:4], ALU.add))
                link(tt(m[:, SEQ:T], f[:, SEQ:T], ig[:, SEQ:T], ALU.max))
                link(dve.tensor_copy(oc('mp')[0:4], m[:, SEQ - 1:SEQ]))
                link(dve.tensor_copy(oc('ms', 0, 8)[0:4], m[:, SEQ:T]))
                beta = slot(6)[0:4, :]
                link(tt(beta[:, 0:SEQ], ig[:, 0:SEQ], f[:, 0:SEQ], ALU.subtract))
                link(tt(ig[:, SEQ:T], ig[:, SEQ:T], m[:, SEQ:T], ALU.subtract))
                link(tt(ig[:, 0:SEQ], f[:, 0:SEQ], m[:, 0:SEQ], ALU.subtract))
                link(tt(z[:, SEQ:T], f[:, SEQ:T], m[:, SEQ:T], ALU.subtract))
                a3 = ig[:, 0:SEQ].rearrange("p (c t) -> p c t", c=NC)
                m3 = m[:, 0:SEQ].rearrange("p (c t) -> p c t", c=NC)
                z3 = z[:, 0:SEQ].rearrange("p (c t) -> p c t", c=NC)
                link(dve.tensor_copy(z3[:, 0, :], a3[:, 0, :]))
                link(tt(z3[:, 1:, :], a3[:, 1:, :], m3[:, 0:NC - 1, CH - 1:CH].to_broadcast([4, NC - 1, CH]), ALU.add))
                link(tt(t1[:, 0:SEQ].rearrange("p (c t) -> p c t", c=NC),
                        beta[:, 0:SEQ].rearrange("p (c t) -> p c t", c=NC),
                        a3[:, :, CH - 1:CH].to_broadcast([4, NC, CH]), ALU.add))
                for n in range(3):
                    dve.sem_inc(rows_v, 1)
                dve.wait_ge(rows_a, 6)
                for n in range(4):
                    dve.sem_inc(rows_v, 1)
                link(dve.tensor_reduce(tiny[:, 20:22], pc('gam', 0, 4).rearrange("p (l j) -> p j l", l=2), AX_X, ALU.max))
                link(tt(tiny[:, 12:16].rearrange("p (l j) -> p l j", l=2), pc('gam', 0, 4).rearrange("p (l j) -> p l j", l=2),
                        tiny[:, 20:22].unsqueeze(1).to_broadcast([P, 2, 2]), ALU.subtract))
                dve.wait_ge(rows_a, 7)
                dve.tensor_scalar(tiny[:, 4:6], tiny[:, 2:4], 1.0, None, ALU.add).then_inc(rows_v, 1)
                dve.wait_ge(rows_a, 8)
                dve.tensor_scalar(tiny[:, 4:6], tiny[:, 4:6], -1.0, 1e-30, ALU.add, ALU.max).then_inc(rows_v, 1)
                dve.wait_ge(rows_v, 11)
                link(dve.reciprocal(tiny[:, 4:6], tiny[:, 4:6]))
                link(tt(tiny[:, 4:6], tiny[:, 4:6], tiny[:, 2:4], ALU.mult))
                link(tt(tiny[:, 6:8], tiny[:, 6:8], tiny[:, 4:6], ALU.mult))
                link(dve.tensor_scalar(tiny[:, 8:10], pc('lam', 0, 2), -1.0, 0.0, ALU.mult, ALU.max))
                link(tt(tiny[:, 8:10], tiny[:, 8:10], tiny[:, 6:8], ALU.add))
                dve.tensor_scalar(tiny[:, 10:12], tiny[:, 8:10], 4.0, None, ALU.mult).then_inc(rows_v, 1)
                dve.wait_ge(rows_a, 9)
                link(tt(tiny[:, 20:22], tiny[:, 16:18], tiny[:, 18:20], ALU.add))
                link(dve.reciprocal(tiny[:, 20:22], tiny[:, 20:22]))
                link(tt(tiny[:, 20:22], tiny[:, 20:22], tiny[:, 18:20], ALU.mult))
                link(dve.tensor_scalar(tiny[:, 36:38], tiny[:, 20:22], pc('lm'), None, ALU.mult))
                link(dve.tensor_scalar(tiny[:, 38:40], tiny[:, 36:38], -1.0, 1.0, ALU.mult, ALU.add))
                link(dve.memset(tiny[:, 24:36], 0.0))

            def conv(_):
                for t in range(3):
                    dve.wait_ge(ev[t], 3)
                cv = pc('conv', 0, 48).rearrange("p (j w b) -> p j w b", j=2, w=3)
                for j in range(2):
                    x, o = slot(10 + j), slot(j)
                    link(dve.tensor_scalar(o, x, pc('cw', 3 * 2 + j), pc('cb', j), ALU.mult, ALU.add))
                    for w in range(3):
                        s = 3 - w
                        wc = pc('cw', w * 2 + j)
                        link(dve.scalar_tensor_tensor(o[:, s:SEQ], x[:, 0:SEQ - s], wc, o[:, s:SEQ], ALU.mult, ALU.add))
                        link(dve.scalar_tensor_tensor(o[:, S0:T], cv[:, j, w, :], wc, o[:, S0:T], ALU.mult, ALU.add))
                    link(dve.tensor_copy(oc('convp', 3 * j, 3), x[:, SEQ - 3:SEQ]))
                    cs = oc('convs', 24 * j, 24).rearrange("p (w b) -> p w b", w=3)
                    link(dve.tensor_copy(cs[:, 0:2, :], cv[:, j, 1:3, :]))
                    link(dve.tensor_copy(cs[:, 2, :], x[:, S0:T]))
                dve.sem_inc(conv_v, 1)

            def lru(_):
                dve.wait_ge(lru_a, 4)
                for j in range(2):
                    xc, u, i, su, rc = slot(j), slot(2 + j), slot(4 + j), slot(6 + j), slot(10 + j)
                    link(dve.tensor_scalar(rc, u, 1.0, None, ALU.add))
                    link(dve.reciprocal(rc, rc))
                    link(tt(i, i, xc, ALU.mult))
                    link(tt(su, su, rc, ALU.mult))
                    link(dve.scalar_tensor_tensor(i, su, 2.0, i, ALU.mult, ALU.mult))
                    link(dve.tensor_scalar(u, u, -1.0, 1.0, ALU.mult, ALU.add))
                    link(tt(u, u, rc, ALU.mult))
                    link(dve.tensor_tensor_scan(xc[:, 0:SEQ], u[:, 0:SEQ], i[:, 0:SEQ], 0.0, ALU.mult, ALU.add))
                    link(tt(xc[:, S0:T], u[:, S0:T], pc('h0', 8 * j, 8), ALU.mult))
                    link(tt(xc[:, S0:T], xc[:, S0:T], i[:, S0:T], ALU.add))
                    link(dve.tensor_copy(oc('hp', j), xc[:, SEQ - 1:SEQ]))
                    link(dve.tensor_copy(oc('hs', 8 * j, 8), xc[:, S0:T]))
                    dve.wait_ge(lru_a, 5 + j)
                    tt(slot(12 + j), slot(12 + j), xc, ALU.mult).then_inc(lru_v, 1)
                dve.wait_ge(lru_v, 2)

            def rope(_):
                dve.wait_ge(rope_ld, 16)
                for n in range(3):
                    dve.wait_ge(mix_ev, 5 + n)
                    link(dve.reciprocal(slot(3 + n), slot(3 + n)))
                    dve.scalar_tensor_tensor(slot(14 + n), slot(14 + n), pc('kg' if n == 2 else 'qg'), slot(3 + n),
                                             ALU.mult, ALU.mult).then_inc(rope_v, 1)
                for n in range(3):
                    dve.wait_ge(mix_mm, 8 + n)
                    dve.wait_ge(rope_v, 3 + n)
                    tmp = slot(n)
                    tt(tmp.rearrange(three, a=3), pm3, slot(19).rearrange(three, a=3), ALU.mult).then_inc(mix_ev, 1)
                    link(tt(slot(14 + n), slot(14 + n), slot(18), ALU.mult))
                    dve.wait_ge(mix_ev, 8 + n)
                    tt(slot(14 + n), slot(14 + n), tmp, ALU.add).then_inc(rope_v, 1)
                dve.wait_ge(rope_v, 6)

            def attn(c):
                sc = flat(0)[:, 0:1024].rearrange("p (i s) -> p i s", i=4)
                lo_k = 0 if c else CH
                dve.wait_ge(at_s, c + 1)
                if c:
                    dve.wait_ge(at_t, c)
                mask = cst[:, C_MP + lo_k:C_MP + 256].unsqueeze(1).to_broadcast([P, 4, 256 - lo_k])
                ps = pm[:, 0:2, :].rearrange("p a (j s) -> p (a j) s", j=2)[:, :, lo_k:]
                link(dve.scalar_tensor_tensor(sc[:, :, lo_k:], ps, 0.125, mask, ALU.mult, ALU.add))
                mx = tiny[:, 20:24]
                link(dve.tensor_reduce(mx, sc[:, :, lo_k:], AX_X, ALU.max))
                link(tt(mx, mx, pc('sink', 0, 4), ALU.max))
                link(tt(tiny[:, 32:36], pc('sink', 0, 4), mx, ALU.subtract))
                dve.tensor_scalar(tiny[:, 24:28], mx, -1.0, None, ALU.mult).then_inc(at_m, 1)
                dve.wait_ge(at_e, c + 1)
                link(tt(tiny[:, 40:44], tiny[:, 28:32], tiny[:, 32:36], ALU.add))
                link(dve.reciprocal(tiny[:, 40:44], tiny[:, 40:44]))
                tt(sc[:, :, lo_k:], sc[:, :, lo_k:], tiny[:, 40:44].unsqueeze(2).to_broadcast([P, 4, 256 - lo_k]),
                   ALU.mult).then_inc(at_p, 1)

            def sattn(_):
                dve.wait_ge(at_t, NC)
                dve.wait_ge(at_o, NC)
                dve.wait_ge(smp_ld, 32)
                qb = flat(0)[:, 0:32].rearrange("p (b i) -> p b i", b=DEC)
                link(dve.memset(flat(0)[:, 0:32], 0.0))
                for j in range(2):
                    link(dve.tensor_copy(qb[0:64, :, j], slot(14 + j)[0:64, S0:T]))
                    link(dve.tensor_copy(qb[64:P, :, 2 + j], slot(14 + j)[64:P, S0:T]))
                kc = flat(6)[:, 0:1024].rearrange("p (b s) -> p b s", b=DEC)
                dve.tensor_copy(kc[:, :, 0], slot(16)[:, S0:T]).then_inc(sa_v, 1)
                dve.wait_ge(sa_t, 2)
                s = flat(2)[0:4, 0:1024]
                s3 = s.rearrange("p (b s) -> p b s", b=DEC)
                link(dve.tensor_scalar(s.rearrange("p (a s) -> p a s", a=2), pm[0:4, 2:4, :], 0.125, None, ALU.mult))
                mx = tiny[0:4, 0:8]
                link(dve.tensor_reduce(mx, s3, AX_X, ALU.max))
                link(dve.tensor_scalar(mx, mx, pc('sinkc')[0:4], None, ALU.max))
                link(tt(s3, s3, mx.unsqueeze(2).to_broadcast([4, DEC, CH]), ALU.subtract))
                link(dve.tensor_scalar(tiny[0:4, 8:16], mx, -1.0, pc('sinkc')[0:4], ALU.mult, ALU.add))
                dve.sem_inc(sa_x, 1)
                dve.wait_ge(sa_a, 3)
                link(dve.tensor_reduce(mx, s3, AX_X, ALU.add))
                link(tt(mx, mx, tiny[0:4, 8:16], ALU.add))
                link(dve.reciprocal(mx, mx))
                tt(s3, s3, mx.unsqueeze(2).to_broadcast([4, DEC, CH]), ALU.mult).then_inc(sa_v, 1)
                dve.wait_ge(sa_t, 3)
                dve.tensor_copy(flat(3)[:, 0:32], pm[:, 4, 0:32]).then_inc(sa_v, 1)
                dve.wait_ge(sa_t, 4)
                o = pm[:, 4, 64:96].rearrange("p (b i) -> p b i", b=DEC)
                for j in range(2):
                    link(dve.tensor_copy(slot(14 + j)[0:64, S0:T], o[0:64, :, j]))
                    link(dve.tensor_copy(slot(14 + j)[64:P, S0:T], o[64:P, :, 2 + j]))
                dve.sem_inc(sa_v, 1)

            def hprep(_):
                for t in range(3):
                    dve.wait_ge(ev[t], JOB['cf1'] + 1)
                dve.wait_ge(vt_c, 10)
                dve.wait_ge(hp_a, 4)
                for j in range(2):
                    f = slot(2 + j)
                    link(dve.tensor_scalar(f, f, tiny[:, 38 + j:39 + j], tiny[:, 36 + j:37 + j], ALU.mult, ALU.add))
                    link(dve.tensor_scalar(slot(4 + j), f, -1.0, 1.0, ALU.mult, ALU.add))
                link(dve.memset(att[:, 0, :], 1.0))
                link(dve.memset(h_st[:], 0.0))
                dve.sem_inc(hp_v, 1)
                dve.wait_ge(hp_a, 6)
                for j in range(2):
                    f = slot(2 + j)
                    for c in range(NC):
                        cc = slice(c * CH, (c + 1) * CH)
                        last = dve.tensor_tensor_scan(f[:, cc], att[:, 0, :], f[:, cc], 0.0, ALU.mult, ALU.add)
                        link(last)

            def hchunk(c):
                cc = slice(c * CH, (c + 1) * CH)
                q, b, k = slot(0, 2)[:, :, cc], slot(2, 2)[:, :, cc], slot(4, 2)[:, :, cc]
                el = flat(18, 2)[:, 0:NLEV * 256].rearrange("p (l j t) -> p l j t", l=NLEV, j=2)
                if c:
                    dve.wait_ge(hc_lt, 3 * c)
                    dve.wait_ge(hc_ot, 2 * c)
                    dve.wait_ge(hc_tt, c)

                def halves(x, l):
                    v = x.rearrange("p j (n two b) -> p j n two b", two=2, b=1 << l)
                    return v[:, :, :, 0, :], v[:, :, :, 1, :]
                for l in range(NLEV):
                    b0, b1 = halves(b, l)
                    e0, e1 = halves(el[:, l], l)
                    n, half = CH >> (l + 1), 1 << l
                    for j in range(2):
                        ref = b0[:, j, :, half - 1:half].to_broadcast([P, n, half])
                        tt(e1[:, j], b1[:, j], ref, ALU.subtract)
                        last = tt(e0[:, j], ref, b0[:, j], ALU.subtract)
                link(last)
                dve.tensor_copy(ex2[:, 0], b)
                link(tt(ex2[:, 1], b[:, :, CH - 1:CH].to_broadcast([P, 2, CH]), b, ALU.subtract))
                dve.sem_inc(hc_sub, 1)
                dve.wait_ge(hc_exp, 2 * c + 2)
                for l in range(NLEV):
                    k0, q1 = halves(k, l)[0], halves(q, l)[1]
                    e0, e1 = halves(el[:, l], l)
                    for j in range(2):
                        tt(e0[:, j], e0[:, j], k0[:, j], ALU.mult)
                        tt(e1[:, j], e1[:, j], q1[:, j], ALU.mult)
                tt(qe[:], ex2[:, 0], q, ALU.mult)
                last = tt(ex2[:, 1], ex2[:, 1], k, ALU.mult)
                link(last)
                dve.sem_inc(hc_kq, 1)
                dve.wait_ge(hc_lt, 3 * c + 1)
                pv4 = [pm[:, a:a + 2, :].rearrange("p a (j s) -> p (a j) s", j=2) for a in (0, 2)]
                tt(att[:], pv4[0][:, :, 0:128], ident.unsqueeze(1).to_broadcast([P, 4, CH]),
                   ALU.mult).then_inc(hc_lv, 1)
                for l in range(NLEV):
                    dve.wait_ge(hc_lt, 3 * c + (1 if l < 2 else 2 if l < 6 else 3))
                    dve.wait_ge(hc_lv, 8 * c + 1 + l)
                    half, n = 1 << l, CH >> (l + 1)
                    out = att[:].rearrange("p i (n two b) -> p i n two b", two=2, b=half)[:, :, :, 1, :]
                    mk = cst[:, C_LEV + 64 * l:C_LEV + 64 * l + 64].bitcast(U32).rearrange("p (n b) -> p n b", b=half)
                    dat = pv4[LEV_AT[l][0] // 2][:, :, LEV_AT[l][1]:LEV_AT[l][1] + 64].rearrange("p i (n b) -> p i n b", b=half)
                    dve.copy_predicated(out, mk.unsqueeze(1).to_broadcast([P, 4, n, half]), dat).then_inc(hc_lv, 1)
                dve.wait_ge(hc_ot, 2 * c + 2)
                for j in range(2):
                    for hh in range(2):
                        r, e = slice(64 * hh, 64 * hh + 64), slice(64 * hh, 64 * hh + 64)
                        last = dve.scalar_tensor_tensor(h_st[r, j, e], h_st[r, j, e], ex2[r, 0, j, CH - 1:CH],
                                                        pm[r, 3, j * P + 64 * hh:j * P + 64 * hh + 64], ALU.mult, ALU.add)
                link(last)
                dve.sem_inc(hc_sv, 1)

            def sample(g, dec, kk, q, v0, st_at, o):
                w = flat(sm_tmp[g])
                w0, w1 = (w[:, 0:512].rearrange("p (b e) -> p b e", b=DEC),
                          w[:, 512:1024].rearrange("p (b e) -> p b e", b=DEC))
                for j in range(2):
                    st = flat(st_at)[:, 512 * j:512 * j + 512].rearrange("p (b e) -> p b e", b=DEC)
                    eb = eye.unsqueeze(1).to_broadcast([P, DEC, 64])
                    tt(w0, v_smp[:, v0 + j, :].unsqueeze(2).to_broadcast([P, DEC, 64]), eb, ALU.mult).then_inc(ss_v, 1)
                    dve.wait_ge(ss_t, 4 * g + 2 * j + 1)
                    vb = pm[:, j, :].rearrange("p (b e) -> p b e", b=DEC)
                    link(tt(w1, vb, kk[:, j, :].unsqueeze(2).to_broadcast([P, DEC, 64]), ALU.mult))
                    link(tt(st, st, dec[:, j, :].unsqueeze(2).to_broadcast([P, DEC, 64]), ALU.mult))
                    link(tt(st, st, w1, ALU.add))
                    tt(w1, st, q[:, j, :].unsqueeze(2).to_broadcast([P, DEC, 64]), ALU.mult).then_inc(ss_v, 1)
                    dve.wait_ge(ss_t, 4 * g + 2 * j + 2)
                    ob = pm[:, 2 + j, :].rearrange("p (b e) -> p b e", b=DEC)
                    link(tt(w1, ob, eb, ALU.mult))
                    link(dve.tensor_reduce(o[:, j, :], w1, AX_X, ALU.add))

            def hsample(_):
                dve.wait_ge(hc_oc, NC)
                dve.wait_ge(ss_a, 1)
                dve.wait_ge(st_ld, 16)
                sample(0, tiny[:, 0:16].rearrange("p (j b) -> p j b", j=2), slot(4, 2)[:, :, S0:T],
                       slot(0, 2)[:, :, S0:T], 0, st_slot[0], slot(0, 2)[:, :, S0:T])
                dve.sem_inc(ss_v, 1)

            def gnorm(g, n0, o, gain, gate0):
                for t in range(3):
                    dve.wait_ge(ev[t], (JOB['cg1'] if g == 0 else JOB['do1']) + 1)
                for j in range(2):
                    dve.wait_ge(mix_ev, n0 + j)
                    link(dve.reciprocal(slot(4 + j), slot(4 + j)))
                    link(dve.scalar_tensor_tensor(slot(o + j), slot(o + j), pc(gain), slot(4 + j), ALU.mult, ALU.mult))
                    link(tt(slot(o + j), slot(o + j), slot(gate0 + j), ALU.mult))
                dve.sem_inc(nm_v, 1)

            def mprep(_):
                pass

            def mchunk(c):
                cc = slice(c * CH, (c + 1) * CH)
                inter, em = slot(2, 2), slot(4, 2)
                if c == 0:
                    dve.wait_ge(mix_st, 32)
                    link(dve.memset(c_st[:], 0.0))
                    link(dve.memset(n_st[:], 0.0))
                    dve.sem_inc(mc_d, 1)
                    dve.wait_ge(mix_ev, 17)
                else:
                    dve.wait_ge(mc_nt, 2 * c)
                tt(qe[:], slot(10, 2)[:, :, cc], inter[:, :, cc], ALU.mult).then_inc(mc_q, 1)
                dve.wait_ge(mc_t, 2 * c + 2)
                dve.wait_ge(mc_w, c + 1)
                tt(att[:].rearrange("p (a j) t -> p a (j t)", a=2), pm[:, 1:3, 0:256],
                   ex2[:].rearrange("p a j t -> p a (j t)"), ALU.mult).then_inc(mc_s, 1)
                dve.wait_ge(mc_tt, c + 1)
                tt(ktok[:].rearrange("p j (h d) -> p (j h) d", h=2),
                   pm[:, 4, 0:256].rearrange("p (h d) -> p h d", h=4),
                   bw[:, c, 1, :].unsqueeze(2).to_broadcast([P, 4, 64]), ALU.mult).then_inc(mc_k, 1)
                dve.wait_ge(mc_d, c + 2)
                den = vt[:, 0:2, 0:CH]
                link(tt(den, den, em[:, :, cc], ALU.max))
                link(dve.reciprocal(den, den))
                tt(slot(10, 2)[:, :, cc], pm[:, 3, 0:256].rearrange("p (j t) -> p j t", j=2), den,
                   ALU.mult).then_inc(mc_h, 1)
                dve.wait_ge(mc_nt, 2 * c + 2)
                end = (c + 1) * CH - 1
                for j in range(2):
                    for hh in range(2):
                        r = slice(64 * hh, 64 * hh + 64)
                        dec = inter[r, j, end:end + 1]
                        dve.scalar_tensor_tensor(c_st[r, j, r], c_st[r, j, r], dec,
                                                 pm[r, 1, 256 + j * P + 64 * hh:256 + j * P + 64 * hh + 64],
                                                 ALU.mult, ALU.add)
                        last = dve.scalar_tensor_tensor(n_st[r, j, r], n_st[r, j, r], dec,
                                                        pm[r, 2, 256 + 2 * j:257 + 2 * j].to_broadcast([64, 64]),
                                                        ALU.mult, ALU.add)
                link(last)
                dve.sem_inc(mc_sv, 1)

            def msample(_):
                inter, em = slot(2, 2)[:, :, S0:T], slot(4, 2)[:, :, S0:T]
                w = tiny[:, 0:16].rearrange("p (j b) -> p j b", j=2)
                q, k = slot(10, 2)[:, :, S0:T], slot(16, 2)[:, :, S0:T]
                dve.wait_ge(mc_nt, 2 * NC)
                for j in range(2):
                    for hh in range(2):
                        link(dve.tensor_copy(oc('np', j)[64 * hh:64 * hh + 64], n_st[64 * hh:64 * hh + 64, j, 64 * hh:64 * hh + 1]))
                link(tt(w, w, k, ALU.mult))
                ns = oc('ns', 0, 16).rearrange("p (j b) -> p j b", j=2)
                link(tt(ns, pc('n0', 0, 16).rearrange("p (j b) -> p j b", j=2), inter, ALU.mult))
                link(tt(ns, ns, w, ALU.add))
                link(tt(tiny[:, 16:32].rearrange("p (j b) -> p j b", j=2), ns, q, ALU.mult))
                dve.wait_ge(st_ld, 32)
                sample(1, inter, w, q, 2, st_slot[1], q)
                dve.sem_inc(ss_v, 1)
                dve.wait_ge(ss_a, 2)
                d = tiny[:, 32:48].rearrange("p (j b) -> p j b", j=2)
                link(tt(d, d, em, ALU.max))
                link(dve.reciprocal(d, d))
                link(tt(q, q, d, ALU.mult))
                dve.sem_inc(ss_v, 1)

            steps = dict(job=lambda _: None, rows=rows, conv=conv, gate=lambda _: None, lru=lru, rope=rope,
                         vt=lambda _: None, attn=attn, sattn=sattn, hprep=hprep, hchunk=hchunk, hsample=hsample,
                         hnorm=lambda _: gnorm(0, 11, 0, 'hg', 6), mprep=mprep, mchunk=mchunk, msample=msample,
                         mnorm=lambda _: gnorm(1, 18, 10, 'mg', 18))
            dve.wait_ge(cst_ld, 16)
            with dve.Fori(0, LAYERS) as l:
                dve.wait_ge(par_ld, 16)
                norm(0)
                for what, i in ORDER:
                    steps[what](i)
                dve.wait_ge(h_ld, 16)
                for n in range(N_OUT):
                    for t in range(3):
                        cols = slice(t * TT, (t + 1) * TT)
                        dve.wait_ge(mm[t], N_WIN + n + 1)
                        tt(res[:, n, cols], res[:, n, cols], pj[:, t, 0:TT], ALU.add).then_inc(ev[t], 1)
                norm(1)
                with dve.Fori(0, FF_STEPS) as i:
                    U0 = N_WIN + N_OUT
                    for q in range(4):
                        for t in range(3):
                            dve.wait_ge(ev[t], i * 12 + (U0 + q + 1))
                        r = relu[:, q % 2, :]
                        if q >= 2:
                            dve.wait_ge(ff_l, i * 4 + (q - 1))
                        tt(hsq[:, q % 2, :], r, r, ALU.mult).then_inc(ff_q, 1)
                    for n in range(KT):
                        for t in range(3):
                            cols = slice(t * TT, (t + 1) * TT)
                            dve.wait_ge(mm[t], i * 12 + (U0 + 4 + n + 1))
                            tt(res[:, n, cols], res[:, n, cols], pj[:, t, 0:TT], ALU.add).then_inc(ev[t], 1)
                u = N_WIN + N_OUT + 12 * FF_STEPS
                for half in range(2):
                    u += 4
                    for m in range(4):
                        u += 1
                        for t in range(3):
                            dve.wait_ge(ev[t], u)
                        link(tt(ple_sig[:], ple_sig[:], ple_proj[:, m, :], ALU.mult))
                        tt(res[:, 4 * half + m, :], res[:, 4 * half + m, :], ple_sig[:], ALU.add).then_inc(pv, 1)
                layer_end(dve)


def _tiles(w, k0, n):
    K, M = w.shape
    return w.reshape(K // P, P, M // P, P).transpose(1, 2, 0, 3).reshape(P, -1)


def _weights(w_in, w_out, w_up, w_down, w_gate, w_proj):
    W = np.zeros((LAYERS, N_JOBS, P, KT * P), np.float32)
    off = dict(ax=0, ag=256, q=512, k=768, bv=896, cq=1024, cf=1280, ci=1536, cg=1792, dq=2048, dk=2304,
               dv=2560, do=2816, gates=3072)
    h = np.arange(64)
    pair = [np.concatenate([h + 64 * g, h + 128 + 64 * g]) for g in range(2)]
    for l in range(LAYERS):
        for name, j in JOB.items():
            if name == 'gates':
                w = np.zeros((D, P), np.float32)
                w[:, 0:4] = w_in[l][:, 3072:3076]
                w[:, 32:36] = w_in[l][:, 3076:3080]
            elif name in ('q0', 'q1'):
                w = w_in[l][:, 512 + pair[int(name[1])]]
            elif name in off:
                w = w_in[l][:, off[name]:off[name] + P]
            else:
                a = off[name[:-1]] + P * int(name[-1])
                w = w_in[l][:, a:a + P]
            W[l, j] = _tiles(w, 0, 1)
        rows = np.arange(D)
        rows[256:512] = 256 + np.concatenate(pair)
        for m in range(KT):
            W[l, N_WIN + m] = _tiles(w_out[l][rows][:, m * P:(m + 1) * P], 0, 1)
        j = N_WIN + N_OUT
        for f in range(FF_STEPS):
            for q in range(4):
                a = (4 * f + q) * P
                W[l, j] = _tiles(w_up[l][:, a:a + P], 0, 1)
                j += 1
            for q in range(4):
                W[l, j] = _tiles(w_down[l][f * 512:(f + 1) * 512, q * 256:(q + 1) * 256], 0, 2)
                j += 1
        for half in range(2):
            W[l, j] = _tiles(w_proj[l][:, half * 512:(half + 1) * 512], 0, 4)
            j += 1
            for m in range(4):
                a = (4 * half + m) * P
                W[l, j] = _tiles(w_gate[l][:, a:a + P], 0, 1)
                j += 1
    return W


def _cols(x, s):
    a = np.concatenate([x, s], axis=-2)
    a = a.reshape(a.shape[:-1] + (a.shape[-1] // P, P))
    return np.ascontiguousarray(np.moveaxis(a, -3, -1).swapaxes(-3, -2))


def _constants():
    c = np.zeros((P, N_CONST), np.float32)
    p, f = np.arange(P)[:, None], np.arange(P)[None, :]
    c[:, 0:P] = p == f
    c[:, C_ONE:C_ONE + P] = 1.0
    c[:, C_BLK:C_BLK + P] = p // 64 == f // 64
    same = p // 64 == f // 64
    c[:, C_ROT:C_ROT + P] = np.where(same & (f % 64 < 8) & (p == f + 8), -1.0, 0.0) + \
        np.where(same & (f % 64 >= 8) & (f % 64 < 16) & (p == f - 8), 1.0, 0.0)
    c[:, C_MD:C_MD + P] = np.where(p <= f, 0.0, NEG)
    c[:, C_MP:C_MP + P] = np.where(f > p, 0.0, NEG)
    c[:, C_MC:C_MC + P] = np.where(f <= p, 0.0, NEG)
    c[:, C_EYE:C_EYE + 64] = p % 64 == np.arange(64)[None, :]
    for j in range(2):
        c[:, C_SEL + j * P:C_SEL + (j + 1) * P] = p % 32 == 2 * j + f // 64
    for l in range(NLEV):
        b = 1 << l
        t = np.arange(P)[(np.arange(P) // b) % 2 == 1][None, :]
        c[:, C_LEV + 64 * l:C_LEV + 64 * l + 64] = ((p // b) % 2 == 0) & (p // (2 * b) == t // (2 * b))
    return c


def _rope_table():
    inv = np.power(np.float32(500000.0), -np.arange(8, dtype=np.float32) * np.float32(2.0 / 16))
    pos = np.concatenate([np.arange(SEQ), np.full(DEC, 1024)]).astype(np.float32)
    ang = (pos[:, None] * inv[None, :]).astype(np.float32)
    r = np.zeros((P, 2, T), np.float32)
    r[:, 0] = 1.0
    for d in range(P):
        if d % 64 < 16:
            r[d, 0] = np.cos(ang[:, d % 8])
            r[d, 1] = np.sin(ang[:, d % 8])
    return r


def _layout(i):
    L = LAYERS

    def chan(a):
        return a.reshape((L, -1, P) + a.shape[2:]).swapaxes(1, 2)

    par = np.zeros((L, P, N_PAR), np.float32)

    def put(name, a):
        a = a.reshape(L, a.shape[1], -1)
        par[:, :a.shape[1], PC[name]:PC[name] + a.shape[2]] = a

    put('g1', chan(i['norm1_g']))
    put('g2', chan(i['norm2_g']))
    put('cw', chan(i['conv_w'].transpose(0, 2, 1)).transpose(0, 1, 3, 2))
    for n, k in (('cb', 'conv_b'), ('br', 'lru_br'), ('bi', 'lru_bi'), ('lam', 'lru_lam')):
        put(n, chan(i[k]))
    for n, k in (('qg', 'q_norm_g'), ('kg', 'k_norm_g'), ('hg', 'hgrn_norm_g'), ('mg', 'mlstm_norm_g')):
        put(n, np.tile(i[k], (1, 2))[:, :, None])
    gam = chan(i['hgrn_gamma'])
    for l in range(L):
        par[l, :, PC['gam']:PC['gam'] + 4] = gam.transpose(1, 0, 2).reshape(P, 4)
        par[l, :, PC['lm']] = float(l > 0)
        par[l, :, PC['sink']:PC['sink'] + 4] = i['attn_sinks'][l][None, :]
    put('sinkc', i['attn_sinks'][:, :, None])
    put('ib', i['mlstm_ib'][:, :, None])
    put('fb', i['mlstm_fb'][:, :, None])
    for n, k in (('wr', 'lru_wr'), ('wi', 'lru_wi')):
        for j in range(2):
            for h in range(2):
                a = PC[n] + j * P + 64 * h
                par[:, 64 * h:64 * h + 64, a:a + 64] = i[k][:, 2 * j + h]
    put('conv', chan(i['state_rglru_conv'].transpose(0, 3, 2, 1)))
    put('h0', chan(i['state_rglru_h'].transpose(0, 2, 1)))
    put('n0', chan(i['state_mlstm_n'].reshape(L, DEC, 256).transpose(0, 2, 1)))
    put('m0', i['state_mlstm_m'].transpose(0, 2, 1))

    def state(a):
        return np.ascontiguousarray(chan(a.transpose(0, 2, 3, 1, 4).reshape(L, 256, DEC, 64)).reshape(L, P, 1024))

    kc = i['cache_swa_k'].reshape(L, DEC, P, P)[:, :, 1:]
    vc = i['cache_swa_v'].reshape(L, DEC, P, P)[:, :, 1:]
    return dict(
        x=_cols(i['x_prompt'][0], i['x_sample'][:, 0]),
        consts=_constants(), rope=_rope_table(), par=par,
        w=_weights(i['w_in'], i['w_out'], i['w_up'], i['w_down'], i['w_ple_gate'], i['w_ple_proj']),
        p=_cols(i['p_prompt'][:, 0], i['p_sample'][:, :, 0]),
        kc=np.ascontiguousarray(kc.transpose(0, 3, 1, 2)), vc=np.ascontiguousarray(vc.transpose(0, 2, 1, 3)),
        hs=state(i['state_hgrn_s']), cs=state(i['state_mlstm_c']))


_OUTS = dict(y=(P, KT, T), so=(LAYERS, P, N_SO), kv=(LAYERS, P, 2, CH), kc=(LAYERS, P, DEC, P), vc=(LAYERS, P, DEC, P),
             hp=(LAYERS, P, 2, P), cp=(LAYERS, P, 2, P), hs=(LAYERS, P, 1024), cs=(LAYERS, P, 1024))


def _results(r):
    L = LAYERS
    y = r['y'].transpose(2, 1, 0).reshape(T, D)
    so = r['so']

    def part(name, *shape):
        n = int(np.prod(shape))
        return so[:, :, OC[name]:OC[name] + n].reshape((L, P) + shape)

    def unchan(a):
        return a.swapaxes(1, 2).reshape((L, 256) + a.shape[3:])

    def blocks(a):
        o = np.stack([a[:, 64 * h:64 * h + 64, j, 64 * h:64 * h + 64] for j in range(2) for h in range(2)], axis=1)
        return o[:, None]

    def states(a):
        return unchan(a.reshape(L, P, 2, DEC, 64)).reshape(L, 4, 64, DEC, 64).transpose(0, 3, 1, 2, 4)

    def cache(a):
        return np.roll(a, -1, axis=1).transpose(0, 2, 1, 3).reshape(L, DEC, P, 2, 64)

    kv = r['kv'].transpose(0, 2, 3, 1).reshape(L, 2, 1, CH, 2, 64)
    outs = (
        y[:SEQ].reshape(1, SEQ, D), y[SEQ:].reshape(DEC, 1, D),
        unchan(part('hp', 2)).reshape(L, 1, 256),
        unchan(part('convp', 2, 3)).transpose(0, 2, 1).reshape(L, 1, 3, 256),
        kv[:, 0], kv[:, 1], blocks(r['hp']), blocks(r['cp']),
        unchan(part('np', 2)).reshape(L, 1, 4, 64), part('mp', 1)[:, 0:4, 0].reshape(L, 1, 4),
        unchan(part('hs', 2, DEC)).transpose(0, 2, 1),
        unchan(part('convs', 2, 3, DEC)).transpose(0, 3, 2, 1),
        cache(r['kc'].transpose(0, 3, 2, 1)), cache(r['vc']), states(r['hs']), states(r['cs']),
        unchan(part('ns', 2, DEC)).transpose(0, 2, 1).reshape(L, DEC, 4, 64),
        part('ms', DEC)[:, 0:4].transpose(0, 2, 1))
    return tuple(np.ascontiguousarray(o) for o in outs)


def kernel(**inputs):
    import concourse.bacc as bacc
    from concourse.bass_utils import run_bass_kernel_spmd

    nc = bacc.Bacc("TRN2", target_bir_lowering=False, num_devices=1)
    arrays = {f"in_{k}": v for k, v in _layout({k: np.asarray(v) for k, v in inputs.items()}).items()}
    ins = {k: nc.dram_tensor(k, v.shape, mybir.dt.from_np(v.dtype), kind="ExternalInput").ap() for k, v in arrays.items()}
    outs = {k: nc.dram_tensor(f"out_{k}", s, F32, kind="ExternalOutput").ap() for k, s in _OUTS.items()}
    build(nc, ins['in_x'], ins['in_consts'], ins['in_rope'], ins['in_par'], ins['in_w'], ins['in_p'], ins['in_kc'],
          ins['in_vc'], ins['in_hs'], ins['in_cs'], outs['y'], outs['so'], outs['kv'], outs['kc'], outs['vc'],
          outs['hp'], outs['cp'], outs['hs'], outs['cs'])
    r = run_bass_kernel_spmd(nc, [arrays], core_ids=[0])
    return _results({k: r.results[0][f"out_{k}"] for k in _OUTS})
```

```python
from contextlib import ExitStack

import numpy as np

import concourse.bass as bass
from concourse import mybir

ALU = mybir.AluOpType
ACT = mybir.ActivationFunctionType
AX_X = mybir.AxisListType.X
F32 = mybir.dt.float32
F32R = mybir.dt.float32r
U32 = mybir.dt.uint32

P = 128
LAYERS, SEQ, DEC, D, D_FF, PLE = 2, 1024, 8, 1024, 4096, 256
T = SEQ + DEC
TT = T // 3
KT = D // P
CH = 128
NC = SEQ // CH
NLEV = 7
NEG = -1e30
EPS = 1e-6
FF_TILES = 4
FF_STEPS = D_FF // (P * FF_TILES)
WIN = ['gates', 'ax0', 'ax1', 'ag0', 'ag1', 'q0', 'q1', 'k', 'bv', 'ci0', 'ci1', 'dv0', 'dv1',
       'dq0', 'dq1', 'do0', 'do1', 'cf0', 'cf1', 'cq0', 'cq1', 'cg0', 'cg1', 'dk0', 'dk1']
JOB = {name: j for j, name in enumerate(WIN)}
SLOT = dict(ax0=10, ax1=11, ag0=12, ag1=13, q0=14, q1=15, k=16, bv=17, ci0=18, ci1=19, dv0=4, dv1=5,
            dq0=10, dq1=11, cq0=0, cq1=1, cf0=2, cf1=3, cg0=6, cg1=7, dk0=16, dk1=17, do0=18, do1=19)
VT_COL = dict(bv=0, ci0=128, ci1=256, dv0=384, dv1=512)
N_WIN, N_OUT, N_FF, N_PLE = len(WIN), KT, FF_STEPS * 8, KT + 2
N_JOBS = N_WIN + N_OUT + N_FF + N_PLE

LEV_AT = [(0, 128), (0, 192), (2, 0), (2, 64), (2, 128), (2, 192), (0, 0)]

Y_SLOT = (12, 13, 14, 15, 0, 1, 10, 11)

C_ID, C_ONE, C_BLK, C_ROT, C_MD, C_MP, C_MC, C_EYE, C_LEV = 0, 128, 256, 384, 512, 640, 768, 896, 960
C_SEL = C_LEV + NLEV * 64
N_CONST = C_SEL + 2 * P
_sizes = dict(g1=8, g2=8, cw=8, cb=2, br=2, bi=2, lam=2, qg=1, kg=1, hg=1, mg=1, gam=4, lm=1, sink=4,
              sinkc=1, ib=1, fb=1, wr=256, wi=256, conv=48, h0=16, n0=16, m0=8)
PC, N_PAR = {}, 0
for _n, _s in _sizes.items():
    PC[_n] = N_PAR
    N_PAR += _s
_sizes = dict(convp=6, convs=48, hp=2, hs=16, np=2, ns=16, mp=1, ms=8)
OC, N_SO = {}, 0
for _n, _s in _sizes.items():
    OC[_n] = N_SO
    N_SO += _s

def _order():
    o = [('job', 0), ('rows', 0), ('job', 1), ('rows', 1), ('job', 2), ('job', 3), ('rows', 2), ('job', 4), ('rows', 3),
         ('conv', 0), ('job', 5), ('job', 6), ('gate', 0), ('lru', 0), ('job', 7), ('job', 8), ('rope', 0), ('vt', 0)]
    fill = [[('job', 9)], [('vt', 1)], [('job', 10)], [('vt', 2), ('job', 11)], [], [('vt', 3), ('job', 12)],
            [('job', 13)], [('vt', 4)], [('job', 14)], []]
    for c in range(NC + 2):
        o += [('attn', c)] + fill[c]
    o += [('sattn', 0), ('job', 15), ('sattn', 1), ('job', 16), ('sattn', 2), ('job', 17), ('job', 18), ('hprep', 0), ('job', 19),
          ('job', 20)]
    for c in range(NC):
        o += [('hchunk', c)] + ([('job', 21 + c // 2)] if c % 2 == 0 else [])
    o += [('hsample', 0), ('hnorm', 0), ('mprep', 0)]
    return o + [('mchunk', c) for c in range(NC + 1)] + [('msample', 0), ('mnorm', 0)]


ORDER = _order()


def build(nc, x_in, consts, rope_in, par_in, w_in, p_in, kc_in, vc_in, hs_in, cs_in,
          y_out, so_out, kv_out, kc_out, vc_out, hp_out, cp_out, hs_out, cs_out):
    with ExitStack() as ctx:
        def sem(name):
            s = ctx.enter_context(nc.semaphore(name))
            sems.append(s)
            return s

        def sb(name, shape, dt=F32, stack=ctx):
            return stack.enter_context(nc.sbuf_tensor(name, shape, dt))

        sems = []
        h_saved = nc.dram_tensor("h_saved", (P, KT, T), F32, kind="Internal").ap()
        pj = ctx.enter_context(nc.psum_tensor("pj", [P, 3, 512], F32))
        pm = ctx.enter_context(nc.psum_tensor("pm", [P, 5, 512], F32))

        res = sb("res", [P, KT, T])
        n_hi, n_lo = sb("n_hi", [P, KT, T], F32R), sb("n_lo", [P, KT, T], F32R)
        w_raw = sb("w_raw", [P, 2, KT * P])
        w_hi, w_lo = sb("w_hi", [P, 2, KT * P], F32R), sb("w_lo", [P, 2, KT * P], F32R)
        cst, par, so = sb("cst", [P, N_CONST]), sb("par", [P, N_PAR]), sb("so", [P, N_SO])
        ex2, qe = sb("ex2", [P, 2, 2, CH]), sb("qe", [P, 2, CH])
        ktok, att = sb("ktok", [P, 2, CH]), sb("att", [P, 4, CH])
        h_st, c_st = sb("h_st", [P, 2, P]), sb("c_st", [P, 2, P])
        n_st = h_st
        v_smp = sb("v_smp", [P, 4, DEC])
        bw = sb("bw", [P, NC, 2, 4])
        tiny = sb("tiny", [P, 48])
        with ExitStack() as mixer:
            ext = sb("ext", [P, 12, T], stack=mixer)
            vt = sb("vt", [P, NC, 640], stack=mixer)
        with ExitStack() as ff:
            hid_hi = sb("hid_hi", [P, FF_TILES, T], F32R, ff)
            hid_lo = sb("hid_lo", [P, FF_TILES, T], F32R, ff)
            relu = sb("relu", [P, 2, T], stack=ff)
            hsq = sb("hsq", [P, 2, T], stack=ff)
        with ExitStack() as ple:
            ple_hi, ple_lo = sb("ple_hi", [P, 2, T], F32R, ple), sb("ple_lo", [P, 2, T], F32R, ple)
            ple_raw = sb("ple_raw", [P, 2, T], stack=ple)
            ple_proj = sb("ple_proj", [P, 4, T], stack=ple)
            ple_sig = sb("ple_sig", [P, T], stack=ple)

        def slot(a, n=1):
            t = res[:, a:a + n, :] if a < KT else ext[:, a - KT:a - KT + n, :]
            return t if n > 1 else t[:, 0, :]

        def flat(a, n=1):
            return (res[:, a:a + n, :] if a < KT else ext[:, a - KT:a - KT + n, :]).rearrange("p a t -> p (a t)")

        def pc(name, i=0, n=1):
            return par[:, PC[name] + i:PC[name] + i + n]

        def oc(name, i=0, n=1):
            return so[:, OC[name] + i:OC[name] + i + n]

        ident, ones, blk = cst[:, 0:P], cst[:, C_ONE:C_ONE + P], cst[:, C_BLK:C_BLK + P]
        rot, mask_d = cst[:, C_ROT:C_ROT + P], cst[:, C_MD:C_MD + P]
        eye, sel = cst[:, C_EYE:C_EYE + 64], cst[:, C_SEL:C_SEL + 2 * P]
        three = "p (a t) -> p a t"
        pm3 = pm[:, 0:3, 0:TT]
        S0 = SEQ

        w_ld = [sem("w_ld0"), sem("w_ld1")]
        hi_made, lo_made = sem("hi_made"), sem("lo_made")
        mm = [sem(f"mm{t}") for t in range(3)]
        ev = [sem(f"ev{t}") for t in range(3)]
        cst_ld, par_ld, rope_ld, h_out = (sem(n) for n in ("cst_ld", "par_ld", "rope_ld", "h_out"))
        h_ld, ff_l3, mc_c = [sem("h_ld0"), sem("h_ld1")], sem("ff_l3"), sem("mc_c")
        smp_ld, st_ld, ple_ld = sem("smp_ld"), sem("st_ld"), sem("ple_ld")
        mix_mm, mix_ev = sem("mix_mm"), sem("mix_ev")
        nrm_sq, nrm_mm, nrm_rs, nrm_n = (sem("nrm_" + n) for n in ("sq", "mm", "rs", "n"))
        nrm_hi, nrm_lo = sem("nrm_hi"), sem("nrm_lo")
        rows_a, rows_v, rows_t, rows_c = (sem("rows_" + n) for n in "avtc")
        conv_v, lru_a, lru_v = sem("conv_v"), sem("lru_a"), sem("lru_v")
        rope_a, rope_v = sem("rope_a"), sem("rope_v")
        vt_t, vt_c = sem("vt_t"), sem("vt_c")
        at_s, at_m, at_e, at_p, at_t, at_c, at_o, at_w = (sem("at_" + n) for n in
                                                          ("s", "m", "e", "p", "t", "c", "o", "w"))
        sa_v, sa_t, sa_a, sa_x = sem("sa_v"), sem("sa_t"), sem("sa_a"), sem("sa_x")
        hp_v, hp_a = sem("hp_v"), sem("hp_a")
        hc_subk, hc_kk = sem("hc_subk"), sem("hc_kk")
        hc_sub, hc_exp, hc_kq, hc_lt, hc_lv, hc_tt, hc_tc, hc_ot, hc_oc, hc_sv = (
            sem("hc_" + n) for n in ("sub", "exp", "kq", "lt", "lv", "tt", "tc", "ot", "oc", "sv"))
        ss_v, ss_t, ss_a = sem("ss_v"), sem("ss_t"), sem("ss_a")
        nm_a, nm_v = sem("nm_a"), sem("nm_v")
        mp_a = sem("mp_a")
        mc_t, mc_w, mc_s, mc_tt, mc_k, mc_q, mc_nt, mc_d, mc_h, mc_sv = (
            sem("mc_" + n) for n in ("t", "w", "s", "tt", "k", "q", "nt", "d", "h", "sv"))
        y_hi, y_lo = sem("y_hi"), sem("y_lo")
        ff_r, ff_q, ff_h, ff_l = sem("ff_r"), sem("ff_q"), sem("ff_h"), sem("ff_l")
        ph, pl, pg, pv = sem("ph"), sem("pl"), sem("pg"), sem("pv")
        kv_st, so_st, smp_st, mix_st = sem("kv_st"), sem("so_st"), sem("smp_st"), sem("mix_st")
        ch_a, ch_v, ch_g = sem("ch_a"), sem("ch_v"), sem("ch_g")
        clearable = sems[:]
        clearable.remove(cst_ld)
        arrived, go, left = sem("arrived"), sem("go"), sem("left")
        y_st = sem("y_st")

        def linker(eng, s):
            n = [0]

            def link(ins):
                n[0] += 1
                ins.then_inc(s, 1)
                eng.wait_ge(s, n[0])
            return link

        def layer_end(eng):
            eng.drain().then_inc(arrived, 1)
            eng.wait_ge(go, 1)
            eng.sem_inc(left, 1)

        early = vt[:, :, 0:CH]

        def level(l):
            if l < 4:
                return early[:, 2 * l:2 * l + 2, :]
            return (c_st[:] if l == 4 else pc('wr', (l - 5) * 256, 256).rearrange("p (j t) -> p j t", j=2))

        def halves(x, l):
            v = x.rearrange("p j (n two b) -> p j n two b", two=2, b=1 << l)
            return v[:, :, :, 0, :], v[:, :, :, 1, :]

        GROUPS = ((0, 1), (2, 3, 4, 5), (6,))

        def sm_half(g, h):
            if g:
                return flat(7)[:, 512 * h:512 * h + 512]
            return early[:, 4 * h:4 * h + 4, :]

        def sm_state(g, j):
            if g:
                return flat(6)[:, 512 * j:512 * j + 512]
            return ex2[:].rearrange("p a j t -> p (a j t)") if j else pc('wr', 0, 512)

        mc_att = (att[:], pc('wr', 0, 512).rearrange("p (i t) -> p i t", i=4))
        mc_qe, mc_kt = (qe[:], early[:, 2:4, :]), (ktok[:], early[:, 4:6, :])

        block = ctx.enter_context(nc.Block())

        @block.sync
        def _(sp):
            sp.dma_start(cst[:], consts).then_inc(cst_ld, 16)
            sp.dma_start(res[:], x_in).then_inc(y_st, 16)
            sp.wait_ge(y_st, 16)

            with sp.Fori(0, LAYERS) as l:
                def load(j, wait):
                    if wait:
                        sp.wait_ge(hi_made, j - 1)
                        sp.wait_ge(lo_made, j - 1)
                    sp.dma_start(w_raw[:, j % 2, :], w_in[l, j]).then_inc(w_ld[j % 2], 16)

                sp.dma_start(par[:], par_in[l]).then_inc(par_ld, 16)
                load(0, False)
                load(1, False)
                sp.dma_start(h_saved, res[:]).then_inc(h_out, 16)
                sp.dma_start(slot(18, 2), rope_in).then_inc(rope_ld, 16)
                for j in range(2, N_WIN + N_OUT):
                    load(j, True)
                with sp.Fori(0, FF_STEPS) as i:
                    for q in range(8):
                        j0 = N_WIN + N_OUT + q
                        sp.wait_ge(hi_made, i * 8 + (j0 - 1))
                        sp.wait_ge(lo_made, i * 8 + (j0 - 1))
                        sp.dma_start(w_raw[:, j0 % 2, :], w_in[l, i * 8 + j0]).then_inc(w_ld[j0 % 2], 16)
                for j in range(N_WIN + N_OUT + N_FF, N_JOBS):
                    load(j, True)
                sp.wait_ge(arrived, 4)
                for s in clearable + [arrived]:
                    sp.sem_clear(s)
                sp.sem_inc(go, 4)
                sp.wait_ge(left, 4)
                sp.sem_clear(left)
                sp.sem_clear(go)
            sp.dma_start(y_out, res[:]).then_inc(y_st, 16)
            sp.wait_ge(y_st, 32)

        @block.tensor
        def _(pe):
            def unit(par_j, k0, nk, hi, lo, u, first_waits=None, vals=None, tail=0):
                for ks in ((range(nk),) if not tail else (range(nk - tail), range(nk - tail, nk))):
                    for t in range(3):
                        if ks[0] == 0 and (vals is not None or u):
                            pe.wait_ge(ev[t], u if vals is None else vals)
                        cols = slice(t * TT, (t + 1) * TT)
                        for k in ks:
                            if first_waits is not None and t == 0:
                                first_waits(k)
                            ws = slice((k0 + k) * P, (k0 + k + 1) * P)
                            wh, wl = w_hi[:, par_j, ws], w_lo[:, par_j, ws]
                            pe.matmul(pj[:, t, 0:TT], wh, hi[:, k, cols], start=(k == 0), stop=False)
                            pe.matmul(pj[:, t, 0:TT], wh, lo[:, k, cols], start=False, stop=False)
                            last = pe.matmul(pj[:, t, 0:TT], wl, hi[:, k, cols], start=False, stop=(k == nk - 1))
                        if ks[-1] == nk - 1:
                            last.then_inc(mm[t], 1)

            def mix(n, lhs, rhs):
                if n > 1:
                    pe.wait_ge(mix_ev, n - 1)
                for t in range(3):
                    last = pe.matmul(pm[:, t, 0:TT], lhs, rhs[:, t * TT:(t + 1) * TT], start=True, stop=True)
                last.then_inc(mix_mm, 1)

            def norm(i):
                pe.wait_ge(cst_ld, 16)
                if i:
                    pe.wait_ge(mix_ev, 19)
                for k in range(KT):
                    pe.wait_ge(nrm_sq, KT * i + k + 1)
                    for t in range(3):
                        last = pe.matmul(pm[:, t, 0:TT], ones, ext[:, k % 2, t * TT:(t + 1) * TT],
                                         start=(k == 0), stop=(k == KT - 1))
                    last.then_inc(nrm_mm, 1)

            def job(j):
                pe.wait_ge(lo_made, j + 1)
                unit(j % 2, 0, KT, n_hi, n_lo, j,
                     (lambda k: pe.wait_ge(nrm_lo, k + 1)) if j == 0 else None)

            def rows(i):
                if i < 3:
                    return
                pe.wait_ge(rows_v, 9)
                for c in range(NC):
                    pe.matmul(pm[:, 3, c * 8:c * 8 + 4], slot(6)[0:4, c * CH:(c + 1) * CH], ident[0:4, 0:4],
                              is_transpose=True, start=True, stop=True)
                    last = pe.matmul(pm[:, 4, c * 8:c * 8 + 4], slot(6)[32:36, c * CH:(c + 1) * CH],
                                     ident[32:36, 32:36], is_transpose=True, start=True, stop=True)
                last.then_inc(rows_t, 1)

            def gate(_):
                pe.wait_ge(conv_v, 1)
                for n, (w, j) in enumerate((('wr', 0), ('wr', 1), ('wi', 0), ('wi', 1))):
                    if n == 0:
                        pe.wait_ge(nrm_rs, 1)
                    mix_first = n + 1
                    mix(mix_first, pc(w, j * P, P), slot(j))

            def rope(_):
                for n in range(3):
                    pe.wait_ge(rope_a, n + 1)
                    mix(5 + n, blk, slot(n))
                for n in range(3):
                    pe.wait_ge(rope_v, n + 1)
                    mix(8 + n, rot, slot(14 + n))

            def vtrans(v):
                src = slot(SLOT[list(VT_COL)[v]])
                pe.wait_ge(ev[2], JOB[list(VT_COL)[v]] + 1)
                if v == 0:
                    pe.wait_ge(rows_c, 2)
                if attn_before[v]:
                    pe.wait_ge(at_o, attn_before[v])
                for h in range(2):
                    if 2 * v + h >= 1:
                        pe.wait_ge(vt_c, 2 * v + h)
                    for q in range(4):
                        c = 4 * h + q
                        last = pe.transpose(pm[:, 4, q * P:(q + 1) * P], src[:, c * CH:(c + 1) * CH], ident)
                    last.then_inc(vt_t, 1)

            def attn(step):
                c = step
                if c < NC:
                    if c == 0:
                        pe.wait_ge(mix_ev, 10)
                        pe.wait_ge(rope_v, 6)
                    else:
                        pe.wait_ge(at_m, c)
                    lo_k = 0 if c else CH
                    for j in range(2):
                        for hh in range(2):
                            r = slice(64 * hh, 64 * hh + 64)
                            last = pe.matmul(pm[:, hh, j * 256 + lo_k:j * 256 + 256],
                                             slot(14 + j)[r, c * CH:(c + 1) * CH],
                                             slot(16)[r, (c - 1) * CH + lo_k:(c + 1) * CH], start=True, stop=True)
                    last.then_inc(at_s, 1)
                c = step - 2
                if c >= 0:
                    pt = flat(2 + c % 2)[:, 0:1024].rearrange("p (i h t) -> p i h t", i=4, h=2)
                    pe.wait_ge(at_c, c + 1)
                    pe.wait_ge(vt_c, max(2, vt_before[step]))
                    if c:
                        pe.wait_ge(at_o, c)
                    for j in range(2):
                        for hh in range(2):
                            for h in range(0 if c else 1, 2):
                                last = pe.matmul(pm[64 * hh:64 * hh + 64, 4, j * CH:(j + 1) * CH],
                                                 vt[:, c - 1 + h, 64 * hh:64 * hh + 64], pt[:, 2 * hh + j, h, :],
                                                 start=(h == (0 if c else 1)), stop=(h == 1))
                    last.then_inc(at_w, 1)
                c = step - 1
                if 0 <= c < NC:
                    pe.wait_ge(at_p, c + 1)
                    if c:
                        pe.wait_ge(at_c, c)
                    sc = flat(c % 2)[:, 0:1024].rearrange("p (i s) -> p i s", i=4)
                    for i in range(4):
                        for h in range(0 if c else 1, 2):
                            last = pe.transpose(pm[:, 2 + i // 2, (i % 2 * 2 + h) * P:(i % 2 * 2 + h + 1) * P],
                                                sc[:, i, h * CH:(h + 1) * CH], ident)
                    last.then_inc(at_t, 1)

            vt_before, attn_before, n, m = {}, {}, 0, 0
            for what, i in ORDER:
                if what == 'vt':
                    n, attn_before[i] = n + 2, m
                if what == 'attn':
                    vt_before[i], m = n, max(0, i - 1)

            def sattn(part):
                kc = flat(6)[:, 0:1024].rearrange("p (b s) -> p b s", b=DEC)
                qb = flat(0)[:, 0:32].rearrange("p (b i) -> p b i", b=DEC)
                pr = flat(2)[0:4, 0:1024].rearrange("p (b s) -> p b s", b=DEC)
                vc = flat(7)[:, 0:1024].rearrange("p (b d) -> p b d", b=DEC)
                if part == 0:
                    pe.wait_ge(at_o, NC)
                    pe.wait_ge(sa_v, 1)
                    pe.wait_ge(vt_c, 10)
                    for b in range(DEC):
                        last = pe.matmul(pm[0:1, b // 4, (b % 4) * P:(b % 4 + 1) * P], slot(17)[:, S0 + b:S0 + b + 1],
                                         ident, start=True, stop=True)
                    last.then_inc(sa_t, 1)
                    for b in range(DEC):
                        last = pe.matmul(pm[0:4, 2 + b // 4, (b % 4) * P:(b % 4 + 1) * P], qb[:, b, :], kc[:, b, :],
                                         start=True, stop=True)
                    last.then_inc(sa_t, 1)
                elif part == 1:
                    pe.wait_ge(sa_v, 2)
                    for b in range(DEC):
                        last = pe.transpose(pm[:, 4, b * 4:b * 4 + 4], pr[:, b, :], ident[0:4, 0:4])
                    last.then_inc(sa_t, 1)
                else:
                    pe.wait_ge(sa_v, 3)
                    pe.wait_ge(sa_a, 1)
                    for b in range(DEC):
                        last = pe.matmul(pm[:, 4, 64 + b * 4:64 + b * 4 + 4], vc[:, b, :],
                                         flat(3)[:, b * 4:b * 4 + 4], start=True, stop=True)
                    last.then_inc(sa_t, 1)

            def hchunk(c):
                if c == 0:
                    pe.wait_ge(sa_v, 4)
                    pe.wait_ge(hp_v, 1)
                    for t in range(3):
                        pe.wait_ge(ev[t], JOB['cq1'] + 1)
                else:
                    pe.wait_ge(hc_lv, 8 * c)
                q, k = slot(0, 2), slot(4, 2)
                cc = slice(c * CH, (c + 1) * CH)
                for j in range(2):
                    for hh in range(2):
                        r = slice(64 * hh, 64 * hh + 64)
                        pe.matmul(pm[:, hh, j * 256:j * 256 + 128], k[r, j, cc], q[r, j, cc], start=True, stop=True)
                for g, levels in enumerate(GROUPS):
                    pe.wait_ge(hc_kq, 3 * c + g + 1)
                    pe.wait_ge(hc_kk, 3 * c + g + 1)
                    if g == 1 and c:
                        pe.wait_ge(hc_oc, c)
                        pe.wait_ge(hc_sv, c)
                    if g == 2:
                        pe.wait_ge(hc_lv, 8 * c + 3)
                    for l in levels:
                        bank, at = LEV_AT[l]
                        el, half = level(l), 1 << l
                        for j in range(2):
                            for hh in range(2):
                                r = slice(64 * hh, 64 * hh + 64)
                                rhs = el[r, j, :].rearrange("p (n two b) -> p n two b", two=2, b=half)[:, :, 1, :]
                                out = pm[:, bank + hh, j * 256 + at:j * 256 + at + 64]
                                last = pe.matmul(out.rearrange("p (n b) -> p n b", b=half), el[r, j, :], rhs,
                                                 start=True, stop=True)
                    last.then_inc(hc_lt, 1)
                if c:
                    pe.wait_ge(hc_tc, c)
                for j in range(2):
                    last = pe.transpose(pm[:, 4, j * P:(j + 1) * P], ex2[:, 1, j, :], ident)
                last.then_inc(hc_tt, 1)
                pe.wait_ge(hc_lv, 8 * (c + 1))
                for j in range(2):
                    pe.matmul(pm[:, 2, j * CH:(j + 1) * CH], h_st[:, j, :], qe[:, j, :], start=True, stop=False,
                              skip_group_check=True)
                    for hh in range(2):
                        v0 = 128 + (2 * j + hh) * 64
                        last = pe.matmul(pm[64 * hh:64 * hh + 64, 2, j * CH:(j + 1) * CH], vt[:, c, v0:v0 + 64],
                                         att[:, 2 * hh + j, :], start=False, stop=(hh == 1), skip_group_check=True)
                last.then_inc(hc_ot, 1)
                pe.wait_ge(hc_tc, c + 1)
                for j in range(2):
                    last = pe.matmul(pm[:, 3, j * P:(j + 1) * P], ktok[:, j, :], vt[:, c, 128 + j * P:128 + (j + 1) * P],
                                     start=True, stop=True)
                last.then_inc(hc_ot, 1)

            def sample(g, prev):
                def bank(g, b):
                    return pm[:, b, :] if g else pm[:, b, :].rearrange("p (c t) -> p c t", c=DEC // 2)

                for j in range(2):
                    pe.wait_ge(ss_v, 5 * g + 2 * j + 1)
                    pe.matmul(bank(g, j), blk, sm_half(g, 0), start=True, stop=True).then_inc(ss_t, 1)
                    pe.wait_ge(ss_v, 5 * g + 2 * j + 2)
                    pe.matmul(bank(g, 2 + j), blk, sm_half(g, 1), start=True,
                              stop=True).then_inc(ss_t, 1)

            def hsample(_):
                pe.wait_ge(hc_oc, NC)
                pe.wait_ge(hc_sv, NC)
                sample(0, 0)

            def gnorm(g, n0):
                for j in range(2):
                    pe.wait_ge(nm_a, 2 * g + j + 1)
                    if j == 0:
                        pe.wait_ge(ss_v, 5 * g + 5)
                    mix(n0 + j, blk, slot(2 + j))

            def mprep(_):
                pe.wait_ge(nm_v, 1)
                for j in range(2):
                    mix(13 + j, sel[0:4, j * P:(j + 1) * P], slot(9)[0:4, :])
                for j in range(2):
                    mix(15 + j, sel[32:36, j * P:(j + 1) * P],
                        slot(8)[32:36, :])
                pe.wait_ge(mix_ev, 16)
                for j in range(2):
                    last = pe.matmul(pm[:, 3, j * 8:j * 8 + 8],
                                     sel[0:4, j * P:(j + 1) * P],
                                     slot(8)[0:4, S0:S0 + 8], start=True, stop=True)
                last.then_inc(mix_mm, 1)

            def mchunk(step):
                q, k = slot(10, 2), slot(16, 2)
                c = step
                if c < NC:
                    cc = slice(c * CH, (c + 1) * CH)
                    if c == 0:
                        pe.wait_ge(mix_ev, 17)
                        for t in range(3):
                            pe.wait_ge(ev[t], N_WIN)
                    else:
                        pe.wait_ge(mc_w, c)
                        pe.wait_ge(mc_s, c)
                        pe.wait_ge(mc_k, c)
                    pe.matmul(pj[:, 0, :], ident, mask_d.unsqueeze(1).to_broadcast([P, 4, CH]), start=True, stop=False,
                              skip_group_check=True)
                    for i in range(4):
                        head = 2 * (i % 2) + i // 2
                        last = pe.matmul(pj[:, 0, i * CH:(i + 1) * CH], ident[0:4, head:head + 1].to_broadcast([4, P]),
                                         slot(8)[0:4, cc], start=False, stop=(i == 3), skip_group_check=True)
                    last.then_inc(mc_t, 1)
                    for j in range(2):
                        for hh in range(2):
                            r = slice(64 * hh, 64 * hh + 64)
                            last = pe.matmul(pj[:, 1 + hh, j * CH:(j + 1) * CH], k[r, j, cc], q[r, j, cc],
                                             start=True, stop=True)
                    last.then_inc(mc_t, 1)
                    for j in range(2):
                        last = pe.transpose(pm[:, 2, j * P:(j + 1) * P], k[:, j, cc], ident)
                    last.then_inc(mc_tt, 1)
                c = step - 1
                if c < 0:
                    return
                a, b = mc_att[c % 2], c % 2
                pe.wait_ge(mc_q, c + 1)
                pe.wait_ge(mc_s, c + 1)
                if c >= 1:
                    pe.wait_ge(mc_sv, c)
                if c >= 2:
                    pe.wait_ge(mc_h, c - 1)
                for n, st in enumerate((c_st, n_st)):
                    for j in range(2):
                        at = (2 * n + j) * CH
                        pe.matmul(pm[:, b, at:at + CH], st[:, j, :], mc_qe[c % 2][:, j, :], start=True, stop=False,
                                  skip_group_check=True)
                        for hh in range(2):
                            v0 = 384 + (2 * j + hh) * 64
                            lhs = ones[:, 0:64] if n else vt[:, c, v0:v0 + 64]
                            last = pe.matmul(pm[64 * hh:64 * hh + 64, b, at:at + CH], lhs, a[:, 2 * hh + j, :],
                                             start=False, stop=(hh == 1), skip_group_check=True)
                last.then_inc(mc_nt, 1)
                pe.wait_ge(mc_k, c + 1)
                for j in range(2):
                    pe.matmul(pm[:, 3, j * P:(j + 1) * P], mc_kt[c % 2][:, j, :],
                              vt[:, c, 384 + j * P:384 + (j + 1) * P], start=True, stop=True)
                    last = pe.matmul(pm[:, 3, 256 + 2 * j:258 + 2 * j], mc_kt[c % 2][:, j, :], ones[:, 0:2],
                                     start=True, stop=True)
                last.then_inc(mc_nt, 1)

            def msample(_):
                pe.wait_ge(mc_h, NC)
                pe.wait_ge(mc_sv, NC)
                sample(1, 0)
                pe.wait_ge(ss_v, 10)
                for j in range(2):
                    last = pe.matmul(pm[:, 4, 384 + j * 8:392 + j * 8], blk, tiny[:, 16 + j * 8:24 + j * 8],
                                     start=True, stop=True)
                last.then_inc(ss_t, 1)

            steps = dict(job=job, rows=rows, conv=lambda _: None, gate=gate, lru=lambda _: None, rope=rope,
                         vt=vtrans, attn=attn, sattn=sattn, hprep=lambda _: None, hchunk=hchunk, hsample=hsample,
                         hnorm=lambda _: gnorm(0, 11), mprep=mprep, mchunk=mchunk, msample=msample,
                         mnorm=lambda _: gnorm(1, 18))
            with pe.Fori(0, LAYERS) as l:
                norm(0)
                for what, i in ORDER:
                    steps[what](i)
                for j in range(N_WIN, N_WIN + N_OUT):
                    pe.wait_ge(lo_made, j + 1)
                    unit(j % 2, 0, KT, n_hi, n_lo, j,
                         (lambda k: pe.wait_ge(y_lo, k + 1)) if j == N_WIN else None, tail=2 if j == N_WIN else 0)
                norm(1)
                with pe.Fori(0, FF_STEPS) as i:
                    U0 = N_WIN + N_OUT
                    for q in range(4):
                        pe.wait_ge(lo_made, i * 8 + (U0 + q + 1))
                        unit((U0 + q) % 2, 0, KT, n_hi, n_lo, 0,
                             (lambda k: pe.wait_ge(nrm_lo, KT + k + 1)) if q == 0 else None,
                             vals=i * 12 + (U0 + q))
                    for q in range(4, 8):
                        pe.wait_ge(lo_made, i * 8 + (U0 + q + 1))
                        for m in range(2):
                            unit((U0 + q) % 2, 4 * m, 4, hid_hi, hid_lo, 0,
                                 (lambda k: pe.wait_ge(ff_l, i * 3 + (k + 1)) if k < 3 else
                                  pe.wait_ge(ff_l3, i + 1)) if q == 4 and m == 0 else None,
                                 tail=1 if q == 4 and m == 0 else 0,
                                 vals=i * 12 + (U0 + 4 + (q - 4) * 2 + m))
                u = N_WIN + N_OUT + 12 * FF_STEPS
                j = N_WIN + N_OUT + N_FF
                for half in range(2):
                    pe.wait_ge(lo_made, j + 1)
                    for m in range(4):
                        unit(j % 2, 2 * m, 2, ple_hi, ple_lo, u,
                             (lambda k: pe.wait_ge(pl, k + 1)) if half == 0 and m == 0 else None)
                        u += 1
                    j += 1
                    for m in range(4):
                        pe.wait_ge(lo_made, j + 1)
                        unit(j % 2, 0, KT, n_hi, n_lo, u,
                             (lambda k: pe.wait_ge(pl, 2 + k + 1)) if half == 0 and m == 0 else None)
                        u += 1
                        j += 1
                layer_end(pe)


        @block.scalar
        def _(act):
            link = linker(act, ch_a)

            def split_hi(j, done=None):
                act.wait_ge(w_ld[j % 2], 16 * (j // 2 + 1))
                if done:
                    act.wait_ge(mm[2], done)
                act.activation(w_hi[:, j % 2, :], w_raw[:, j % 2, :], ACT.Copy).then_inc(hi_made, 1)

            def take(dst, func, n, rows=slice(0, P), out_rows=None, **kw):
                for t in range(3):
                    act.wait_ge(mm[t], n)
                    o = dst[out_rows or rows, t * TT:(t + 1) * TT]
                    act.activation(o, pj[rows, t, 0:TT], func, **kw).then_inc(ev[t], 1)

            def norm(i):
                for k in range(KT):
                    if k >= 2:
                        act.wait_ge(nrm_mm, KT * i + k - 1)
                    act.activation(ext[:, k % 2, :], res[:, k, :], ACT.Square).then_inc(nrm_sq, 1)
                act.wait_ge(nrm_mm, KT * (i + 1))
                act.activation(ext[:, 2, :].rearrange(three, a=3), pm3, ACT.Sqrt, bias=EPS,
                               scale=1.0 / D).then_inc(nrm_rs, 1)
                for k in range(KT):
                    act.wait_ge(nrm_n, KT * i + k + 1)
                    act.activation(n_hi[:, k, :], ext[:, 3 + k % 2, :], ACT.Copy).then_inc(nrm_hi, 1)

            kind = dict(cq0=ACT.Silu, cq1=ACT.Silu, cg0=ACT.Silu, cg1=ACT.Silu, cf0=ACT.Sigmoid, cf1=ACT.Sigmoid,
                        do0=ACT.Sigmoid, do1=ACT.Sigmoid)

            def job(j):
                name = WIN[j]
                split_hi(j + 1, j if j >= 1 else None)
                if name == 'gates':
                    for t in range(3):
                        act.wait_ge(mm[t], 1)
                        act.activation(slot(8)[0:4, t * TT:(t + 1) * TT], pj[0:4, t, 0:TT], ACT.Copy)
                        act.activation(slot(9)[0:4, t * TT:(t + 1) * TT], pj[32:36, t, 0:TT],
                                       ACT.Copy).then_inc(ev[t], 1)
                    return
                if name in ('ci0', 'ci1'):
                    act.wait_ge(rope_v, 6)
                if name in ('dv0', 'dv1', 'dq0', 'dq1'):
                    act.wait_ge(lru_v, 2)
                    act.wait_ge(rope_v, 6)
                if name in ('cq0', 'cf0'):
                    act.wait_ge(sa_v, 4)
                    act.wait_ge(sa_t, 4)
                if name == 'cg0':
                    act.wait_ge(smp_st, 32)
                if name == 'dk0':
                    act.wait_ge(kv_st, 32)
                    act.wait_ge(sa_v, 4)
                if name == 'do0':
                    act.wait_ge(vt_c, 6)
                kw = dict(scale=0.125) if name in ('dk0', 'dk1') else {}
                take(slot(SLOT[name]), kind.get(name, ACT.Copy), j + 1, **kw)
                if name in ('ci0', 'ci1', 'dv0', 'dv1'):
                    act.wait_ge(ev[2], j + 1)
                    i = ('ci0', 'ci1', 'dv0', 'dv1').index(name)
                    act.activation(v_smp[:, i, :], slot(SLOT[name])[:, S0:T], ACT.Copy).then_inc(hp_a, 1)

            def rows(i):
                z = slot(9)[0:4, :]
                if i == 0:
                    act.wait_ge(rows_v, 1)
                    link(act.activation(slot(2)[0:4, :], z, ACT.Abs))
                    act.activation(slot(2)[0:4, :], slot(2)[0:4, :], ACT.Exp, scale=-1.0).then_inc(rows_a, 1)
                elif i == 1:
                    act.wait_ge(rows_v, 2)
                    act.activation(slot(5)[0:4, :], slot(3)[0:4, :], ACT.Ln).then_inc(rows_a, 1)
                elif i == 2:
                    act.wait_ge(rows_v, 5)
                    act.activation(slot(6)[32:36, 0:SEQ], slot(2)[0:4, 0:SEQ], ACT.Exp).then_inc(rows_a, 1)
                    act.activation(slot(9)[0:4, :], slot(9)[0:4, :], ACT.Exp).then_inc(rows_a, 1)
                    act.activation(slot(8)[32:36, :], slot(5)[0:4, :], ACT.Exp, scale=-1.0).then_inc(rows_a, 1)
                    act.activation(slot(8)[0:4, S0:T], slot(8)[0:4, S0:T], ACT.Exp).then_inc(rows_a, 1)
                    link(act.activation(tiny[:, 0:2], pc('lam', 0, 2), ACT.Abs))
                    act.activation(tiny[:, 2:4], tiny[:, 0:2], ACT.Exp, scale=-1.0).then_inc(rows_a, 1)
                    act.wait_ge(rows_v, 10)
                    act.activation(tiny[:, 6:8], tiny[:, 4:6], ACT.Ln).then_inc(rows_a, 1)
                    act.wait_ge(rows_v, 11)
                    act.activation(tiny[:, 16:20], tiny[:, 12:16], ACT.Exp).then_inc(rows_a, 1)
                else:
                    act.wait_ge(rows_t, 1)
                    act.activation(bw[:, :, 0, :], pm[:, 3, 0:64].rearrange("p (c e) -> p c e", c=NC)[:, :, 0:4],
                                   ACT.Copy).then_inc(rows_c, 1)
                    act.activation(bw[:, :, 1, :], pm[:, 4, 0:64].rearrange("p (c e) -> p c e", c=NC)[:, :, 0:4],
                                   ACT.Copy).then_inc(rows_c, 1)

            def gate(_):
                for n in range(4):
                    act.wait_ge(mix_mm, n + 1)
                    b = pc('br' if n < 2 else 'bi', n % 2)
                    act.activation(slot(2 + n).rearrange(three, a=3), pm3, ACT.Sigmoid, bias=b).then_inc(mix_ev, 1)
                act.wait_ge(mix_ev, 4)
                act.wait_ge(rows_v, 12)
                for j in range(2):
                    act.activation(slot(2 + j), slot(2 + j), ACT.Tanh, scale=tiny[:, 10 + j:11 + j]).then_inc(lru_a, 1)
                act.wait_ge(lru_a, 2)
                for j in range(2):
                    act.activation(slot(6 + j), slot(2 + j), ACT.Sqrt).then_inc(lru_a, 1)
                act.wait_ge(ev[2], 5)
                for j in range(2):
                    act.activation(slot(12 + j), slot(12 + j), ACT.Gelu_apprx_tanh).then_inc(lru_a, 1)

            def rope(_):
                act.wait_ge(lru_v, 2)
                act.wait_ge(ev[2], JOB['k'] + 1)
                for n in range(3):
                    act.activation(slot(n), slot(14 + n), ACT.Square).then_inc(rope_a, 1)
                for n in range(3):
                    act.wait_ge(mix_mm, 5 + n)
                    act.activation(slot(3 + n).rearrange(three, a=3), pm3, ACT.Sqrt, bias=EPS,
                                   scale=1.0 / 64).then_inc(mix_ev, 1)

            def vtrans(v):
                col = VT_COL[list(VT_COL)[v]]
                for h in range(2):
                    act.wait_ge(vt_t, 2 * v + h + 1)
                    act.activation(vt[:, 4 * h:4 * h + 4, col:col + P],
                                   pm[:, 4, :].rearrange("p (c d) -> p c d", c=4), ACT.Copy).then_inc(vt_c, 1)

            def attn(step):
                c = step
                if c == 0:
                    act.wait_ge(rope_v, 6)
                    act.dma_start(kv_out[l][:, 0, :], slot(16)[:, SEQ - CH:SEQ]).then_inc(kv_st, 16)
                    act.wait_ge(ev[2], JOB['bv'] + 1)
                    act.dma_start(kv_out[l][:, 1, :], slot(17)[:, SEQ - CH:SEQ]).then_inc(kv_st, 16)
                    act.wait_ge(lru_v, 2)
                    kc = flat(6)[:, 0:1024].rearrange("p (b s) -> p b s", b=DEC)
                    vc = flat(7)[:, 0:1024].rearrange("p (b d) -> p b d", b=DEC)
                    act.dma_start(kc[:, :, 1:P], kc_in[l]).then_inc(smp_ld, 16)
                    act.dma_start(vc[1:P, :, :], vc_in[l]).then_inc(smp_ld, 16)
                if c < NC:
                    sc = flat(c % 2)[:, 0:1024].rearrange("p (i s) -> p i s", i=4)
                    lo_k, b = (0 if c else CH), 12 * (c % 2)
                    act.wait_ge(at_m, c + 1)
                    for i in range(4):
                        act.activation(sc[:, i, lo_k:], sc[:, i, lo_k:], ACT.Exp, bias=tiny[:, b + i:b + i + 1],
                                       accum_out=tiny[:, b + 4 + i:b + 5 + i])
                    act.activation(tiny[:, b + 8:b + 12], tiny[:, b + 8:b + 12], ACT.Exp).then_inc(at_e, 1)
                c = step - 2
                if c >= 0:
                    act.wait_ge(at_w, c + 1)
                    act.activation(slot(14, 2)[:, :, c * CH:(c + 1) * CH],
                                   pm[:, 4, 0:256].rearrange("p (j t) -> p j t", j=2), ACT.Copy).then_inc(at_o, 1)
                c = step - 1
                if 0 <= c < NC:
                    act.wait_ge(at_t, c + 1)
                    pt = flat(2 + c % 2)[:, 0:1024]
                    if c:
                        act.activation(pt.rearrange("p (a s) -> p a s", a=2), pm[:, 2:4, :],
                                       ACT.Copy).then_inc(at_c, 1)
                    else:
                        act.activation(pt.rearrange("p (i h t) -> p i h t", i=4, h=2)[:, :, 1, :],
                                       pm[:, 2:4, :].rearrange("p a (i h t) -> p (a i) h t", i=2, h=2)[:, :, 1, :],
                                       ACT.Copy).then_inc(at_c, 1)

            def sattn(part):
                vc = flat(7)[:, 0:1024].rearrange("p (b d) -> p b d", b=DEC)
                if part == 0:
                    act.wait_ge(sa_t, 1)
                    act.activation(vc[0:1, :, :].rearrange("p (a b) d -> p a (b d)", a=2), pm[0:1, 0:2, :],
                                   ACT.Copy).then_inc(sa_a, 1)
                    act.wait_ge(sa_x, 1)
                    act.activation(flat(2)[0:4, 0:1024], flat(2)[0:4, 0:1024], ACT.Exp).then_inc(sa_a, 1)
                    act.activation(tiny[0:4, 8:16], tiny[0:4, 8:16], ACT.Exp).then_inc(sa_a, 1)
                elif part == 2:
                    act.wait_ge(sa_t, 2)
                    act.wait_ge(sa_a, 1)
                    act.dma_start(kc_out[l], flat(6)[:, 0:1024].rearrange("p (b s) -> p b s", b=DEC)).then_inc(smp_st, 16)
                    act.dma_start(vc_out[l], vc).then_inc(smp_st, 16)

            def hprep(_):
                act.wait_ge(hp_v, 1)
                for j in range(2):
                    act.activation(slot(2 + j), slot(2 + j), ACT.Ln).then_inc(hp_a, 1)

            def hexp(c):
                for g in range(3):
                    act.wait_ge(hc_sub, 3 * c + g + 1)
                    act.wait_ge(hc_subk, 3 * c + g + 1)
                    if g == 0:
                        last = act.activation(early[:, 0:4, :], early[:, 0:4, :], ACT.Exp)
                    elif g == 1:
                        act.activation(early[:, 4:8, :], early[:, 4:8, :], ACT.Exp)
                        act.activation(level(4), level(4), ACT.Exp)
                        last = act.activation(level(5), level(5), ACT.Exp)
                    else:
                        act.activation(level(6), level(6), ACT.Exp)
                        last = act.activation(ex2[:], ex2[:], ACT.Exp)
                    last.then_inc(hc_exp, 1)

            def hchunk(c):
                if c == 0:
                    hexp(0)
                act.wait_ge(hc_tt, c + 1)
                act.activation(ktok[:], pm[:, 4, 0:256].rearrange("p (j t) -> p j t", j=2), ACT.Copy).then_inc(hc_tc, 1)
                act.wait_ge(hc_ot, 2 * c + 1)
                act.activation(slot(0, 2)[:, :, c * CH:(c + 1) * CH],
                               pm[:, 2, 0:256].rearrange("p (j t) -> p j t", j=2), ACT.Copy).then_inc(hc_oc, 1)
                if c + 1 < NC:
                    hexp(c + 1)

            def hsample(_):
                act.wait_ge(hc_sv, NC)
                act.dma_start(sm_state(0, 0), hs_in[l][:, 0:512]).then_inc(st_ld, 16)
                act.dma_start(sm_state(0, 1), hs_in[l][:, 512:1024]).then_inc(st_ld, 16)
                act.activation(tiny[:, 0:16].rearrange("p (j b) -> p j b", j=2), slot(2, 2)[:, :, S0:T],
                               ACT.Exp).then_inc(ss_a, 1)
                act.dma_start(hp_out[l], h_st[:]).then_inc(mix_st, 16)
                act.wait_ge(ss_v, 5)
                act.dma_start(hs_out[l][:, 0:512], sm_state(0, 0)).then_inc(mix_st, 16)
                act.dma_start(hs_out[l][:, 512:1024], sm_state(0, 1)).then_inc(mix_st, 16)

            def y_split(ks):
                for k in ks:
                    act.activation(n_hi[:, k, :], slot(Y_SLOT[k]), ACT.Copy).then_inc(y_hi, 1)

            def gnorm(g, n0, o):
                act.wait_ge(ss_v, 5 if g == 0 else 11)
                act.wait_ge(hc_oc, NC)
                for j in range(2):
                    act.activation(slot(2 + j), slot(o + j), ACT.Square).then_inc(nm_a, 1)
                for j in range(2):
                    act.wait_ge(mix_mm, n0 + j)
                    act.activation(slot(4 + j).rearrange(three, a=3), pm3, ACT.Sqrt, bias=EPS,
                                   scale=1.0 / 64).then_inc(mix_ev, 1)

            def mprep(_):
                act.wait_ge(nm_v, 1)
                act.dma_start(flat(6)[:, 0:1024], cs_in[l]).then_inc(st_ld, 16)
                act.wait_ge(mm[2], N_WIN)
                y_split(range(6))
                for n in range(4):
                    act.wait_ge(mix_mm, 13 + n)
                    act.activation(slot(2 + n).rearrange(three, a=3), pm3, ACT.Copy).then_inc(mix_ev, 1)
                act.wait_ge(mix_mm, 17)
                act.activation(tiny[:, 0:16], pm[:, 3, 0:16], ACT.Copy).then_inc(mix_ev, 1)

            def mchunk(step):
                w = ex2[:].rearrange("p a j t -> p (a j) t")
                c = step
                if c < NC:
                    act.wait_ge(mc_t, 2 * c + 1)
                    if c == 0:
                        act.wait_ge(mc_c, 1)
                    else:
                        act.wait_ge(mc_s, c)
                    for i in range(4):
                        head = 2 * (i % 2) + i // 2
                        last = act.activation(w[:, i, :], pj[:, 0, i * CH:(i + 1) * CH], ACT.Exp,
                                              bias=bw[:, c, 0, head:head + 1])
                    last.then_inc(mc_w, 1)
                c = step - 1
                if c >= 0:
                    act.wait_ge(mc_nt, 2 * c + 1)
                    if c:
                        act.wait_ge(mc_h, c)
                    act.activation(early[:, 0:2, :], pm[:, c % 2, 256:512].rearrange("p (j t) -> p j t", j=2),
                                   ACT.Abs).then_inc(mc_d, 1)

            def msample(_):
                act.wait_ge(mc_sv, NC)
                act.dma_start(cp_out[l], c_st[:]).then_inc(mix_st, 16)
                act.wait_ge(ss_t, 9)
                act.activation(tiny[:, 32:48], pm[:, 4, 384:400], ACT.Abs).then_inc(ss_a, 1)
                act.dma_start(cs_out[l], flat(6)[:, 0:1024]).then_inc(mix_st, 16)

            steps = dict(job=job, rows=rows, conv=lambda _: None, gate=gate, lru=lambda _: None, rope=rope,
                         vt=vtrans, attn=attn, sattn=sattn, hprep=hprep, hchunk=hchunk, hsample=hsample,
                         hnorm=lambda _: gnorm(0, 11, 0), mprep=mprep, mchunk=mchunk, msample=msample,
                         mnorm=lambda _: gnorm(1, 18, 10))
            with act.Fori(0, LAYERS) as l:
                act.wait_ge(par_ld, 16)
                split_hi(0)
                norm(0)
                act.wait_ge(h_out, 16)
                for what, i in ORDER:
                    steps[what](i)
                act.wait_ge(y_lo, 6)
                act.dma_start(res[:, 0:2, :], h_saved[:, 0:2, :]).then_inc(h_ld[0], 16)
                act.wait_ge(nm_v, 2)
                y_split(range(6, KT))
                act.wait_ge(mix_st, 80)
                act.dma_start(res[:, 2:KT, :], h_saved[:, 2:KT, :]).then_inc(h_ld[1], 16)
                act.dma_start(so_out[l], so[:]).then_inc(so_st, 16)
                for j in range(N_WIN, N_WIN + N_OUT):
                    split_hi(j + 1, j)
                act.wait_ge(ev[2], N_WIN + N_OUT)
                norm(1)
                with act.Fori(0, FF_STEPS) as i:
                    for q in range(8):
                        j = N_WIN + N_OUT + q + 1
                        done = N_WIN + N_OUT + (q if q < 5 else 4 + (q - 4) * 2)
                        n_ld = (i * 4 + (j // 2 + 1)) * 16
                        act.wait_ge(w_ld[j % 2], n_ld)
                        act.wait_ge(mm[2], i * 12 + done)
                        act.activation(w_hi[:, j % 2, :], w_raw[:, j % 2, :], ACT.Copy).then_inc(hi_made, 1)
                        if q < 4:
                            for t in range(3):
                                act.wait_ge(mm[t], i * 12 + (N_WIN + N_OUT + q + 1))
                                act.activation(relu[:, q % 2, t * TT:(t + 1) * TT], pj[:, t, 0:TT],
                                               ACT.Relu).then_inc(ev[t], 1)
                            act.wait_ge(ff_q, i * 4 + (q + 1))
                            act.activation(hid_hi[:, q, :], hsq[:, q % 2, :], ACT.Copy).then_inc(ff_h, 1)
                act.wait_ge(mm[2], N_WIN + N_OUT + 12 * FF_STEPS)
                act.wait_ge(ff_l, 3 * FF_STEPS)
                act.wait_ge(ff_l3, FF_STEPS)
                act.dma_start(ple_raw[:], p_in[l]).then_inc(ple_ld, 16)
                act.wait_ge(ple_ld, 16)
                for k in range(2):
                    act.activation(ple_hi[:, k, :], ple_raw[:, k, :], ACT.Copy).then_inc(ph, 1)
                act.wait_ge(ev[2], N_WIN + N_OUT + 12 * FF_STEPS)
                for k in range(KT):
                    act.activation(n_hi[:, k, :], res[:, k, :], ACT.Copy).then_inc(ph, 1)
                u = N_WIN + N_OUT + 12 * FF_STEPS
                j = N_WIN + N_OUT + N_FF
                for half in range(2):
                    split_hi(j + 1, u)
                    for m in range(4):
                        if half:
                            act.wait_ge(pv, 4 * half)
                        u += 1
                        take(ple_proj[:, m, :], ACT.Copy, u)
                    j += 1
                    for m in range(4):
                        if j + 1 < N_JOBS:
                            split_hi(j + 1, u)
                        u += 1
                        if 4 * half + m:
                            act.wait_ge(pv, 4 * half + m)
                        take(ple_sig, ACT.Sigmoid, u)
                        j += 1
                act.wait_ge(pv, KT)
                act.wait_ge(so_st, 16)
                layer_end(act)

        @block.gpsimd
        def _(pool):
            def split_lo(j, done=None):
                pool.wait_ge(hi_made, j + 1)
                if done:
                    pool.wait_ge(mm[2], done)
                pool.tensor_tensor(w_lo[:, j % 2, :], w_raw[:, j % 2, :], w_hi[:, j % 2, :].bitcast(F32),
                                   ALU.subtract).then_inc(lo_made, 1)

            def norm(i):
                for k in range(KT):
                    pool.wait_ge(nrm_hi, KT * i + k + 1)
                    pool.tensor_tensor(n_lo[:, k, :], ext[:, 3 + k % 2, :], n_hi[:, k, :].bitcast(F32),
                                       ALU.subtract).then_inc(nrm_lo, 1)

            def hsub(c):
                cc = slice(c * CH, (c + 1) * CH)
                b = slot(2, 2)[:, :, cc]
                if c == 0:
                    pool.wait_ge(hp_v, 2)
                    pool.wait_ge(sa_t, 4)
                for g, levels in enumerate(GROUPS):
                    if c:
                        pool.wait_ge(hc_lt, 3 * (c - 1) + g + 1)
                    for lev in levels:
                        b0, e0 = halves(b, lev)[0], halves(level(lev), lev)[0]
                        n, half = CH >> (lev + 1), 1 << lev
                        ref = b0[:, :, :, half - 1:half].to_broadcast([P, 2, n, half])
                        last = pool.tensor_tensor(e0, ref, b0, ALU.subtract)
                    if g == 2:
                        if c:
                            pool.wait_ge(hc_tt, c)
                        last = pool.tensor_tensor(ex2[:, 1], b[:, :, CH - 1:CH].to_broadcast([P, 2, CH]), b, ALU.subtract)
                    last.then_inc(hc_subk, 1)

            def hmul(c):
                k = slot(4, 2)[:, :, c * CH:(c + 1) * CH]
                for g, levels in enumerate(GROUPS):
                    pool.wait_ge(hc_exp, 3 * c + g + 1)
                    for lev in levels:
                        e0 = halves(level(lev), lev)[0]
                        last = pool.tensor_tensor(e0, e0, halves(k, lev)[0], ALU.mult)
                    if g == 2:
                        last = pool.tensor_tensor(ex2[:, 1], ex2[:, 1], k, ALU.mult)
                    last.then_inc(hc_kk, 1)

            with pool.Fori(0, LAYERS) as l:
                split_lo(0)
                norm(0)
                for what, c in ORDER:
                    if what == 'job':
                        split_lo(c + 1, c if c >= 1 else None)
                    if what == 'hprep':
                        hsub(0)
                    if what == 'hchunk':
                        hmul(c)
                        if c + 1 < NC:
                            hsub(c + 1)
                for k, s in enumerate(Y_SLOT):
                    pool.wait_ge(y_hi, k + 1)
                    pool.tensor_tensor(n_lo[:, k, :], slot(s), n_hi[:, k, :].bitcast(F32),
                                       ALU.subtract).then_inc(y_lo, 1)
                for j in range(N_WIN + 1, N_WIN + N_OUT + 1):
                    split_lo(j, j - 1)
                norm(1)
                with pool.Fori(0, FF_STEPS) as i:
                    for q in range(8):
                        j = N_WIN + N_OUT + q + 1
                        done = N_WIN + N_OUT + (q if q < 5 else 4 + (q - 4) * 2)
                        pool.wait_ge(hi_made, i * 8 + (j + 1))
                        pool.wait_ge(mm[2], i * 12 + done)
                        pool.tensor_tensor(w_lo[:, j % 2, :], w_raw[:, j % 2, :], w_hi[:, j % 2, :].bitcast(F32),
                                           ALU.subtract).then_inc(lo_made, 1)
                        if q < 3:
                            pool.wait_ge(ff_h, i * 4 + (q + 1))
                            pool.tensor_tensor(hid_lo[:, q, :], hsq[:, q % 2, :], hid_hi[:, q, :].bitcast(F32),
                                               ALU.subtract).then_inc(ff_l, 1)
                for k in range(2):
                    pool.wait_ge(ph, k + 1)
                    pool.tensor_tensor(ple_lo[:, k, :], ple_raw[:, k, :], ple_hi[:, k, :].bitcast(F32),
                                       ALU.subtract).then_inc(pl, 1)
                for k in range(KT):
                    pool.wait_ge(ph, 2 + k + 1)
                    pool.tensor_tensor(n_lo[:, k, :], res[:, k, :], n_hi[:, k, :].bitcast(F32),
                                       ALU.subtract).then_inc(pl, 1)
                u = N_WIN + N_OUT + 12 * FF_STEPS
                j = N_WIN + N_OUT + N_FF
                for half in range(2):
                    split_lo(j + 1, u)
                    u += 4
                    j += 1
                    for m in range(4):
                        if j + 1 < N_JOBS:
                            split_lo(j + 1, u)
                        u += 1
                        j += 1
                layer_end(pool)

        @block.vector
        def _(dve):
            link = linker(dve, ch_v)

            def tt(o, a, b, op):
                return dve.tensor_tensor(o, a, b, op)

            def norm(i):
                dve.wait_ge(nrm_rs, i + 1)
                rs = ext[:, 2, :]
                link(dve.reciprocal(rs, rs))
                for k in range(KT):
                    if k >= 2:
                        dve.wait_ge(nrm_lo, KT * i + k - 1)
                    dve.scalar_tensor_tensor(ext[:, 3 + k % 2, :], res[:, k, :], pc('g1' if i == 0 else 'g2', k), rs,
                                             ALU.mult, ALU.mult).then_inc(nrm_n, 1)

            def rows(i):
                if i:
                    return
                z, ig = slot(9)[0:4, :], slot(8)[0:4, :]
                t1, t2, ln, f = slot(2)[0:4, :], slot(3)[0:4, :], slot(5)[0:4, :], slot(4)[0:4, :]
                for t in range(3):
                    dve.wait_ge(ev[t], 1)
                dve.wait_ge(h_out, 16)
                link(dve.memset(so[:], 0.0))
                link(dve.tensor_scalar(ig, ig, pc('ib')[0:4], None, ALU.add))
                dve.tensor_scalar(z, z, pc('fb')[0:4], None, ALU.add).then_inc(rows_v, 1)
                dve.wait_ge(rows_a, 1)
                dve.tensor_scalar(t2, t1, 1.0, None, ALU.add).then_inc(rows_v, 1)
                dve.wait_ge(rows_a, 2)
                link(dve.tensor_scalar(t2, t2, -1.0, 1e-30, ALU.add, ALU.max))
                link(dve.reciprocal(t2, t2))
                link(tt(t2, t2, t1, ALU.mult))
                link(tt(ln, ln, t2, ALU.mult))
                link(dve.scalar_tensor_tensor(z, z, 0.0, ln, ALU.min, ALU.subtract))
                one = flat(7)[0:4, 0:CH]
                link(dve.memset(flat(7)[0:P, 0:CH], 1.0))
                for c in range(NC):
                    last = dve.tensor_tensor_scan(f[:, c * CH:(c + 1) * CH], one, z[:, c * CH:(c + 1) * CH], 0.0,
                                                  ALU.mult, ALU.add)
                link(last)
                m = ln
                link(dve.tensor_tensor_scan(m[:, 0:SEQ], z[:, 0:SEQ], ig[:, 0:SEQ], 0.0, ALU.add, ALU.max))
                link(tt(f[:, SEQ:T], z[:, SEQ:T], pc('m0', 0, 8)[0:4], ALU.add))
                link(tt(m[:, SEQ:T], f[:, SEQ:T], ig[:, SEQ:T], ALU.max))
                link(dve.tensor_copy(oc('mp')[0:4], m[:, SEQ - 1:SEQ]))
                link(dve.tensor_copy(oc('ms', 0, 8)[0:4], m[:, SEQ:T]))
                beta = slot(6)[0:4, :]
                link(tt(beta[:, 0:SEQ], ig[:, 0:SEQ], f[:, 0:SEQ], ALU.subtract))
                link(tt(ig[:, SEQ:T], ig[:, SEQ:T], m[:, SEQ:T], ALU.subtract))
                link(tt(ig[:, 0:SEQ], f[:, 0:SEQ], m[:, 0:SEQ], ALU.subtract))
                link(tt(z[:, SEQ:T], f[:, SEQ:T], m[:, SEQ:T], ALU.subtract))
                a3 = ig[:, 0:SEQ].rearrange("p (c t) -> p c t", c=NC)
                m3 = m[:, 0:SEQ].rearrange("p (c t) -> p c t", c=NC)
                z3 = z[:, 0:SEQ].rearrange("p (c t) -> p c t", c=NC)
                link(dve.tensor_copy(z3[:, 0, :], a3[:, 0, :]))
                link(tt(z3[:, 1:, :], a3[:, 1:, :], m3[:, 0:NC - 1, CH - 1:CH].to_broadcast([4, NC - 1, CH]), ALU.add))
                link(tt(t1[:, 0:SEQ].rearrange("p (c t) -> p c t", c=NC),
                        beta[:, 0:SEQ].rearrange("p (c t) -> p c t", c=NC),
                        a3[:, :, CH - 1:CH].to_broadcast([4, NC, CH]), ALU.add))
                for n in range(3):
                    dve.sem_inc(rows_v, 1)
                dve.wait_ge(rows_a, 6)
                for n in range(4):
                    dve.sem_inc(rows_v, 1)
                link(dve.tensor_reduce(tiny[:, 20:22], pc('gam', 0, 4).rearrange("p (l j) -> p j l", l=2), AX_X, ALU.max))
                link(tt(tiny[:, 12:16].rearrange("p (l j) -> p l j", l=2), pc('gam', 0, 4).rearrange("p (l j) -> p l j", l=2),
                        tiny[:, 20:22].unsqueeze(1).to_broadcast([P, 2, 2]), ALU.subtract))
                dve.wait_ge(rows_a, 7)
                dve.tensor_scalar(tiny[:, 4:6], tiny[:, 2:4], 1.0, None, ALU.add).then_inc(rows_v, 1)
                dve.wait_ge(rows_a, 8)
                dve.tensor_scalar(tiny[:, 4:6], tiny[:, 4:6], -1.0, 1e-30, ALU.add, ALU.max).then_inc(rows_v, 1)
                dve.wait_ge(rows_v, 11)
                link(dve.reciprocal(tiny[:, 4:6], tiny[:, 4:6]))
                link(tt(tiny[:, 4:6], tiny[:, 4:6], tiny[:, 2:4], ALU.mult))
                link(tt(tiny[:, 6:8], tiny[:, 6:8], tiny[:, 4:6], ALU.mult))
                link(dve.tensor_scalar(tiny[:, 8:10], pc('lam', 0, 2), -1.0, 0.0, ALU.mult, ALU.max))
                link(tt(tiny[:, 8:10], tiny[:, 8:10], tiny[:, 6:8], ALU.add))
                dve.tensor_scalar(tiny[:, 10:12], tiny[:, 8:10], 4.0, None, ALU.mult).then_inc(rows_v, 1)
                dve.wait_ge(rows_a, 9)
                link(tt(tiny[:, 20:22], tiny[:, 16:18], tiny[:, 18:20], ALU.add))
                link(dve.reciprocal(tiny[:, 20:22], tiny[:, 20:22]))
                link(tt(tiny[:, 20:22], tiny[:, 20:22], tiny[:, 18:20], ALU.mult))
                link(dve.tensor_scalar(tiny[:, 36:38], tiny[:, 20:22], pc('lm'), None, ALU.mult))
                link(dve.tensor_scalar(tiny[:, 38:40], tiny[:, 36:38], -1.0, 1.0, ALU.mult, ALU.add))
                link(dve.memset(tiny[:, 24:36], 0.0))

            def conv(_):
                for t in range(3):
                    dve.wait_ge(ev[t], 3)
                cv = pc('conv', 0, 48).rearrange("p (j w b) -> p j w b", j=2, w=3)
                for j in range(2):
                    x, o = slot(10 + j), slot(j)
                    link(dve.tensor_scalar(o, x, pc('cw', 3 * 2 + j), pc('cb', j), ALU.mult, ALU.add))
                    for w in range(3):
                        s = 3 - w
                        wc = pc('cw', w * 2 + j)
                        link(dve.scalar_tensor_tensor(o[:, s:SEQ], x[:, 0:SEQ - s], wc, o[:, s:SEQ], ALU.mult, ALU.add))
                        link(dve.scalar_tensor_tensor(o[:, S0:T], cv[:, j, w, :], wc, o[:, S0:T], ALU.mult, ALU.add))
                    link(dve.tensor_copy(oc('convp', 3 * j, 3), x[:, SEQ - 3:SEQ]))
                    cs = oc('convs', 24 * j, 24).rearrange("p (w b) -> p w b", w=3)
                    link(dve.tensor_copy(cs[:, 0:2, :], cv[:, j, 1:3, :]))
                    link(dve.tensor_copy(cs[:, 2, :], x[:, S0:T]))
                dve.sem_inc(conv_v, 1)

            def lru(_):
                dve.wait_ge(lru_a, 4)
                for j in range(2):
                    xc, u, i, su, rc = slot(j), slot(2 + j), slot(4 + j), slot(6 + j), slot(10 + j)
                    link(dve.tensor_scalar(rc, u, 1.0, None, ALU.add))
                    link(dve.reciprocal(rc, rc))
                    link(tt(i, i, xc, ALU.mult))
                    link(tt(su, su, rc, ALU.mult))
                    link(dve.scalar_tensor_tensor(i, su, 2.0, i, ALU.mult, ALU.mult))
                    link(dve.tensor_scalar(u, u, -1.0, 1.0, ALU.mult, ALU.add))
                    link(tt(u, u, rc, ALU.mult))
                    link(dve.tensor_tensor_scan(xc[:, 0:SEQ], u[:, 0:SEQ], i[:, 0:SEQ], 0.0, ALU.mult, ALU.add))
                    link(tt(xc[:, S0:T], u[:, S0:T], pc('h0', 8 * j, 8), ALU.mult))
                    link(tt(xc[:, S0:T], xc[:, S0:T], i[:, S0:T], ALU.add))
                    link(dve.tensor_copy(oc('hp', j), xc[:, SEQ - 1:SEQ]))
                    link(dve.tensor_copy(oc('hs', 8 * j, 8), xc[:, S0:T]))
                    dve.wait_ge(lru_a, 5 + j)
                    tt(slot(12 + j), slot(12 + j), xc, ALU.mult).then_inc(lru_v, 1)
                dve.wait_ge(lru_v, 2)

            def rope(_):
                dve.wait_ge(rope_ld, 16)
                for n in range(3):
                    dve.wait_ge(mix_ev, 5 + n)
                    link(dve.reciprocal(slot(3 + n), slot(3 + n)))
                    dve.scalar_tensor_tensor(slot(14 + n), slot(14 + n), pc('kg' if n == 2 else 'qg'), slot(3 + n),
                                             ALU.mult, ALU.mult).then_inc(rope_v, 1)
                for n in range(3):
                    dve.wait_ge(mix_mm, 8 + n)
                    dve.wait_ge(rope_v, 3 + n)
                    tmp = slot(n)
                    tt(tmp.rearrange(three, a=3), pm3, slot(19).rearrange(three, a=3), ALU.mult).then_inc(mix_ev, 1)
                    link(tt(slot(14 + n), slot(14 + n), slot(18), ALU.mult))
                    dve.wait_ge(mix_ev, 8 + n)
                    tt(slot(14 + n), slot(14 + n), tmp, ALU.add).then_inc(rope_v, 1)
                dve.wait_ge(rope_v, 6)

            def attn(step):
                c = step - 1
                if 0 <= c < NC:
                    sc = flat(c % 2)[:, 0:1024].rearrange("p (i s) -> p i s", i=4)
                    lo_k, b = (0 if c else CH), 12 * (c % 2)
                    dve.wait_ge(at_e, c + 1)
                    link(tt(tiny[:, 28:32], tiny[:, b + 4:b + 8], tiny[:, b + 8:b + 12], ALU.add))
                    link(dve.reciprocal(tiny[:, 28:32], tiny[:, 28:32]))
                    tt(sc[:, :, lo_k:], sc[:, :, lo_k:], tiny[:, 28:32].unsqueeze(2).to_broadcast([P, 4, 256 - lo_k]),
                       ALU.mult).then_inc(at_p, 1)
                    dve.wait_ge(at_p, c + 1)
                c = step
                if c < NC:
                    sc = flat(c % 2)[:, 0:1024].rearrange("p (i s) -> p i s", i=4)
                    lo_k, b = (0 if c else CH), 12 * (c % 2)
                    dve.wait_ge(at_s, c + 1)
                    if c >= 2:
                        dve.wait_ge(at_t, c - 1)
                    mask = cst[:, C_MP + lo_k:C_MP + 256].unsqueeze(1).to_broadcast([P, 4, 256 - lo_k])
                    ps = pm[:, 0:2, :].rearrange("p a (j s) -> p (a j) s", j=2)[:, :, lo_k:]
                    link(dve.scalar_tensor_tensor(sc[:, :, lo_k:], ps, 0.125, mask, ALU.mult, ALU.add))
                    mx = tiny[:, 24:28]
                    link(dve.tensor_reduce(mx, sc[:, :, lo_k:], AX_X, ALU.max))
                    link(tt(mx, mx, pc('sink', 0, 4), ALU.max))
                    link(tt(tiny[:, b + 8:b + 12], pc('sink', 0, 4), mx, ALU.subtract))
                    dve.tensor_scalar(tiny[:, b:b + 4], mx, -1.0, None, ALU.mult).then_inc(at_m, 1)
                    dve.wait_ge(at_m, c + 1)

            def sattn(part):
                if part:
                    return
                dve.wait_ge(at_t, NC)
                dve.wait_ge(at_o, NC)
                dve.wait_ge(smp_ld, 32)
                qb = flat(0)[:, 0:32].rearrange("p (b i) -> p b i", b=DEC)
                link(dve.memset(flat(0)[:, 0:32], 0.0))
                for j in range(2):
                    link(dve.tensor_copy(qb[0:64, :, j], slot(14 + j)[0:64, S0:T]))
                    link(dve.tensor_copy(qb[64:P, :, 2 + j], slot(14 + j)[64:P, S0:T]))
                kc = flat(6)[:, 0:1024].rearrange("p (b s) -> p b s", b=DEC)
                dve.tensor_copy(kc[:, :, 0], slot(16)[:, S0:T]).then_inc(sa_v, 1)
                dve.wait_ge(sa_t, 2)
                s = flat(2)[0:4, 0:1024]
                s3 = s.rearrange("p (b s) -> p b s", b=DEC)
                link(dve.tensor_scalar(s.rearrange("p (a s) -> p a s", a=2), pm[0:4, 2:4, :], 0.125, None, ALU.mult))
                mx = tiny[0:4, 0:8]
                link(dve.tensor_reduce(mx, s3, AX_X, ALU.max))
                link(dve.tensor_scalar(mx, mx, pc('sinkc')[0:4], None, ALU.max))
                link(tt(s3, s3, mx.unsqueeze(2).to_broadcast([4, DEC, CH]), ALU.subtract))
                link(dve.tensor_scalar(tiny[0:4, 8:16], mx, -1.0, pc('sinkc')[0:4], ALU.mult, ALU.add))
                dve.sem_inc(sa_x, 1)
                dve.wait_ge(sa_a, 3)
                link(dve.tensor_reduce(mx, s3, AX_X, ALU.add))
                link(tt(mx, mx, tiny[0:4, 8:16], ALU.add))
                link(dve.reciprocal(mx, mx))
                tt(s3, s3, mx.unsqueeze(2).to_broadcast([4, DEC, CH]), ALU.mult).then_inc(sa_v, 1)
                dve.wait_ge(sa_t, 3)
                dve.tensor_copy(flat(3)[:, 0:32], pm[:, 4, 0:32]).then_inc(sa_v, 1)
                dve.wait_ge(sa_t, 4)
                o = pm[:, 4, 64:96].rearrange("p (b i) -> p b i", b=DEC)
                for j in range(2):
                    link(dve.tensor_copy(slot(14 + j)[0:64, S0:T], o[0:64, :, j]))
                    link(dve.tensor_copy(slot(14 + j)[64:P, S0:T], o[64:P, :, 2 + j]))
                dve.sem_inc(sa_v, 1)

            def hprep(_):
                for t in range(3):
                    dve.wait_ge(ev[t], JOB['cf1'] + 1)
                dve.wait_ge(vt_c, 10)
                dve.wait_ge(hp_a, 4)
                for j in range(2):
                    f = slot(2 + j)
                    link(dve.tensor_scalar(f, f, tiny[:, 38 + j:39 + j], tiny[:, 36 + j:37 + j], ALU.mult, ALU.add))
                    link(dve.tensor_scalar(slot(4 + j), f, -1.0, 1.0, ALU.mult, ALU.add))
                link(dve.memset(att[:, 0, :], 1.0))
                link(dve.memset(h_st[:], 0.0))
                dve.sem_inc(hp_v, 1)
                dve.wait_ge(hp_a, 6)
                for j in range(2):
                    f = slot(2 + j)
                    for c in range(NC):
                        cc = slice(c * CH, (c + 1) * CH)
                        last = dve.tensor_tensor_scan(f[:, cc], att[:, 0, :], f[:, cc], 0.0, ALU.mult, ALU.add)
                link(last)
                dve.sem_inc(hp_v, 1)
                hsub(0, 0)
                hsub(0, 1)
                hsub(0, 2)

            def hsub(c, g):
                b = slot(2, 2)[:, :, c * CH:(c + 1) * CH]
                for lev in GROUPS[g]:
                    b0, b1 = halves(b, lev)
                    n, half = CH >> (lev + 1), 1 << lev
                    ref = b0[:, :, :, half - 1:half].to_broadcast([P, 2, n, half])
                    last = tt(halves(level(lev), lev)[1], b1, ref, ALU.subtract)
                if g == 2:
                    last = dve.tensor_copy(ex2[:, 0], b)
                last.then_inc(hc_sub, 1)

            def hchunk(c):
                q = slot(0, 2)[:, :, c * CH:(c + 1) * CH]
                if c == 0:
                    for t in range(3):
                        dve.wait_ge(ev[t], JOB['cq1'] + 1)
                for g, levels in enumerate(GROUPS):
                    dve.wait_ge(hc_exp, 3 * c + g + 1)
                    for lev in levels:
                        e1 = halves(level(lev), lev)[1]
                        last = tt(e1, e1, halves(q, lev)[1], ALU.mult)
                    if g == 2:
                        dve.tensor_copy(tiny[:, 40 + 2 * (c % 2):42 + 2 * (c % 2)], ex2[:, 0, :, CH - 1])
                        if c:
                            dve.wait_ge(hc_ot, 2 * c - 1)
                        last = tt(qe[:], ex2[:, 0], q, ALU.mult)
                    last.then_inc(hc_kq, 1)
                dve.wait_ge(hc_kq, 3 * c + 3)
                dve.wait_ge(hc_lt, 3 * c + 1)
                if c:
                    dve.wait_ge(hc_ot, 2 * c - 1)
                pv4 = [pm[:, a:a + 2, :].rearrange("p a (j s) -> p (a j) s", j=2) for a in (0, 2)]
                tt(att[:], pv4[0][:, :, 0:128], ident.unsqueeze(1).to_broadcast([P, 4, CH]),
                   ALU.mult).then_inc(hc_lv, 1)
                for g, levels in enumerate(GROUPS):
                    dve.wait_ge(hc_lt, 3 * c + g + 1)
                    for lev in levels:
                        dve.wait_ge(hc_lv, 8 * c + 1 + lev)
                        half, n = 1 << lev, CH >> (lev + 1)
                        out = att[:].rearrange("p i (n two b) -> p i n two b", two=2, b=half)[:, :, :, 1, :]
                        mk = cst[:, C_LEV + 64 * lev:C_LEV + 64 * lev + 64].bitcast(U32).rearrange("p (n b) -> p n b", b=half)
                        dat = pv4[LEV_AT[lev][0] // 2][:, :, LEV_AT[lev][1]:LEV_AT[lev][1] + 64]
                        dve.copy_predicated(out, mk.unsqueeze(1).to_broadcast([P, 4, n, half]),
                                            dat.rearrange("p i (n b) -> p i n b", b=half)).then_inc(hc_lv, 1)
                    if c + 1 < NC:
                        hsub(c + 1, g)
                dve.wait_ge(hc_ot, 2 * c + 2)
                for j in range(2):
                    for hh in range(2):
                        r = slice(64 * hh, 64 * hh + 64)
                        last = dve.scalar_tensor_tensor(h_st[r, j, r], h_st[r, j, r],
                                                        tiny[r, 40 + 2 * (c % 2) + j:41 + 2 * (c % 2) + j],
                                                        pm[r, 3, j * P + 64 * hh:j * P + 64 * hh + 64], ALU.mult, ALU.add)
                link(last)
                dve.sem_inc(hc_sv, 1)

            def sample(g, dec, kk, q, v0, o):
                w0, w1 = ((x.rearrange("p (c b e) -> p c b e", b=2, e=64) if g else
                           x.rearrange("p c (b e) -> p c b e", e=64)) for x in (sm_half(g, 0), sm_half(g, 1)))
                wide = [P, DEC // 2, 2, 64]

                def each(x):
                    return x.rearrange("p (c b) -> p c b", b=2).unsqueeze(3).to_broadcast(wide)

                def full(x):
                    return x.rearrange("p (c b e) -> p c b e", b=2, e=64)

                eb = eye.unsqueeze(1).unsqueeze(1).to_broadcast(wide)
                for j in range(2):
                    st = full(sm_state(g, j))
                    tt(w0, each(v_smp[:, v0 + j, :]), eb, ALU.mult).then_inc(ss_v, 1)
                    dve.wait_ge(ss_t, 4 * g + 2 * j + 1)
                    link(tt(w1, full(pm[:, j, :]), each(kk[:, j, :]), ALU.mult))
                    link(tt(st, st, each(dec[:, j, :]), ALU.mult))
                    link(tt(st, st, w1, ALU.add))
                    tt(w1, st, each(q[:, j, :]), ALU.mult).then_inc(ss_v, 1)
                    dve.wait_ge(ss_t, 4 * g + 2 * j + 2)
                    link(tt(w1, full(pm[:, 2 + j, :]), eb, ALU.mult))
                    link(dve.tensor_reduce(o[:, j, :].rearrange("p (c b) -> p c b", b=2), w1, AX_X, ALU.add))

            def hsample(_):
                dve.wait_ge(hc_oc, NC)
                dve.wait_ge(ss_a, 1)
                dve.wait_ge(st_ld, 32)
                sample(0, tiny[:, 0:16].rearrange("p (j b) -> p j b", j=2), slot(4, 2)[:, :, S0:T],
                       slot(0, 2)[:, :, S0:T], 0, slot(0, 2)[:, :, S0:T])
                dve.sem_inc(ss_v, 1)

            def gnorm(g, n0, o, gain, gate0):
                for t in range(3):
                    dve.wait_ge(ev[t], (JOB['cg1'] if g == 0 else JOB['do1']) + 1)
                for j in range(2):
                    dve.wait_ge(mix_ev, n0 + j)
                    link(dve.reciprocal(slot(4 + j), slot(4 + j)))
                    link(dve.scalar_tensor_tensor(slot(o + j), slot(o + j), pc(gain), slot(4 + j), ALU.mult, ALU.mult))
                    link(tt(slot(o + j), slot(o + j), slot(gate0 + j), ALU.mult))
                dve.sem_inc(nm_v, 1)

            def mprep(_):
                pass

            def mchunk(step):
                inter, em = slot(2, 2), slot(4, 2)
                c = step
                if c < NC:
                    cc = slice(c * CH, (c + 1) * CH)
                    if c == 0:
                        dve.wait_ge(mix_st, 48)
                        link(dve.memset(c_st[:], 0.0))
                        link(dve.memset(n_st[:], 0.0))
                        dve.sem_inc(mc_c, 1)
                        dve.wait_ge(mix_ev, 17)
                    if c >= 2:
                        dve.wait_ge(mc_nt, 2 * (c - 1))
                    tt(mc_qe[c % 2], slot(10, 2)[:, :, cc], inter[:, :, cc], ALU.mult).then_inc(mc_q, 1)
                    dve.wait_ge(mc_t, 2 * c + 2)
                    dve.wait_ge(mc_w, c + 1)
                    tt(mc_att[c % 2].rearrange("p (a j) t -> p a (j t)", a=2), pj[:, 1:3, 0:256],
                       ex2[:].rearrange("p a j t -> p a (j t)"), ALU.mult).then_inc(mc_s, 1)
                    dve.wait_ge(mc_tt, c + 1)
                    tt(mc_kt[c % 2].rearrange("p j (h d) -> p j h d", h=2),
                       pm[:, 2, 0:256].rearrange("p (j h d) -> p j h d", j=2, h=2),
                       bw[:, c, 1, :].rearrange("p (j h) -> p j h", j=2).unsqueeze(3).to_broadcast([P, 2, 2, 64]),
                       ALU.mult).then_inc(mc_k, 1)
                c = step - 1
                if c < 0:
                    return
                cc = slice(c * CH, (c + 1) * CH)
                dve.wait_ge(mc_d, c + 1)
                den = early[:, 0:2, :]
                link(tt(den, den, em[:, :, cc], ALU.max))
                link(dve.reciprocal(den, den))
                tt(slot(10, 2)[:, :, cc], pm[:, c % 2, 0:256].rearrange("p (j t) -> p j t", j=2), den,
                   ALU.mult).then_inc(mc_h, 1)
                dve.wait_ge(mc_nt, 2 * c + 2)
                end = (c + 1) * CH - 1
                for j in range(2):
                    for hh in range(2):
                        r = slice(64 * hh, 64 * hh + 64)
                        dec = inter[r, j, end:end + 1]
                        dve.scalar_tensor_tensor(c_st[r, j, r], c_st[r, j, r], dec,
                                                 pm[r, 3, j * P + 64 * hh:j * P + 64 * hh + 64], ALU.mult, ALU.add)
                        last = dve.scalar_tensor_tensor(n_st[r, j, r], n_st[r, j, r], dec,
                                                        pm[r, 3, 256 + 2 * j:257 + 2 * j].to_broadcast([64, 64]),
                                                        ALU.mult, ALU.add)
                link(last)
                dve.sem_inc(mc_sv, 1)

            def msample(_):
                inter, em = slot(2, 2)[:, :, S0:T], slot(4, 2)[:, :, S0:T]
                w = tiny[:, 0:16].rearrange("p (j b) -> p j b", j=2)
                q, k = slot(10, 2)[:, :, S0:T], slot(16, 2)[:, :, S0:T]
                dve.wait_ge(mc_nt, 2 * NC)
                for j in range(2):
                    for hh in range(2):
                        link(dve.tensor_copy(oc('np', j)[64 * hh:64 * hh + 64], n_st[64 * hh:64 * hh + 64, j, 64 * hh:64 * hh + 1]))
                link(tt(w, w, k, ALU.mult))
                ns = oc('ns', 0, 16).rearrange("p (j b) -> p j b", j=2)
                link(tt(ns, pc('n0', 0, 16).rearrange("p (j b) -> p j b", j=2), inter, ALU.mult))
                link(tt(ns, ns, w, ALU.add))
                link(tt(tiny[:, 16:32].rearrange("p (j b) -> p j b", j=2), ns, q, ALU.mult))
                dve.wait_ge(st_ld, 48)
                sample(1, inter, w, q, 2, q)
                dve.sem_inc(ss_v, 1)
                dve.wait_ge(ss_a, 2)
                d = tiny[:, 32:48].rearrange("p (j b) -> p j b", j=2)
                link(tt(d, d, em, ALU.max))
                link(dve.reciprocal(d, d))
                link(tt(q, q, d, ALU.mult))
                dve.sem_inc(ss_v, 1)

            steps = dict(job=lambda _: None, rows=rows, conv=conv, gate=lambda _: None, lru=lru, rope=rope,
                         vt=lambda _: None, attn=attn, sattn=sattn, hprep=hprep, hchunk=hchunk, hsample=hsample,
                         hnorm=lambda _: gnorm(0, 11, 0, 'hg', 6), mprep=mprep, mchunk=mchunk, msample=msample,
                         mnorm=lambda _: gnorm(1, 18, 10, 'mg', 18))
            dve.wait_ge(cst_ld, 16)
            with dve.Fori(0, LAYERS) as l:
                dve.wait_ge(par_ld, 16)
                norm(0)
                for what, i in ORDER:
                    steps[what](i)
                for n in range(N_OUT):
                    dve.wait_ge(h_ld[0 if n < 2 else 1], 16)
                    for t in range(3):
                        cols = slice(t * TT, (t + 1) * TT)
                        dve.wait_ge(mm[t], N_WIN + n + 1)
                        tt(res[:, n, cols], res[:, n, cols], pj[:, t, 0:TT], ALU.add).then_inc(ev[t], 1)
                norm(1)
                with dve.Fori(0, FF_STEPS) as i:
                    U0 = N_WIN + N_OUT
                    for q in range(4):
                        for t in range(3):
                            dve.wait_ge(ev[t], i * 12 + (U0 + q + 1))
                        r = relu[:, q % 2, :]
                        if q >= 2:
                            dve.wait_ge(ff_l, i * 3 + (q - 1))
                        tt(hsq[:, q % 2, :], r, r, ALU.mult).then_inc(ff_q, 1)
                    dve.wait_ge(ff_h, i * 4 + 4)
                    tt(hid_lo[:, 3, :], hsq[:, 1, :], hid_hi[:, 3, :].bitcast(F32), ALU.subtract).then_inc(ff_l3, 1)
                    for n in range(KT):
                        for t in range(3):
                            cols = slice(t * TT, (t + 1) * TT)
                            dve.wait_ge(mm[t], i * 12 + (U0 + 4 + n + 1))
                            tt(res[:, n, cols], res[:, n, cols], pj[:, t, 0:TT], ALU.add).then_inc(ev[t], 1)
                u = N_WIN + N_OUT + 12 * FF_STEPS
                for half in range(2):
                    u += 4
                    for m in range(4):
                        u += 1
                        for t in range(3):
                            dve.wait_ge(ev[t], u)
                        link(tt(ple_sig[:], ple_sig[:], ple_proj[:, m, :], ALU.mult))
                        tt(res[:, 4 * half + m, :], res[:, 4 * half + m, :], ple_sig[:], ALU.add).then_inc(pv, 1)
                layer_end(dve)


def _tiles(w, k0, n):
    K, M = w.shape
    return w.reshape(K // P, P, M // P, P).transpose(1, 2, 0, 3).reshape(P, -1)


def _weights(w_in, w_out, w_up, w_down, w_gate, w_proj):
    W = np.zeros((LAYERS, N_JOBS, P, KT * P), np.float32)
    off = dict(ax=0, ag=256, q=512, k=768, bv=896, cq=1024, cf=1280, ci=1536, cg=1792, dq=2048, dk=2304,
               dv=2560, do=2816, gates=3072)
    h = np.arange(64)
    pair = [np.concatenate([h + 64 * g, h + 128 + 64 * g]) for g in range(2)]
    for l in range(LAYERS):
        for name, j in JOB.items():
            if name == 'gates':
                w = np.zeros((D, P), np.float32)
                w[:, 0:4] = w_in[l][:, 3072:3076]
                w[:, 32:36] = w_in[l][:, 3076:3080]
            elif name in ('q0', 'q1'):
                w = w_in[l][:, 512 + pair[int(name[1])]]
            elif name in off:
                w = w_in[l][:, off[name]:off[name] + P]
            else:
                a = off[name[:-1]] + P * int(name[-1])
                w = w_in[l][:, a:a + P]
            W[l, j] = _tiles(w, 0, 1)
        rows = np.arange(D)
        rows[256:512] = 256 + np.concatenate(pair)
        for m in range(KT):
            W[l, N_WIN + m] = _tiles(w_out[l][rows][:, m * P:(m + 1) * P], 0, 1)
        j = N_WIN + N_OUT
        for f in range(FF_STEPS):
            for q in range(4):
                a = (4 * f + q) * P
                W[l, j] = _tiles(w_up[l][:, a:a + P], 0, 1)
                j += 1
            for q in range(4):
                W[l, j] = _tiles(w_down[l][f * 512:(f + 1) * 512, q * 256:(q + 1) * 256], 0, 2)
                j += 1
        for half in range(2):
            W[l, j] = _tiles(w_proj[l][:, half * 512:(half + 1) * 512], 0, 4)
            j += 1
            for m in range(4):
                a = (4 * half + m) * P
                W[l, j] = _tiles(w_gate[l][:, a:a + P], 0, 1)
                j += 1
    return W


def _cols(x, s):
    a = np.concatenate([x, s], axis=-2)
    a = a.reshape(a.shape[:-1] + (a.shape[-1] // P, P))
    return np.ascontiguousarray(np.moveaxis(a, -3, -1).swapaxes(-3, -2))


def _constants():
    c = np.zeros((P, N_CONST), np.float32)
    p, f = np.arange(P)[:, None], np.arange(P)[None, :]
    c[:, 0:P] = p == f
    c[:, C_ONE:C_ONE + P] = 1.0
    c[:, C_BLK:C_BLK + P] = p // 64 == f // 64
    same = p // 64 == f // 64
    c[:, C_ROT:C_ROT + P] = np.where(same & (f % 64 < 8) & (p == f + 8), -1.0, 0.0) + \
        np.where(same & (f % 64 >= 8) & (f % 64 < 16) & (p == f - 8), 1.0, 0.0)
    c[:, C_MD:C_MD + P] = np.where(p <= f, 0.0, NEG)
    c[:, C_MP:C_MP + P] = np.where(f > p, 0.0, NEG)
    c[:, C_MC:C_MC + P] = np.where(f <= p, 0.0, NEG)
    c[:, C_EYE:C_EYE + 64] = p % 64 == np.arange(64)[None, :]
    for j in range(2):
        c[:, C_SEL + j * P:C_SEL + (j + 1) * P] = p % 32 == 2 * j + f // 64
    for l in range(NLEV):
        b = 1 << l
        t = np.arange(P)[(np.arange(P) // b) % 2 == 1][None, :]
        c[:, C_LEV + 64 * l:C_LEV + 64 * l + 64] = ((p // b) % 2 == 0) & (p // (2 * b) == t // (2 * b))
    return c


def _rope_table():
    inv = np.power(np.float32(500000.0), -np.arange(8, dtype=np.float32) * np.float32(2.0 / 16))
    pos = np.concatenate([np.arange(SEQ), np.full(DEC, 1024)]).astype(np.float32)
    ang = (pos[:, None] * inv[None, :]).astype(np.float32)
    r = np.zeros((P, 2, T), np.float32)
    r[:, 0] = 1.0
    for d in range(P):
        if d % 64 < 16:
            r[d, 0] = np.cos(ang[:, d % 8])
            r[d, 1] = np.sin(ang[:, d % 8])
    return r


def _layout(i):
    L = LAYERS

    def chan(a):
        return a.reshape((L, -1, P) + a.shape[2:]).swapaxes(1, 2)

    par = np.zeros((L, P, N_PAR), np.float32)

    def put(name, a):
        a = a.reshape(L, a.shape[1], -1)
        par[:, :a.shape[1], PC[name]:PC[name] + a.shape[2]] = a

    put('g1', chan(i['norm1_g']))
    put('g2', chan(i['norm2_g']))
    put('cw', chan(i['conv_w'].transpose(0, 2, 1)).transpose(0, 1, 3, 2))
    for n, k in (('cb', 'conv_b'), ('br', 'lru_br'), ('bi', 'lru_bi'), ('lam', 'lru_lam')):
        put(n, chan(i[k]))
    for n, k in (('qg', 'q_norm_g'), ('kg', 'k_norm_g'), ('hg', 'hgrn_norm_g'), ('mg', 'mlstm_norm_g')):
        put(n, np.tile(i[k], (1, 2))[:, :, None])
    gam = chan(i['hgrn_gamma'])
    for l in range(L):
        par[l, :, PC['gam']:PC['gam'] + 4] = gam.transpose(1, 0, 2).reshape(P, 4)
        par[l, :, PC['lm']] = float(l > 0)
        par[l, :, PC['sink']:PC['sink'] + 4] = i['attn_sinks'][l][None, :]
    put('sinkc', i['attn_sinks'][:, :, None])
    put('ib', i['mlstm_ib'][:, :, None])
    put('fb', i['mlstm_fb'][:, :, None])
    for n, k in (('wr', 'lru_wr'), ('wi', 'lru_wi')):
        for j in range(2):
            for h in range(2):
                a = PC[n] + j * P + 64 * h
                par[:, 64 * h:64 * h + 64, a:a + 64] = i[k][:, 2 * j + h]
    put('conv', chan(i['state_rglru_conv'].transpose(0, 3, 2, 1)))
    put('h0', chan(i['state_rglru_h'].transpose(0, 2, 1)))
    put('n0', chan(i['state_mlstm_n'].reshape(L, DEC, 256).transpose(0, 2, 1)))
    put('m0', i['state_mlstm_m'].transpose(0, 2, 1))

    def state(a):
        return np.ascontiguousarray(chan(a.transpose(0, 2, 3, 1, 4).reshape(L, 256, DEC, 64)).reshape(L, P, 1024))

    kc = i['cache_swa_k'].reshape(L, DEC, P, P)[:, :, 1:]
    vc = i['cache_swa_v'].reshape(L, DEC, P, P)[:, :, 1:]
    return dict(
        x=_cols(i['x_prompt'][0], i['x_sample'][:, 0]),
        consts=_constants(), rope=_rope_table(), par=par,
        w=_weights(i['w_in'], i['w_out'], i['w_up'], i['w_down'], i['w_ple_gate'], i['w_ple_proj']),
        p=_cols(i['p_prompt'][:, 0], i['p_sample'][:, :, 0]),
        kc=np.ascontiguousarray(kc.transpose(0, 3, 1, 2)), vc=np.ascontiguousarray(vc.transpose(0, 2, 1, 3)),
        hs=state(i['state_hgrn_s']), cs=state(i['state_mlstm_c']))


_OUTS = dict(y=(P, KT, T), so=(LAYERS, P, N_SO), kv=(LAYERS, P, 2, CH), kc=(LAYERS, P, DEC, P), vc=(LAYERS, P, DEC, P),
             hp=(LAYERS, P, 2, P), cp=(LAYERS, P, 2, P), hs=(LAYERS, P, 1024), cs=(LAYERS, P, 1024))


def _results(r):
    L = LAYERS
    y = r['y'].transpose(2, 1, 0).reshape(T, D)
    so = r['so']

    def part(name, *shape):
        n = int(np.prod(shape))
        return so[:, :, OC[name]:OC[name] + n].reshape((L, P) + shape)

    def unchan(a):
        return a.swapaxes(1, 2).reshape((L, 256) + a.shape[3:])

    def blocks(a):
        o = np.stack([a[:, 64 * h:64 * h + 64, j, 64 * h:64 * h + 64] for j in range(2) for h in range(2)], axis=1)
        return o[:, None]

    def states(a):
        return unchan(a.reshape(L, P, 2, DEC, 64)).reshape(L, 4, 64, DEC, 64).transpose(0, 3, 1, 2, 4)

    def cache(a):
        return np.roll(a, -1, axis=1).transpose(0, 2, 1, 3).reshape(L, DEC, P, 2, 64)

    kv = r['kv'].transpose(0, 2, 3, 1).reshape(L, 2, 1, CH, 2, 64)
    outs = (
        y[:SEQ].reshape(1, SEQ, D), y[SEQ:].reshape(DEC, 1, D),
        unchan(part('hp', 2)).reshape(L, 1, 256),
        unchan(part('convp', 2, 3)).transpose(0, 2, 1).reshape(L, 1, 3, 256),
        kv[:, 0], kv[:, 1], blocks(r['hp']), blocks(r['cp']),
        unchan(part('np', 2)).reshape(L, 1, 4, 64), part('mp', 1)[:, 0:4, 0].reshape(L, 1, 4),
        unchan(part('hs', 2, DEC)).transpose(0, 2, 1),
        unchan(part('convs', 2, 3, DEC)).transpose(0, 3, 2, 1),
        cache(r['kc'].transpose(0, 3, 2, 1)), cache(r['vc']), states(r['hs']), states(r['cs']),
        unchan(part('ns', 2, DEC)).transpose(0, 2, 1).reshape(L, DEC, 4, 64),
        part('ms', DEC)[:, 0:4].transpose(0, 2, 1))
    return tuple(np.ascontiguousarray(o) for o in outs)


def kernel(**inputs):
    import concourse.bacc as bacc
    from concourse.bass_utils import run_bass_kernel_spmd

    nc = bacc.Bacc("TRN2", target_bir_lowering=False, num_devices=1)
    arrays = {f"in_{k}": v for k, v in _layout({k: np.asarray(v) for k, v in inputs.items()}).items()}
    ins = {k: nc.dram_tensor(k, v.shape, mybir.dt.from_np(v.dtype), kind="ExternalInput").ap() for k, v in arrays.items()}
    outs = {k: nc.dram_tensor(f"out_{k}", s, F32, kind="ExternalOutput").ap() for k, s in _OUTS.items()}
    build(nc, ins['in_x'], ins['in_consts'], ins['in_rope'], ins['in_par'], ins['in_w'], ins['in_p'], ins['in_kc'],
          ins['in_vc'], ins['in_hs'], ins['in_cs'], outs['y'], outs['so'], outs['kv'], outs['kc'], outs['vc'],
          outs['hp'], outs['cp'], outs['hs'], outs['cs'])
    r = run_bass_kernel_spmd(nc, [arrays], core_ids=[0])
    return _results({k: r.results[0][f"out_{k}"] for k in _OUTS})
```

```python
from contextlib import ExitStack

import numpy as np

import concourse.bass as bass
from concourse import mybir

ALU = mybir.AluOpType
ACT = mybir.ActivationFunctionType
AX_X = mybir.AxisListType.X
F32 = mybir.dt.float32
F32R = mybir.dt.float32r
U32 = mybir.dt.uint32

P = 128
LAYERS, SEQ, DEC, D, D_FF, PLE = 2, 1024, 8, 1024, 4096, 256
T = SEQ + DEC
TT = T // 3
KT = D // P
CH = 128
NC = SEQ // CH
NLEV = 7
NEG = -1e30
EPS = 1e-6
FF_TILES = 4
FF_STEPS = D_FF // (P * FF_TILES)
WIN = ['gates', 'ax0', 'ax1', 'q0', 'q1', 'k', 'ag0', 'ag1', 'bv', 'ci0', 'ci1', 'dv0', 'dv1',
       'dq0', 'dq1', 'do0', 'do1', 'cf0', 'cf1', 'cq0', 'cq1', 'dk0', 'cg0', 'cg1', 'dk1']
JOB = {name: j for j, name in enumerate(WIN)}
SLOT = dict(ax0=10, ax1=11, ag0=12, ag1=13, q0=14, q1=15, k=16, bv=17, ci0=18, ci1=19, dv0=4, dv1=5,
            dq0=10, dq1=11, cq0=0, cq1=1, cf0=2, cf1=3, cg0=6, cg1=7, dk0=16, dk1=17, do0=18, do1=19)
VT_COL = dict(bv=0, ci0=128, ci1=256, dv0=384, dv1=512)
N_WIN, N_OUT, N_FF, N_PLE = len(WIN), KT, FF_STEPS * 8, KT + 2
N_JOBS = N_WIN + N_OUT + N_FF + N_PLE

LEV_AT = [(0, 128), (0, 192), (2, 0), (2, 64), (2, 128), (2, 192), (0, 0)]

Y_SLOT = (12, 13, 14, 15, 0, 1, 10, 11)

C_ID, C_ONE, C_BLK, C_ROT, C_MD, C_MP, C_MC, C_EYE, C_LEV = 0, 128, 256, 384, 512, 640, 768, 896, 960
C_SEL = C_LEV + NLEV * 64
N_CONST = C_SEL + 2 * P
_sizes = dict(g1=8, g2=8, cw=8, cb=2, br=2, bi=2, lam=2, qg=1, kg=1, hg=1, mg=1, gam=4, lm=1, sink=4,
              sinkc=1, ib=1, fb=1, wr=256, wi=256, conv=48, h0=16, n0=16, m0=8)
PC, N_PAR = {}, 0
for _n, _s in _sizes.items():
    PC[_n] = N_PAR
    N_PAR += _s
_sizes = dict(convp=6, convs=48, hp=2, hs=16, np=2, ns=16, mp=1, ms=8)
OC, N_SO = {}, 0
for _n, _s in _sizes.items():
    OC[_n] = N_SO
    N_SO += _s

def _order():
    o = [('job', 0), ('rows', 0), ('job', 1), ('rows', 1), ('job', 2), ('job', 3), ('rows', 2), ('job', 4), ('rows', 3),
         ('conv', 0), ('job', 5), ('rope', 0), ('job', 6), ('rope', 1), ('gate', 0), ('job', 7), ('lru', 0), ('job', 8),
         ('vt', 0)]
    fill = [[('job', 9)], [('job', 10)], [('vt', 1)], [('job', 11)], [('vt', 2)], [('job', 12)],
            [('vt', 3)], [('job', 13)], [('vt', 4)], [('job', 14)]]
    for c in range(NC + 2):
        o += [('attn', c)] + fill[c]
    o += [('sattn', 0), ('job', 15), ('sattn', 1), ('job', 16), ('sattn', 2), ('job', 17), ('job', 18), ('hprep', 0),
          ('job', 19), ('hsample', 0), ('job', 20), ('job', 21), ('hsample', 1), ('job', 22), ('hdiag', 0)]
    fill = {0: [('job', 23)], 2: [('job', 24)], 4: [('mprep', 0)], 5: [('mprep', 1)],
            6: [('mprep', 2), ('mprep', 3)], 7: [('hnorm', 0)]}
    for c in range(NC):
        o += [('hchunk', c)] + fill.get(c, [])
    for c in range(NC + 1):
        o += [('mchunk', c)] + ([('hnorm', 1)] if c == 1 else [])
    return o + [('msample', 0), ('mnorm', 0)]


ORDER = _order()


def build(nc, x_in, consts, rope_in, par_in, w_in, p_in, kc_in, vc_in, hs_in, cs_in,
          y_out, so_out, kv_out, kc_out, vc_out, hp_out, cp_out, hs_out, cs_out):
    with ExitStack() as ctx:
        def sem(name):
            s = ctx.enter_context(nc.semaphore(name))
            sems.append(s)
            return s

        def sb(name, shape, dt=F32, stack=ctx):
            return stack.enter_context(nc.sbuf_tensor(name, shape, dt))

        sems = []
        pj = ctx.enter_context(nc.psum_tensor("pj", [P, 3, 512], F32))
        pm = ctx.enter_context(nc.psum_tensor("pm", [P, 5, 512], F32))

        res = sb("res", [P, KT, T])
        w_raw = sb("w_raw", [P, 2, KT * P])
        w_hi, w_lo = sb("w_hi", [P, 2, KT * P], F32R), sb("w_lo", [P, 2, KT * P], F32R)
        cst, par, so = sb("cst", [P, N_CONST]), sb("par", [P, N_PAR]), sb("so", [P, N_SO])
        small = sb("small", [P, 2 * T])
        ex2 = small[:, 0:4 * CH].rearrange("p (a j t) -> p a j t", a=2, j=2)
        att = small[:, 4 * CH:8 * CH].rearrange("p (i t) -> p i t", i=4)
        qe, ktok, h_st, lev4 = (small[:, (8 + 2 * i) * CH:(10 + 2 * i) * CH].rearrange("p (j t) -> p j t", j=2)
                                for i in range(4))
        nrm, sqr = small[:, 0:T], small[:, T:2 * T]
        v_smp = sb("v_smp", [P, 4, DEC])
        bw = sb("bw", [P, NC, 2, 4])
        same = sb("same", [P, 2, NC, 2])
        tiny, warm = sb("tiny", [P, 48]), sb("warm", [P, 1])
        with ExitStack() as proj:
            n_hi, n_lo = sb("n_hi", [P, KT, T], F32R, proj), sb("n_lo", [P, KT, T], F32R, proj)
        with ExitStack() as rows_mem:
            mrow = sb("mrow", [P, 2 * KT, T], stack=rows_mem)
        inter, em = mrow[:, 6:8, :], mrow[:, KT + 6:KT + 8, :]
        with ExitStack() as ff:
            hid_hi, hid_lo = (sb(n, [P, FF_TILES, T], F32R, ff) for n in ("hid_hi", "hid_lo"))
        ple_out = sb("ple_out", [P, 2 * FF_TILES, T])
        relu, hsq = sb("relu", [P, 2, T]), sb("hsq", [P, 2, T])
        ple_hi, ple_lo = sb("ple_hi", [P, 2, T], F32R), sb("ple_lo", [P, 2, T], F32R)
        ple_raw, ple_proj, ple_sig = hsq, ple_out[:, 0:4, :], ple_out[:, 4, :]
        with ExitStack() as mixer:
            ext = sb("ext", [P, 12, T], stack=mixer)
            vt = sb("vt", [P, NC, 640], stack=mixer)
        m_hi, m_lo = sb("m_hi", [P, KT, T], F32R), sb("m_lo", [P, KT, T], F32R)

        def slot(a, n=1):
            t = res[:, a:a + n, :] if a < KT else ext[:, a - KT:a - KT + n, :]
            return t if n > 1 else t[:, 0, :]

        def flat(a, n=1):
            return (res[:, a:a + n, :] if a < KT else ext[:, a - KT:a - KT + n, :]).rearrange("p a t -> p (a t)")

        def pc(name, i=0, n=1):
            return par[:, PC[name] + i:PC[name] + i + n]

        def oc(name, i=0, n=1):
            return so[:, OC[name] + i:OC[name] + i + n]

        ident, ones, blk = cst[:, 0:P], cst[:, C_ONE:C_ONE + P], cst[:, C_BLK:C_BLK + P]
        rot, mask_d = cst[:, C_ROT:C_ROT + P], cst[:, C_MD:C_MD + P]
        eye, sel = cst[:, C_EYE:C_EYE + 64], cst[:, C_SEL:C_SEL + 2 * P]
        S0 = SEQ

        w_ld = [sem("w_ld0"), sem("w_ld1")]
        hi_made, lo_made = sem("hi_made"), sem("lo_made")
        mm = [sem(f"mm{t}") for t in range(3)]
        ev = [sem(f"ev{t}") for t in range(3)]
        cst_ld, par_ld, rope_ld, w_nx = (sem(n) for n in ("cst_ld", "par_ld", "rope_ld", "w_nx"))
        h_ld, ff_l3 = [sem("h_ld0"), sem("h_ld1")], sem("ff_l3")
        smp_ld, st_ld, ple_ld = sem("smp_ld"), sem("st_ld"), sem("ple_ld")
        mix_mm, mix_ev = sem("mix_mm"), sem("mix_ev")
        n1, n2 = ([sem(f"n{i}_" + n) for n in ("sq", "add", "mm", "rs")] for i in (1, 2))
        nrm_n, nrm_hi, nrm_lo, nrm_lo_v = (sem("nrm_" + n) for n in ("n", "hi", "lo", "lo_v"))
        m_h, m_l, r_h, r_l = sem("m_h"), sem("m_l"), sem("r_h"), sem("r_l")
        rows_a, rows_v, rows_t, rows_c = (sem("rows_" + n) for n in "avtc")
        lam_a, lam_v = sem("lam_a"), sem("lam_v")
        conv_v, lru_a, lru_v = sem("conv_v"), sem("lru_a"), sem("lru_v")
        rope_a, rope_r, rope_v = sem("rope_a"), sem("rope_r"), sem("rope_v")
        vt_t, vt_c = sem("vt_t"), sem("vt_c")
        at_s, at_m, at_e, at_p, at_t, at_c, at_o, at_w = (sem("at_" + n) for n in
                                                          ("s", "m", "e", "p", "t", "c", "o", "w"))
        sa_v, sa_t, sa_a, sa_x = sem("sa_v"), sem("sa_t"), sem("sa_a"), sem("sa_x")
        hp_v, hp_a = sem("hp_v"), sem("hp_a")
        sm_p, sm_t, sm_c = sem("sm_p"), sem("sm_t"), sem("sm_c")
        hc_subk, hc_kk, hc_kq2 = sem("hc_subk"), sem("hc_kk"), sem("hc_kq2")
        hc_sub, hc_exp, hc_kq, hc_lt, hc_lv, hc_tt, hc_tc, hc_ot, hc_oc, hc_sv = (
            sem("hc_" + n) for n in ("sub", "exp", "kq", "lt", "lv", "tt", "tc", "ot", "oc", "sv"))
        ss_v, ss_t, ss_a = sem("ss_v"), sem("ss_t"), sem("ss_a")
        nm_a, nm_r, nm_g, nm_v = sem("nm_a"), sem("nm_r"), sem("nm_g"), sem("nm_v")
        mp_mm, mp_ev = sem("mp_mm"), sem("mp_ev")
        mc_t, mc_w, mc_s, mc_tt, mc_k, mc_q, mc_nt, mc_d, mc_h, mc_sv = (
            sem("mc_" + n) for n in ("t", "w", "s", "tt", "k", "q", "nt", "d", "h", "sv"))
        y_hi, y_lo, y_lo7 = sem("y_hi"), sem("y_lo"), sem("y_lo7")
        ff_h, ff_l = sem("ff_h"), sem("ff_l")
        ph, pl, pv = sem("ph"), sem("pl"), sem("pv")
        kv_st, so_st, smp_st, mix_st = sem("kv_st"), sem("so_st"), sem("smp_st"), sem("mix_st")
        ch_a, ch_v = sem("ch_a"), sem("ch_v")
        clearable = [s for s in sems if s is not cst_ld]
        late = [hi_made, lo_made, ch_a, ch_v, pv, so_st, w_nx] + w_ld + mm + ev + n1
        middle = [par_ld, ple_ld, ff_h, ff_l, ff_l3, ph, pl, r_h, r_l]
        mixer_sems = [s for s in clearable if s not in late and s not in middle]
        arrived, go, left = sem("arrived"), sem("go"), sem("left")
        y_st = sem("y_st")
        x_ld = [sem(f"x_ld{i}") for i in range(4)]
        w0_hi = sem("w0_hi")
        n0 = [sem("n0_" + n) for n in ("sq", "add", "mm", "rs")]

        def linker(eng, s):
            n = [0]

            def link(ins):
                n[0] += 1
                ins.then_inc(s, 1)
                eng.wait_ge(s, n[0])
            return link

        def layer_end(eng):
            eng.drain().then_inc(arrived, 1)
            eng.wait_ge(go, 1)
            eng.sem_inc(left, 1)

        early = vt[:, :, 0:CH]
        mc_st = slot(9)[:, 0:4 * CH].rearrange("p (j s e) -> p j s e", j=2, s=2)

        def level(l):
            if l < 4:
                return early[:, 2 * l:2 * l + 2, :]
            return (lev4 if l == 4 else pc('wr', (l - 5) * 256, 256).rearrange("p (j t) -> p j t", j=2))

        q_diag = slot(9)[:, 0:8 * CH].rearrange("p (l j h t) -> p l j h t", l=4, j=2, h=2)

        def halves(x, l):
            v = x.rearrange("p j (n two b) -> p j n two b", two=2, b=1 << l)
            return v[:, :, :, 0, :], v[:, :, :, 1, :]

        GROUPS = ((0, 1), (2, 3, 4, 5), (6,))

        def sm_half(h):
            return flat(7)[:, 512 * h:512 * h + 512]

        def sm_state(j):
            return flat(6)[:, 512 * j:512 * j + 512]

        vt_flat = vt[:].rearrange("p c d -> p (c d)")
        rp_sq = [vt_flat[:, n * T:(n + 1) * T] for n in range(3)]
        rp_rs = [vt_flat[:, 3 * T:4 * T], nrm, sqr]

        mc_att = (att[:], pc('wr', 0, 512).rearrange("p (i t) -> p i t", i=4))
        mc_qe, mc_kt = (qe[:], early[:, 2:4, :]), (ktok[:], early[:, 4:6, :])

        DVE_LO = (0, 3, 6)

        def NORM_LO(k):
            mine = k in DVE_LO
            return (nrm_lo_v if mine else nrm_lo), sum((x in DVE_LO) == mine for x in range(k + 1))

        block = ctx.enter_context(nc.Block())

        @block.sync
        def _(sp):
            for g in range(4):
                sp.dma_start(res[:, 2 * g:2 * g + 2, :], x_in[:, 2 * g:2 * g + 2, :]).then_inc(x_ld[g], 16)
            sp.dma_start(cst[:], consts).then_inc(cst_ld, 16)
            sp.dma_start(par[:], par_in[0]).then_inc(cst_ld, 16)
            for j in range(2):
                sp.dma_start(w_raw[:, j, :], w_in[j]).then_inc(cst_ld, 16)
            for k in range(KT):
                if k % 2 == 0:
                    sp.wait_ge(x_ld[k // 2], 16)
                sp.dma_start(y_out[0][:, k, :], res[:, k, :]).then_inc(y_st, 16)

            with sp.Fori(0, LAYERS) as l:
                def load(j):
                    sp.wait_ge(hi_made, j - 1)
                    sp.wait_ge(lo_made, j - 1)
                    sp.dma_start(w_raw[:, j % 2, :], w_in[l * N_JOBS + j]).then_inc(w_ld[j % 2], 16)

                sp.dma_start(slot(18, 2), rope_in).then_inc(rope_ld, 16)
                for j in range(2, N_WIN + N_OUT):
                    load(j)
                with sp.Fori(0, FF_STEPS) as i:
                    for q in range(8):
                        j0 = N_WIN + N_OUT + q
                        sp.wait_ge(hi_made, i * 8 + (j0 - 1))
                        sp.wait_ge(lo_made, i * 8 + (j0 - 1))
                        sp.dma_start(w_raw[:, j0 % 2, :], w_in[l * N_JOBS + i * 8 + j0]).then_inc(w_ld[j0 % 2], 16)
                sp.dma_start(par[:], par_in[l + 1]).then_inc(par_ld, 16)
                for j in range(N_WIN + N_OUT + N_FF, N_JOBS):
                    load(j)
                for s in mixer_sems:
                    sp.sem_clear(s)
                sp.wait_ge(hi_made, N_JOBS)
                sp.wait_ge(lo_made, N_JOBS)
                for j in range(2):
                    sp.dma_start(w_raw[:, j, :], w_in[(l + 1) * N_JOBS + j]).then_inc(w_nx, 16)
                sp.wait_ge(w_nx, 32)
                sp.wait_ge(par_ld, 16)
                for s in middle:
                    sp.sem_clear(s)
                sp.wait_ge(arrived, 4)
                for s in late + [arrived]:
                    sp.sem_clear(s)
                sp.sem_inc(go, 4)
                sp.wait_ge(left, 4)
                sp.sem_clear(left)
                sp.sem_clear(go)
            sp.wait_ge(y_st, 16 * KT * (LAYERS + 1))

        @block.tensor
        def _(pe):
            def unit(par_j, k0, nk, hi, lo, u, first_waits=None, vals=None, tail=0, between=None):
                for ks in ((range(nk),) if not tail else (range(nk - tail), range(nk - tail, nk))):
                    for t in range(3):
                        if ks[0] == 0 and (vals is not None or u):
                            pe.wait_ge(ev[t], u if vals is None else vals)
                        cols = slice(t * TT, (t + 1) * TT)
                        for k in ks:
                            if first_waits is not None and t == 0:
                                first_waits(k)
                            ws = slice((k0 + k) * P, (k0 + k + 1) * P)
                            wh, wl = w_hi[:, par_j, ws], w_lo[:, par_j, ws]
                            pe.matmul(pj[:, t, 0:TT], wh, hi[:, k, cols], start=(k == 0), stop=False)
                            pe.matmul(pj[:, t, 0:TT], wh, lo[:, k, cols], start=False, stop=False)
                            last = pe.matmul(pj[:, t, 0:TT], wl, hi[:, k, cols], start=False, stop=(k == nk - 1))
                        if ks[-1] == nk - 1:
                            last.then_inc(mm[t], 1)
                        elif between and t == between[0]:
                            between[1]()

            def mix(n, lhs, rhs):
                for t in range(3):
                    if n > 1:
                        pe.wait_ge(mix_ev, 3 * (n - 2) + t + 1)
                    pe.matmul(pm[:, t, 0:TT], lhs, rhs[:, t * TT:(t + 1) * TT], start=True, stop=True).then_inc(mix_mm, 1)

            def norm(sems, added=KT - 1):
                pe.wait_ge(sems[1], added - 1)
                for t in range(3):
                    last = pe.matmul(pm[:, t, 0:TT], ones, nrm[:, t * TT:(t + 1) * TT], start=True, stop=added == KT)
                    if added == KT:
                        last.then_inc(sems[2], 1)
                if added == KT:
                    return
                pe.wait_ge(sems[0], KT)
                for t in range(3):
                    pe.matmul(pm[:, t, 0:TT], ones, sqr[:, t * TT:(t + 1) * TT], start=False,
                              stop=True).then_inc(sems[2], 1)

            def norm_tile(k):
                pe.wait_ge(*NORM_LO(k))

            def job(j):
                pe.wait_ge(lo_made, j + 1)
                unit(j % 2, 0, KT, n_hi, n_lo, j,
                     norm_tile if j == 0 else None)

            def rows(i):
                if i < 3:
                    return
                pe.wait_ge(rows_v, 9)
                for c in range(NC):
                    pe.matmul(pm[:, 3, c * 8:c * 8 + 4], slot(6)[0:4, c * CH:(c + 1) * CH], ident[0:4, 0:4],
                              is_transpose=True, start=True, stop=True)
                    last = pe.matmul(pm[:, 4, c * 8:c * 8 + 4], slot(6)[32:36, c * CH:(c + 1) * CH],
                                     ident[32:36, 32:36], is_transpose=True, start=True, stop=True)
                last.then_inc(rows_t, 1)

            def gate(_):
                pe.wait_ge(conv_v, 1)
                for n, (w, j) in enumerate((('wr', 0), ('wr', 1), ('wi', 0), ('wi', 1))):
                    mix(7 + n, pc(w, j * P, P), slot(j))

            def rope(part):
                for n in range(3):
                    if part == 0:
                        pe.wait_ge(rope_a, n + 1)
                        mix(1 + n, blk, rp_sq[n])
                    else:
                        pe.wait_ge(rope_v, n + 1)
                        mix(4 + n, rot, slot(14 + n))

            def vtrans(v):
                src = slot(SLOT[list(VT_COL)[v]])
                pe.wait_ge(ev[2], JOB[list(VT_COL)[v]] + 1)
                if v == 0:
                    pe.wait_ge(rows_c, 2)
                if attn_before[v]:
                    pe.wait_ge(at_o, attn_before[v])
                for h in range(2):
                    if 2 * v + h >= 1:
                        pe.wait_ge(vt_c, 2 * v + h)
                    for q in range(4):
                        c = 4 * h + q
                        last = pe.transpose(pm[:, 4, q * P:(q + 1) * P], src[:, c * CH:(c + 1) * CH], ident)
                    last.then_inc(vt_t, 1)

            def attn(step):
                c = step
                if c < NC:
                    if c == 0:
                        pe.wait_ge(mix_ev, 30)
                        pe.wait_ge(rope_v, 6)
                    else:
                        pe.wait_ge(at_m, c)
                    lo_k = 0 if c else CH
                    for j in range(2):
                        for hh in range(2):
                            r = slice(64 * hh, 64 * hh + 64)
                            last = pe.matmul(pm[:, hh, j * 256 + lo_k:j * 256 + 256],
                                             slot(14 + j)[r, c * CH:(c + 1) * CH],
                                             slot(16)[r, (c - 1) * CH + lo_k:(c + 1) * CH], start=True, stop=True)
                    last.then_inc(at_s, 1)
                c = step - 2
                if c >= 0:
                    pt = flat(2 + c % 2)[:, 0:1024].rearrange("p (i h t) -> p i h t", i=4, h=2)
                    pe.wait_ge(at_c, c + 1)
                    pe.wait_ge(vt_c, max(2, vt_before[step]))
                    if c:
                        pe.wait_ge(at_o, c)
                    for j in range(2):
                        for hh in range(2):
                            for h in range(0 if c else 1, 2):
                                last = pe.matmul(pm[64 * hh:64 * hh + 64, 4, j * CH:(j + 1) * CH],
                                                 vt[:, c - 1 + h, 64 * hh:64 * hh + 64], pt[:, 2 * hh + j, h, :],
                                                 start=(h == (0 if c else 1)), stop=(h == 1))
                    last.then_inc(at_w, 1)
                c = step - 1
                if 0 <= c < NC:
                    pe.wait_ge(at_p, c + 1)
                    if c:
                        pe.wait_ge(at_c, c)
                    sc = flat(c % 2)[:, 0:1024].rearrange("p (i s) -> p i s", i=4)
                    for i in range(4):
                        for h in range(0 if c else 1, 2):
                            last = pe.transpose(pm[:, 2 + i // 2, (i % 2 * 2 + h) * P:(i % 2 * 2 + h + 1) * P],
                                                sc[:, i, h * CH:(h + 1) * CH], ident)
                    last.then_inc(at_t, 1)

            vt_before, attn_before, n, m = {}, {}, 0, 0
            for what, i in ORDER:
                if what == 'vt':
                    n, attn_before[i] = n + 2, m
                if what == 'attn':
                    vt_before[i], m = n, max(0, i - 1)

            def sattn(part):
                kc = flat(6)[:, 0:1024].rearrange("p (b s) -> p b s", b=DEC)
                qb = flat(0)[:, 0:32].rearrange("p (b i) -> p b i", b=DEC)
                pr = flat(2)[0:4, 0:1024].rearrange("p (b s) -> p b s", b=DEC)
                vc = flat(7)[:, 0:1024].rearrange("p (b d) -> p b d", b=DEC)
                if part == 0:
                    pe.wait_ge(at_o, NC)
                    pe.wait_ge(sa_v, 1)
                    pe.wait_ge(vt_c, 10)
                    for b in range(DEC):
                        last = pe.matmul(pm[0:1, b // 4, (b % 4) * P:(b % 4 + 1) * P], slot(17)[:, S0 + b:S0 + b + 1],
                                         ident, start=True, stop=True)
                    last.then_inc(sa_t, 1)
                    for b in range(DEC):
                        last = pe.matmul(pm[0:4, 2 + b // 4, (b % 4) * P:(b % 4 + 1) * P], qb[:, b, :], kc[:, b, :],
                                         start=True, stop=True)
                    last.then_inc(sa_t, 1)
                elif part == 1:
                    pe.wait_ge(sa_v, 2)
                    for b in range(DEC):
                        last = pe.transpose(pm[:, 4, b * 4:b * 4 + 4], pr[:, b, :], ident[0:4, 0:4])
                    last.then_inc(sa_t, 1)
                else:
                    pe.wait_ge(sa_v, 3)
                    pe.wait_ge(sa_a, 1)
                    for b in range(DEC):
                        last = pe.matmul(pm[:, 4, 64 + b * 4:64 + b * 4 + 4], vc[:, b, :],
                                         flat(3)[:, b * 4:b * 4 + 4], start=True, stop=True)
                    last.then_inc(sa_t, 1)

            def hdiag(_):
                for j in range(2):
                    pe.wait_ge(sm_p, j + 1)
                    for c in range(NC):
                        last = pe.matmul(pm[:, 4, (j * NC + c) * 2:(j * NC + c) * 2 + 2], slot(7)[:, c * CH:(c + 1) * CH],
                                         blk[:, 0:P:64], start=True, stop=True)
                    last.then_inc(sm_t, 1)

            def hchunk(c):
                if c == 0:
                    pe.wait_ge(sm_c, 1)
                    pe.wait_ge(sa_v, 4)
                    pe.wait_ge(hp_v, 1)
                    for t in range(3):
                        pe.wait_ge(ev[t], JOB['cq1'] + 1)
                else:
                    pe.wait_ge(hc_lv, 8 * c)
                for g, levels in enumerate(GROUPS):
                    pe.wait_ge(hc_kq, 3 * c + g + 1)
                    pe.wait_ge(hc_kk, 3 * c + g + 1)
                    if g == 1 and c:
                        pe.wait_ge(hc_oc, c)
                        pe.wait_ge(hc_sv, c)
                    if g == 2:
                        pe.wait_ge(hc_lv, 8 * c + 3)
                    for l in levels:
                        bank, at = LEV_AT[l]
                        el, half = level(l), 1 << l
                        if l == 4:
                            pe.wait_ge(hc_kq2, c + 1)
                        for j in range(2):
                            if l < 6:
                                out = pm[:, bank + j, :].rearrange("p (h s) -> p h s", h=2)[:, :, at:at + 64]
                                last = pe.matmul(out, el[:, j, :], q_diag[:, l % 4, j], start=True, stop=True)
                                continue
                            for hh in range(2):
                                r = slice(64 * hh, 64 * hh + 64)
                                last = pe.matmul(pm[:, bank + hh, j * 256 + at:j * 256 + at + 64], el[r, j, :],
                                                 el[r, j, half:], start=True, stop=True)
                    last.then_inc(hc_lt, 1)
                if c:
                    pe.wait_ge(hc_tc, c)
                for j in range(2):
                    last = pe.transpose(pm[:, 4, j * P:(j + 1) * P], ex2[:, 1, j, :], ident)
                last.then_inc(hc_tt, 1)
                pe.wait_ge(hc_lv, 8 * (c + 1))
                for j in range(2):
                    pe.matmul(pm[:, 2, j * CH:(j + 1) * CH], h_st[:, j, :], qe[:, j, :], start=True, stop=False,
                              skip_group_check=True)
                    for hh in range(2):
                        v0 = 128 + (2 * j + hh) * 64
                        last = pe.matmul(pm[64 * hh:64 * hh + 64, 2, j * CH:(j + 1) * CH], vt[:, c, v0:v0 + 64],
                                         att[:, 2 * j + hh, :], start=False, stop=(hh == 1), skip_group_check=True)
                last.then_inc(hc_ot, 1)
                pe.wait_ge(hc_tc, c + 1)
                for j in range(2):
                    last = pe.matmul(pm[:, 3, j * P:(j + 1) * P], ktok[:, j, :], vt[:, c, 128 + j * P:128 + (j + 1) * P],
                                     start=True, stop=True)
                last.then_inc(hc_ot, 1)

            def hsample(part):
                for n in range(2):
                    pe.wait_ge(ss_v, 2 * part + n + 1)
                    pe.matmul(pm[:, 2 * part + n, :], blk, sm_half(1 if part and not n else 0),
                              start=True, stop=True).then_inc(ss_t, 1)

            def gnorm(g, n0):
                for j in range(2):
                    pe.wait_ge(nm_a, 2 * g + j + 1)
                    mix(n0 + j, blk, slot(2 + j))

            def mprep(n):
                if n == 0:
                    for t in range(3):
                        pe.wait_ge(ev[t], N_WIN)
                rows, at = slot(8), (64 if n < 2 else 32)
                for t in range(3):
                    if n:
                        pe.wait_ge(mp_ev, 3 * (n - 1) + t + 1)
                    pe.matmul(pj[:, t, 0:TT], sel[at:at + 4, n % 2 * P:(n % 2 + 1) * P],
                              rows[at:at + 4, t * TT:(t + 1) * TT], start=True, stop=True).then_inc(mp_mm, 1)
                if n == 3:
                    pe.wait_ge(mp_ev, 10)
                    for j in range(2):
                        last = pe.matmul(pj[:, 0, j * 8:j * 8 + 8], sel[0:4, j * P:(j + 1) * P],
                                         slot(8)[0:4, S0:S0 + 8], start=True, stop=True)
                    last.then_inc(mp_mm, 1)

            def mchunk(step):
                q, k = slot(10, 2), slot(16, 2)
                c = step
                if c < NC:
                    cc = slice(c * CH, (c + 1) * CH)
                    if c == 0:
                        pe.wait_ge(mp_ev, 13)
                    else:
                        pe.wait_ge(mc_w, c)
                        pe.wait_ge(mc_s, c)
                        pe.wait_ge(mc_k, c)
                    pe.matmul(pj[:, 0, :], ident, mask_d.unsqueeze(1).to_broadcast([P, 4, CH]), start=True, stop=False,
                              skip_group_check=True)
                    for i in range(4):
                        head = 2 * (i % 2) + i // 2
                        last = pe.matmul(pj[:, 0, i * CH:(i + 1) * CH], ident[0:4, head:head + 1].to_broadcast([4, P]),
                                         slot(8)[0:4, cc], start=False, stop=(i == 3), skip_group_check=True)
                    last.then_inc(mc_t, 1)
                    for j in range(2):
                        for hh in range(2):
                            r = slice(64 * hh, 64 * hh + 64)
                            last = pe.matmul(pj[:, 1 + hh, j * CH:(j + 1) * CH], k[r, j, cc], q[r, j, cc],
                                             start=True, stop=True)
                    last.then_inc(mc_t, 1)
                    if c == 0:
                        gnorm(0, 11)
                        pe.wait_ge(mix_ev, 36)
                    for j in range(2):
                        last = pe.transpose(pm[:, 2, j * P:(j + 1) * P], k[:, j, cc], ident)
                    last.then_inc(mc_tt, 1)
                c = step - 1
                if c < 0:
                    return
                a, b = mc_att[c % 2], c % 2
                pe.wait_ge(mc_q, c + 1)
                pe.wait_ge(mc_s, c + 1)
                if c >= 1:
                    pe.wait_ge(mc_sv, c)
                if c >= 2:
                    pe.wait_ge(mc_h, c - 1)
                for n in range(2):
                    for j in range(2):
                        at = (2 * n + j) * CH
                        pe.matmul(pm[:, b, at:at + CH], mc_st[:, j, n, :], mc_qe[c % 2][:, j, :], start=True, stop=False,
                                  skip_group_check=True)
                        for hh in range(2):
                            v0 = 384 + (2 * j + hh) * 64
                            lhs = ones[:, 0:64] if n else vt[:, c, v0:v0 + 64]
                            last = pe.matmul(pm[64 * hh:64 * hh + 64, b, at:at + CH], lhs, a[:, 2 * hh + j, :],
                                             start=False, stop=(hh == 1), skip_group_check=True)
                last.then_inc(mc_nt, 1)
                pe.wait_ge(mc_k, c + 1)
                for j in range(2):
                    pe.matmul(pm[:, 3, 2 * j * P:(2 * j + 1) * P], mc_kt[c % 2][:, j, :],
                              vt[:, c, 384 + j * P:384 + (j + 1) * P], start=True, stop=True)
                    last = pe.matmul(pm[:, 3, (2 * j + 1) * P:(2 * j + 2) * P], mc_kt[c % 2][:, j, :], ones,
                                     start=True, stop=True)
                last.then_inc(mc_nt, 1)
                if 3 <= step < 8:
                    msample(step - 3)

            def msample(piece):
                pe.wait_ge(ss_v, 6 + piece)
                if piece == 4:
                    for j in range(2):
                        last = pe.matmul(pm[:, 4, 384 + j * 8:392 + j * 8], blk, tiny[:, 16 + j * 8:24 + j * 8],
                                         start=True, stop=True)
                else:
                    last = pe.matmul(pm[:, 4, :], blk, sm_half(piece // 2), start=True, stop=True)
                last.then_inc(ss_t, 1)

            steps = dict(job=job, rows=rows, conv=lambda _: None, gate=gate, lru=lambda _: None, rope=rope,
                         vt=vtrans, attn=attn, sattn=sattn, hprep=lambda _: None, hdiag=hdiag, hchunk=hchunk, hsample=hsample,
                         hnorm=lambda _: None, mprep=mprep, mchunk=mchunk, msample=lambda _: None,
                         mnorm=lambda _: None)

            def norm_2():
                pe.wait_ge(mix_ev, 42)
                norm(n2, KT)

            def ff_step(i, first=False):
                U0 = N_WIN + N_OUT
                for q in range(4):
                    pe.wait_ge(lo_made, i * 8 + (U0 + q + 1))
                    unit((U0 + q) % 2, 0, KT, m_hi, m_lo, 0,
                         (lambda k: pe.wait_ge(m_l, k + 1)) if first and q == 0 else None,
                         tail=1 if first and q == 0 else 0, vals=i * 12 + (U0 + q),
                         between=(1, norm_2) if first and q == 0 else None)
                for q in range(4, 8):
                    pe.wait_ge(lo_made, i * 8 + (U0 + q + 1))
                    for m in range(2):
                        unit((U0 + q) % 2, 4 * m, 4, hid_hi, hid_lo, 0,
                             (lambda k: pe.wait_ge(ff_l, i * 3 + (k + 1)) if k < 3 else
                              pe.wait_ge(ff_l3, i + 1)) if q == 4 and m == 0 else None,
                             tail=1 if q == 4 and m == 0 else 0,
                             vals=i * 12 + (U0 + 4 + (q - 4) * 2 + m))

            pe.wait_ge(cst_ld, 64)
            norm(n0)
            pe.wait_ge(n0[3], 2)
            with pe.Fori(0, LAYERS) as l:
                for what, i in ORDER:
                    steps[what](i)
                for j in range(N_WIN, N_WIN + N_OUT):
                    pe.wait_ge(lo_made, j + 1)
                    if j == N_WIN:
                        pe.wait_ge(mc_w, NC)
                        pe.wait_ge(mc_s, NC)
                        unit(j % 2, 0, KT, n_hi, n_lo, j,
                             lambda k: pe.wait_ge(*((y_lo, k + 1) if k < 7 else (y_lo7, 1))), tail=2,
                             between=(2, lambda: gnorm(1, 13)))
                    else:
                        unit(j % 2, 0, KT, n_hi, n_lo, j)
                ff_step(0, True)
                with pe.Fori(1, FF_STEPS) as i:
                    ff_step(i)
                u = N_WIN + N_OUT + 12 * FF_STEPS
                j = N_WIN + N_OUT + N_FF
                for half in range(2):
                    pe.wait_ge(lo_made, j + 1)
                    for m in range(4):
                        unit(j % 2, 2 * m, 2, ple_hi, ple_lo, u,
                             (lambda k: pe.wait_ge(pl, k + 1)) if half == 0 and m == 0 else None)
                        u += 1
                    j += 1
                    for m in range(4):
                        pe.wait_ge(lo_made, j + 1)
                        unit(j % 2, 0, KT, m_hi, m_lo, u,
                             (lambda k: pe.wait_ge(r_l, k + 1)) if half == 0 and m == 0 else None)
                        u += 1
                        j += 1
                norm(n1)
                layer_end(pe)


        @block.scalar
        def _(act):
            link = linker(act, ch_a)

            def split_hi(j, done=None):
                if j >= 2:
                    act.wait_ge(w_ld[j % 2], 16 * (j // 2))
                if done:
                    act.wait_ge(mm[2], done)
                act.activation(w_hi[:, j % 2, :], w_raw[:, j % 2, :], ACT.Copy).then_inc(hi_made, 1)

            def take(dst, func, n, rows=slice(0, P), out_rows=None, **kw):
                for t in range(3):
                    act.wait_ge(mm[t], n)
                    o = dst[out_rows or rows, t * TT:(t + 1) * TT]
                    act.activation(o, pj[rows, t, 0:TT], func, **kw).then_inc(ev[t], 1)

            def lam():
                link(act.activation(tiny[:, 0:2], pc('lam', 0, 2), ACT.Abs))
                act.activation(tiny[:, 2:4], tiny[:, 0:2], ACT.Exp, scale=-1.0).then_inc(lam_a, 1)
                act.wait_ge(lam_v, 1)
                act.activation(tiny[:, 16:20], tiny[:, 12:16], ACT.Exp).then_inc(lam_a, 1)
                act.wait_ge(lam_v, 2)
                act.activation(tiny[:, 6:8], tiny[:, 4:6], ACT.Ln).then_inc(lam_a, 1)

            def square(sems, k):
                if k >= 2:
                    act.wait_ge(sems[1], k - 1)
                act.activation(sqr if k else nrm, res[:, k, :], ACT.Square).then_inc(sems[0], 1)

            def first_hi():
                act.activation(w_hi[:, 0, :], w_raw[:, 0, :], ACT.Copy).then_inc(w0_hi, 1)

            def factor(sems):
                act.activation(warm[:], ones[:, 0:1], ACT.Ln)
                for t in range(3):
                    act.wait_ge(sems[2], t + 1)
                    last = act.activation(nrm[:, t * TT:(t + 1) * TT], pm[:, t, 0:TT], ACT.Ln, bias=EPS, scale=1.0 / D)
                last.then_inc(sems[3], 1)
                act.wait_ge(sems[3], 1)
                act.activation(nrm, nrm, ACT.Exp, scale=-0.5).then_inc(sems[3], 1)

            def operand(n):
                act.wait_ge(ev[2], N_WIN + n + 1)
                act.activation(m_hi[:, n, :], res[:, n, :], ACT.Identity, scale=pc('g2', n)).then_inc(m_h, 1)
                square(n2, n)

            kind = dict(cq0=ACT.Silu, cq1=ACT.Silu, cg0=ACT.Silu, cg1=ACT.Silu, cf0=ACT.Sigmoid, cf1=ACT.Sigmoid,
                        do0=ACT.Sigmoid, do1=ACT.Sigmoid)

            def job(j):
                name = WIN[j]
                split_hi(j + 1, j if j >= 1 else None)
                if name == 'gates':
                    for t in range(3):
                        act.wait_ge(mm[t], 1)
                        act.activation(slot(8)[0:4, t * TT:(t + 1) * TT], pj[0:4, t, 0:TT], ACT.Copy)
                        act.activation(slot(9)[0:4, t * TT:(t + 1) * TT], pj[32:36, t, 0:TT],
                                       ACT.Copy).then_inc(ev[t], 1)
                    return
                if name in ('ci0', 'ci1'):
                    act.wait_ge(rope_v, 6)
                if name in ('dv0', 'dv1', 'dq0', 'dq1'):
                    act.wait_ge(lru_v, 2)
                    act.wait_ge(rope_v, 6)
                if name in ('cq0', 'cf0'):
                    act.wait_ge(sa_v, 4)
                    act.wait_ge(sa_t, 4)
                if name == 'cg1':
                    act.wait_ge(sm_t, 2)
                if name == 'cg0':
                    act.wait_ge(mix_st, 16)
                if name == 'dk0':
                    act.wait_ge(kv_st, 32)
                    act.wait_ge(sa_v, 4)
                if name == 'do0':
                    act.wait_ge(vt_c, 6)
                kw = dict(scale=0.125) if name in ('dk0', 'dk1') else {}
                take(slot(SLOT[name]), kind.get(name, ACT.Copy), j + 1, **kw)
                if name in ('ci0', 'ci1', 'dv0', 'dv1'):
                    act.wait_ge(ev[2], j + 1)
                    i = ('ci0', 'ci1', 'dv0', 'dv1').index(name)
                    act.activation(v_smp[:, i, :], slot(SLOT[name])[:, S0:T], ACT.Copy).then_inc(hp_a, 1)

            def rows(i):
                z = slot(9)[0:4, :]
                if i == 0:
                    act.wait_ge(rows_v, 1)
                    link(act.activation(slot(2)[0:4, :], z, ACT.Abs))
                    act.activation(slot(2)[0:4, :], slot(2)[0:4, :], ACT.Exp, scale=-1.0).then_inc(rows_a, 1)
                elif i == 1:
                    act.wait_ge(rows_v, 2)
                    act.activation(slot(5)[0:4, :], slot(3)[0:4, :], ACT.Ln).then_inc(rows_a, 1)
                elif i == 2:
                    act.wait_ge(rows_v, 5)
                    act.activation(slot(6)[32:36, 0:SEQ], slot(2)[0:4, 0:SEQ], ACT.Exp).then_inc(rows_a, 1)
                    act.activation(slot(8)[64:68, :], slot(9)[0:4, :], ACT.Exp).then_inc(rows_a, 1)
                    act.activation(slot(8)[32:36, :], slot(5)[0:4, :], ACT.Exp, scale=-1.0).then_inc(rows_a, 1)
                    act.activation(slot(8)[0:4, S0:T], slot(8)[0:4, S0:T], ACT.Exp).then_inc(rows_a, 1)
                else:
                    act.wait_ge(rows_t, 1)
                    act.activation(bw[:, :, 0, :], pm[:, 3, 0:64].rearrange("p (c e) -> p c e", c=NC)[:, :, 0:4],
                                   ACT.Copy).then_inc(rows_c, 1)
                    act.activation(bw[:, :, 1, :], pm[:, 4, 0:64].rearrange("p (c e) -> p c e", c=NC)[:, :, 0:4],
                                   ACT.Copy).then_inc(rows_c, 1)

            def take_mix(n, dst, func, **kw):
                for t in range(3):
                    act.wait_ge(mix_mm, 3 * (n - 1) + t + 1)
                    act.activation(dst[:, t * TT:(t + 1) * TT], pm[:, t, 0:TT], func, **kw).then_inc(mix_ev, 1)

            def gate(_):
                act.wait_ge(mix_ev, 18)
                for n in range(4):
                    take_mix(7 + n, slot(2 + n), ACT.Sigmoid, bias=pc('br' if n < 2 else 'bi', n % 2))
                act.wait_ge(mix_ev, 30)
                act.wait_ge(lam_v, 3)
                for j in range(2):
                    act.activation(slot(6 + j), slot(2 + j), ACT.Tanh, scale=tiny[:, 10 + j:11 + j]).then_inc(lru_a, 1)
                act.wait_ge(lru_a, 2)
                for j in range(2):
                    act.activation(slot(2 + j), slot(2 + j), ACT.Exp, scale=tiny[:, 44 + j:45 + j]).then_inc(lru_a, 1)
                for j in range(2):
                    act.activation(slot(6 + j), slot(6 + j), ACT.Sqrt).then_inc(lru_a, 1)

            def lru(_):
                act.wait_ge(ev[2], JOB['ag1'] + 1)
                for j in range(2):
                    act.activation(slot(12 + j), slot(12 + j), ACT.Gelu_apprx_tanh).then_inc(lru_a, 1)

            def rope(part):
                if part:
                    return
                act.wait_ge(ev[2], JOB['k'] + 1)
                for n in range(3):
                    act.activation(rp_sq[n], slot(14 + n), ACT.Square).then_inc(rope_a, 1)
                for n in range(3):
                    take_mix(1 + n, rp_rs[n], ACT.Ln, bias=EPS, scale=1.0 / 64)
                act.wait_ge(mix_ev, 9)
                for n in range(3):
                    act.activation(rp_rs[n], rp_rs[n], ACT.Exp, scale=-0.5).then_inc(rope_r, 1)

            def vtrans(v):
                col = VT_COL[list(VT_COL)[v]]
                if v == 0:
                    act.wait_ge(rope_v, 6)
                for h in range(2):
                    act.wait_ge(vt_t, 2 * v + h + 1)
                    act.activation(vt[:, 4 * h:4 * h + 4, col:col + P],
                                   pm[:, 4, :].rearrange("p (c d) -> p c d", c=4), ACT.Copy).then_inc(vt_c, 1)

            vt_next = {i for (what, i), (after, _) in zip(ORDER, ORDER[1:]) if what == 'attn' and after == 'vt'}

            def attn(step):
                if step == 0:
                    act.wait_ge(rope_v, 6)
                    act.dma_start(kv_out[l][:, 0, :], slot(16)[:, SEQ - CH:SEQ]).then_inc(kv_st, 16)
                    act.wait_ge(ev[2], JOB['bv'] + 1)
                    act.dma_start(kv_out[l][:, 1, :], slot(17)[:, SEQ - CH:SEQ]).then_inc(kv_st, 16)
                    act.wait_ge(lru_v, 2)
                    kc = flat(6)[:, 0:1024].rearrange("p (b s) -> p b s", b=DEC)
                    vc = flat(7)[:, 0:1024].rearrange("p (b d) -> p b d", b=DEC)
                    act.dma_start(kc[:, :, 1:P], kc_in[l]).then_inc(smp_ld, 16)
                    act.dma_start(vc[1:P, :, :], vc_in[l]).then_inc(smp_ld, 16)

                def exponentials(c):
                    if c < NC:
                        sc = flat(c % 2)[:, 0:1024].rearrange("p (i s) -> p i s", i=4)
                        lo_k, b = (0 if c else CH), 12 * (c % 2)
                        act.wait_ge(at_m, c + 1)
                        for i in range(4):
                            act.activation(sc[:, i, lo_k:], sc[:, i, lo_k:], ACT.Exp, bias=tiny[:, b + i:b + i + 1],
                                           accum_out=tiny[:, b + 4 + i:b + 5 + i])
                        act.activation(tiny[:, b + 8:b + 12], tiny[:, b + 8:b + 12], ACT.Exp).then_inc(at_e, 1)

                def output(c):
                    if c >= 0:
                        act.wait_ge(at_w, c + 1)
                        act.activation(slot(14, 2)[:, :, c * CH:(c + 1) * CH],
                                       pm[:, 4, 0:256].rearrange("p (j t) -> p j t", j=2), ACT.Copy).then_inc(at_o, 1)

                if step in vt_next:
                    output(step - 2)
                    exponentials(step)
                else:
                    exponentials(step)
                    output(step - 2)
                c = step - 1
                if 0 <= c < NC:
                    act.wait_ge(at_t, c + 1)
                    pt = flat(2 + c % 2)[:, 0:1024]
                    if c:
                        act.activation(pt.rearrange("p (a s) -> p a s", a=2), pm[:, 2:4, :],
                                       ACT.Copy).then_inc(at_c, 1)
                    else:
                        act.activation(pt.rearrange("p (i h t) -> p i h t", i=4, h=2)[:, :, 1, :],
                                       pm[:, 2:4, :].rearrange("p a (i h t) -> p (a i) h t", i=2, h=2)[:, :, 1, :],
                                       ACT.Copy).then_inc(at_c, 1)

            def sattn(part):
                vc = flat(7)[:, 0:1024].rearrange("p (b d) -> p b d", b=DEC)
                if part == 0:
                    act.wait_ge(sa_t, 1)
                    act.activation(vc[0:1, :, :].rearrange("p (a b) d -> p a (b d)", a=2), pm[0:1, 0:2, :],
                                   ACT.Copy).then_inc(sa_a, 1)
                    act.wait_ge(sa_x, 1)
                    act.activation(flat(2)[0:4, 0:1024], flat(2)[0:4, 0:1024], ACT.Exp).then_inc(sa_a, 1)
                    act.activation(tiny[0:4, 8:16], tiny[0:4, 8:16], ACT.Exp).then_inc(sa_a, 1)
                elif part == 2:
                    act.wait_ge(sa_t, 2)
                    act.wait_ge(sa_a, 1)
                    act.dma_start(kc_out[l], flat(6)[:, 0:1024].rearrange("p (b s) -> p b s", b=DEC)).then_inc(smp_st, 16)
                    act.dma_start(vc_out[l], vc).then_inc(smp_st, 16)

            def hprep(_):
                act.wait_ge(hp_v, 1)
                for j in range(2):
                    act.activation(slot(2 + j), slot(2 + j), ACT.Ln).then_inc(hp_a, 1)

            def hdiag(_):
                act.wait_ge(sm_t, 2)
                act.activation(same[:], pm[:, 4, 0:4 * NC].rearrange("p (j c h) -> p j c h", j=2, c=NC),
                               ACT.Copy).then_inc(sm_c, 1)

            def hexp(c):
                for g in range(3):
                    act.wait_ge(hc_sub, 3 * c + g + 1)
                    act.wait_ge(hc_subk, 3 * c + g + 1)
                    if g == 0:
                        last = act.activation(early[:, 0:4, :], early[:, 0:4, :], ACT.Exp)
                    elif g == 1:
                        act.activation(early[:, 4:8, :], early[:, 4:8, :], ACT.Exp)
                        act.activation(level(4), level(4), ACT.Exp)
                        last = act.activation(level(5), level(5), ACT.Exp)
                    else:
                        act.activation(level(6), level(6), ACT.Exp)
                        last = act.activation(ex2[:], ex2[:], ACT.Exp)
                    last.then_inc(hc_exp, 1)

            def hchunk(c):
                if c == 0:
                    hexp(0)
                act.wait_ge(hc_tt, c + 1)
                act.activation(ktok[:], pm[:, 4, 0:256].rearrange("p (j t) -> p j t", j=2), ACT.Copy).then_inc(hc_tc, 1)
                if c + 1 < NC:
                    hexp(c + 1)
                act.wait_ge(hc_ot, 2 * c + 1)
                act.activation(slot(0, 2)[:, :, c * CH:(c + 1) * CH],
                               pm[:, 2, 0:256].rearrange("p (j t) -> p j t", j=2), ACT.Copy).then_inc(hc_oc, 1)

            def hsample(part):
                if part == 0:
                    act.wait_ge(smp_st, 32)
                    act.dma_start(flat(6)[:, 0:1024], hs_in[l]).then_inc(st_ld, 16)
                    act.wait_ge(hp_a, 6)
                    act.activation(tiny[:, 0:16].rearrange("p (j b) -> p j b", j=2), slot(2, 2)[:, :, S0:T],
                                   ACT.Exp).then_inc(ss_a, 1)
                else:
                    act.wait_ge(ss_v, 5)
                    act.dma_start(hs_out[l], flat(6)[:, 0:1024]).then_inc(mix_st, 16)

            def y_split(ks):
                for k in ks:
                    act.activation(n_hi[:, k, :], slot(Y_SLOT[k]), ACT.Copy).then_inc(y_hi, 1)

            def squares(g, o):
                act.wait_ge(ss_v, 5 if g == 0 else 11)
                act.wait_ge(hc_oc, NC)
                for j in range(2):
                    act.activation(slot(2 + j), slot(o + j), ACT.Square).then_inc(nm_a, 1)

            def gnorm(g, n0):
                for j in range(2):
                    take_mix(n0 + j, slot(4 + j), ACT.Ln, bias=EPS, scale=1.0 / 64)
                act.wait_ge(mix_ev, 3 * (n0 + 1))
                for j in range(2):
                    act.activation(slot(4 + j), slot(4 + j), ACT.Exp, scale=-0.5).then_inc(nm_r, 1)

            def hnorm(part):
                if part == 0:
                    act.wait_ge(hc_sv, NC)
                    act.dma_start(hp_out[l], h_st[:]).then_inc(mix_st, 16)
                    squares(0, 0)

            def mprep(n):
                if n == 0:
                    act.wait_ge(mm[2], N_WIN)
                for t in range(3):
                    act.wait_ge(mp_mm, 3 * n + t + 1)
                    act.activation((inter if n < 2 else em)[:, n % 2, t * TT:(t + 1) * TT], pj[:, t, 0:TT],
                                   ACT.Copy).then_inc(mp_ev, 1)
                if n == 3:
                    act.wait_ge(mp_mm, 13)
                    act.activation(tiny[:, 0:16], pj[:, 0, 0:16], ACT.Copy).then_inc(mp_ev, 1)

            def mchunk(step):
                w = ex2[:].rearrange("p a j t -> p (a j) t")
                c = step
                if c < NC:
                    act.wait_ge(mc_t, 2 * c + 1)
                    if c:
                        act.wait_ge(mc_s, c)
                    for i in range(4):
                        head = 2 * (i % 2) + i // 2
                        last = act.activation(w[:, i, :], pj[:, 0, i * CH:(i + 1) * CH], ACT.Exp,
                                              bias=bw[:, c, 0, head:head + 1])
                    last.then_inc(mc_w, 1)
                if step == 0:
                    gnorm(0, 11)
                if step == 2:
                    act.wait_ge(nm_v, 1)
                    act.dma_start(flat(6)[:, 0:1024], cs_in[l]).then_inc(st_ld, 16)
                c = step - 1
                if c >= 0:
                    act.wait_ge(mc_nt, 2 * c + 1)
                    if c:
                        act.wait_ge(mc_h, c)
                    act.activation(early[:, 0:2, :], pm[:, c % 2, 256:512].rearrange("p (j t) -> p j t", j=2),
                                   ACT.Abs).then_inc(mc_d, 1)
                    if 2 <= step < 8:
                        y_split([step - 2])

            def msample(_):
                act.wait_ge(ss_t, 9)
                act.activation(tiny[:, 32:48], pm[:, 4, 384:400], ACT.Abs).then_inc(ss_a, 1)
                act.dma_start(cs_out[l], flat(6)[:, 0:1024]).then_inc(mix_st, 16)
                act.wait_ge(mc_sv, NC)
                act.dma_start(cp_out[l], mc_st[:, :, 0, :]).then_inc(mix_st, 16)

            def mnorm(_):
                squares(1, 10)
                gnorm(1, 13)

            steps = dict(job=job, rows=rows, conv=lambda _: None, gate=gate, lru=lru, rope=rope,
                         vt=vtrans, attn=attn, sattn=sattn, hprep=hprep, hdiag=hdiag, hchunk=hchunk, hsample=hsample,
                         hnorm=hnorm, mprep=mprep, mchunk=mchunk, msample=msample, mnorm=mnorm)
            def ff_step(i, first=False, last=False):
                U0 = N_WIN + N_OUT
                for q in range(8):
                    j = U0 + q + 1
                    done = U0 + (q if q < 5 else 4 + (q - 4) * 2)
                    act.wait_ge(w_ld[j % 2], (i * 4 + j // 2) * 16)
                    act.wait_ge(mm[2], i * 12 + done)
                    act.activation(w_hi[:, j % 2, :], w_raw[:, j % 2, :], ACT.Copy).then_inc(hi_made, 1)
                    if first and q == 0:
                        factor(n2)
                    if q < 4:
                        for t in range(3):
                            act.wait_ge(ev[t], i * 12 + (U0 + q + 1))
                        if q >= 2:
                            act.wait_ge(ff_l, i * 3 + (q - 1))
                        act.activation(hid_hi[:, q, :], relu[:, q % 2, :], ACT.Square)
                        act.activation(hsq[:, q % 2, :], relu[:, q % 2, :], ACT.Square).then_inc(ff_h, 1)
                    elif last:
                        if q == 4:
                            act.wait_ge(ff_l, 3 * FF_STEPS)
                            act.wait_ge(ff_l3, FF_STEPS)
                            act.dma_start(ple_raw[:], p_in[l_now[0]]).then_inc(ple_ld, 16)
                        else:
                            for n in (2 * q - 10, 2 * q - 9):
                                residual(n)
                        if q == 5:
                            act.wait_ge(ple_ld, 16)
                            for k in range(2):
                                act.activation(ple_hi[:, k, :], ple_raw[:, k, :], ACT.Copy).then_inc(ph, 1)

            def residual(n):
                act.wait_ge(ev[2], N_WIN + N_OUT + 12 * FF_STEPS - KT + n + 1)
                act.activation(m_hi[:, n, :], res[:, n, :], ACT.Copy).then_inc(r_h, 1)

            for k in range(KT):
                if k % 2 == 0:
                    act.wait_ge(x_ld[k // 2], 16)
                square(n0, k)
            act.wait_ge(cst_ld, 64)
            first_hi()
            factor(n0)
            l_now = [None]
            with act.Fori(0, LAYERS) as l:
                l_now[0] = l
                act.sem_inc(hi_made, 1)
                for k in range(KT):
                    act.wait_ge(nrm_n, k + 1)
                    act.activation(n_hi[:, k, :], ext[:, 3 + k % 3, :], ACT.Copy).then_inc(nrm_hi, 1)
                lam()
                act.wait_ge(y_st, (l + 1) * (16 * KT))
                for what, i in ORDER:
                    steps[what](i)
                act.wait_ge(y_lo, 6)
                act.dma_start(res[:, 0:2, :], y_out[l][:, 0:2, :]).then_inc(h_ld[0], 16)
                for k in (6, 7):
                    act.wait_ge(nm_v, k - 4)
                    y_split([k])
                act.wait_ge(mix_st, 64)
                act.dma_start(res[:, 2:KT, :], y_out[l][:, 2:KT, :]).then_inc(h_ld[1], 16)
                act.dma_start(so_out[l], so[:]).then_inc(so_st, 16)
                for j in range(N_WIN, N_WIN + N_OUT):
                    split_hi(j + 1, j)
                    if j == N_WIN:
                        act.wait_ge(y_lo, 7)
                        act.wait_ge(y_lo7, 1)
                    else:
                        operand(j - 1 - N_WIN)
                operand(KT - 1)
                ff_step(0, True)
                with act.Fori(1, FF_STEPS - 1) as i:
                    ff_step(i)
                ff_step(FF_STEPS - 1, last=True)
                residual(KT - 2)
                residual(KT - 1)
                u = N_WIN + N_OUT + 12 * FF_STEPS
                j = N_WIN + N_OUT + N_FF

                def finished(n):
                    square(n1, n)
                    act.dma_start(y_out[l + 1][:, n, :], res[:, n, :]).then_inc(y_st, 16)

                for half in range(2):
                    split_hi(j + 1, u)
                    for m in range(4):
                        if half:
                            act.wait_ge(pv, 4 * half)
                        u += 1
                        take(ple_proj[:, m, :], ACT.Copy, u)
                    j += 1
                    for m in range(4):
                        if j + 1 < N_JOBS:
                            split_hi(j + 1, u)
                        u += 1
                        if 4 * half + m:
                            act.wait_ge(pv, 4 * half + m)
                        take(ple_sig, ACT.Sigmoid, u)
                        if 4 * half + m:
                            finished(4 * half + m - 1)
                        j += 1
                act.wait_ge(pv, KT)
                finished(KT - 1)
                act.wait_ge(w_nx, 32)
                first_hi()
                factor(n1)
                act.wait_ge(so_st, 16)
                layer_end(act)

        @block.gpsimd
        def _(pool):
            def split_lo(j, done=None):
                pool.wait_ge(hi_made, j + 1)
                if done:
                    pool.wait_ge(mm[2], done)
                pool.tensor_tensor(w_lo[:, j % 2, :], w_raw[:, j % 2, :], w_hi[:, j % 2, :].bitcast(F32),
                                   ALU.subtract).then_inc(lo_made, 1)

            def hsub(c):
                cc = slice(c * CH, (c + 1) * CH)
                b = slot(2, 2)[:, :, cc]
                if c == 0:
                    pool.wait_ge(hp_v, 2)
                    pool.wait_ge(sa_t, 4)
                for g, levels in enumerate(GROUPS):
                    if c:
                        pool.wait_ge(hc_lt, 3 * (c - 1) + g + 1)
                    for lev in levels:
                        b0, e0 = halves(b, lev)[0], halves(level(lev), lev)[0]
                        n, half = CH >> (lev + 1), 1 << lev
                        ref = b0[:, :, :, half - 1:half].to_broadcast([P, 2, n, half])
                        last = pool.tensor_tensor(e0, ref, b0, ALU.subtract)
                    if g == 2:
                        if c:
                            pool.wait_ge(hc_tt, c)
                        last = pool.tensor_tensor(ex2[:, 1], b[:, :, CH - 1:CH].to_broadcast([P, 2, CH]), b, ALU.subtract)
                    last.then_inc(hc_subk, 1)

            def hmul(c):
                k = slot(4, 2)[:, :, c * CH:(c + 1) * CH]
                for g, levels in enumerate(GROUPS):
                    pool.wait_ge(hc_exp, 3 * c + g + 1)
                    for lev in levels:
                        e0 = halves(level(lev), lev)[0]
                        last = pool.tensor_tensor(e0, e0, halves(k, lev)[0], ALU.mult)
                    if g == 2:
                        last = pool.tensor_tensor(ex2[:, 1], ex2[:, 1], k, ALU.mult)
                    last.then_inc(hc_kk, 1)

            def decayed(c):
                if c >= 2:
                    pool.wait_ge(mc_nt, 2 * (c - 1))
                cc = slice(c * CH, (c + 1) * CH)
                pool.tensor_tensor(mc_qe[c % 2], slot(10, 2)[:, :, cc], inter[:, :, cc], ALU.mult).then_inc(mc_q, 1)

            def y_low(k):
                pool.wait_ge(y_hi, k + 1)
                pool.tensor_tensor(n_lo[:, k, :], slot(Y_SLOT[k]), n_hi[:, k, :].bitcast(F32),
                                   ALU.subtract).then_inc(y_lo, 1)

            def ff_step(i, last=False):
                for q in range(8):
                    j = N_WIN + N_OUT + q + 1
                    done = N_WIN + N_OUT + (q if q < 5 else 4 + (q - 4) * 2)
                    pool.wait_ge(hi_made, i * 8 + (j + 1))
                    pool.wait_ge(mm[2], i * 12 + done)
                    pool.tensor_tensor(w_lo[:, j % 2, :], w_raw[:, j % 2, :], w_hi[:, j % 2, :].bitcast(F32),
                                       ALU.subtract).then_inc(lo_made, 1)
                    if q < 3:
                        pool.wait_ge(ff_h, i * 4 + (q + 1))
                        pool.tensor_tensor(hid_lo[:, q, :], hsq[:, q % 2, :], hid_hi[:, q, :].bitcast(F32),
                                           ALU.subtract).then_inc(ff_l, 1)
                    if last and q >= 5:
                        for n in (2 * q - 10, 2 * q - 9):
                            residual(n)
                        if q == 5:
                            for k in range(2):
                                pool.wait_ge(ph, k + 1)
                                pool.tensor_tensor(ple_lo[:, k, :], ple_raw[:, k, :], ple_hi[:, k, :].bitcast(F32),
                                                   ALU.subtract).then_inc(pl, 1)

            def residual(n):
                pool.wait_ge(r_h, n + 1)
                pool.tensor_tensor(m_lo[:, n, :], res[:, n, :], m_hi[:, n, :].bitcast(F32), ALU.subtract).then_inc(r_l, 1)

            def first_lo(n):
                pool.wait_ge(w0_hi, n)
                pool.tensor_tensor(w_lo[:, 0, :], w_raw[:, 0, :], w_hi[:, 0, :].bitcast(F32), ALU.subtract)

            first_lo(1)
            with pool.Fori(0, LAYERS) as l:
                pool.wait_ge(hi_made, 1)
                pool.drain().then_inc(lo_made, 1)
                for k in range(KT):
                    if k not in DVE_LO:
                        pool.wait_ge(nrm_hi, k + 1)
                        pool.tensor_tensor(n_lo[:, k, :], ext[:, 3 + k % 3, :], n_hi[:, k, :].bitcast(F32),
                                           ALU.subtract).then_inc(nrm_lo, 1)
                for what, c in ORDER:
                    if what == 'job':
                        split_lo(c + 1, c if c >= 1 else None)
                    if what == 'hprep':
                        hsub(0)
                    if what == 'mchunk':
                        if c == 0:
                            pool.wait_ge(mp_ev, 13)
                            pool.wait_ge(hc_sv, NC)
                            decayed(0)
                        if c + 1 < NC:
                            decayed(c + 1)
                        if 2 <= c < 8:
                            y_low(c - 2)
                    if (what, c) == ('hnorm', 1):
                        for j in range(2):
                            pool.wait_ge(nm_g, j + 1)
                            last = pool.tensor_tensor(slot(j), slot(j), slot(6 + j), ALU.mult)
                        last.then_inc(nm_v, 1)
                    if what == 'hdiag':
                        pool.wait_ge(ss_v, 5)
                        for t in range(3):
                            pool.wait_ge(ev[t], JOB['cq1'] + 1)
                        for j in range(2):
                            if j:
                                pool.wait_ge(sm_t, 1)
                            pool.tensor_tensor(slot(7), slot(j), slot(4 + j), ALU.mult).then_inc(sm_p, 1)
                    if what == 'hchunk':
                        hmul(c)
                        if c + 1 < NC:
                            hsub(c + 1)
                y_low(6)
                for j in range(N_WIN + 1, N_WIN + N_OUT + 1):
                    split_lo(j, j - 1)
                with pool.Fori(0, FF_STEPS - 1) as i:
                    ff_step(i)
                ff_step(FF_STEPS - 1, last=True)
                residual(KT - 2)
                residual(KT - 1)
                u = N_WIN + N_OUT + 12 * FF_STEPS
                j = N_WIN + N_OUT + N_FF
                for half in range(2):
                    split_lo(j + 1, u)
                    u += 4
                    j += 1
                    for m in range(4):
                        if j + 1 < N_JOBS:
                            split_lo(j + 1, u)
                        u += 1
                        j += 1
                first_lo(l + 2)
                layer_end(pool)

        @block.vector
        def _(dve):
            link = linker(dve, ch_v)

            def tt(o, a, b, op):
                return dve.tensor_tensor(o, a, b, op)

            def lam():
                gam2 = tiny[:, 12:16].rearrange("p (l j) -> p l j", l=2)
                link(dve.tensor_reduce(tiny[:, 20:22], pc('gam', 0, 4).rearrange("p (l j) -> p j l", l=2), AX_X, ALU.max))
                tt(gam2, pc('gam', 0, 4).rearrange("p (l j) -> p l j", l=2),
                   tiny[:, 20:22].unsqueeze(1).to_broadcast([P, 2, 2]), ALU.subtract).then_inc(lam_v, 1)
                dve.wait_ge(lam_a, 1)
                dve.tensor_scalar(tiny[:, 4:6], tiny[:, 2:4], 1.0, None, ALU.add).then_inc(lam_v, 1)
                dve.wait_ge(lam_v, 2)
                dve.wait_ge(lam_a, 3)
                link(dve.tensor_scalar(tiny[:, 4:6], tiny[:, 4:6], -1.0, 1e-30, ALU.add, ALU.max))
                link(dve.reciprocal(tiny[:, 4:6], tiny[:, 4:6]))
                link(tt(tiny[:, 4:6], tiny[:, 4:6], tiny[:, 2:4], ALU.mult))
                link(tt(tiny[:, 6:8], tiny[:, 6:8], tiny[:, 4:6], ALU.mult))
                link(dve.tensor_scalar(tiny[:, 8:10], pc('lam', 0, 2), -1.0, 0.0, ALU.mult, ALU.max))
                link(tt(tiny[:, 8:10], tiny[:, 8:10], tiny[:, 6:8], ALU.add))
                link(dve.tensor_scalar(tiny[:, 10:12], tiny[:, 8:10], 4.0, None, ALU.mult))
                link(dve.tensor_scalar(tiny[:, 44:46], tiny[:, 8:10], -8.0, None, ALU.mult))
                link(tt(tiny[:, 20:22], tiny[:, 16:18], tiny[:, 18:20], ALU.add))
                link(dve.reciprocal(tiny[:, 20:22], tiny[:, 20:22]))
                link(tt(tiny[:, 20:22], tiny[:, 20:22], tiny[:, 18:20], ALU.mult))
                link(dve.tensor_scalar(tiny[:, 36:38], tiny[:, 20:22], pc('lm'), None, ALU.mult))
                link(dve.tensor_scalar(tiny[:, 38:40], tiny[:, 36:38], -1.0, 1.0, ALU.mult, ALU.add))
                dve.sem_inc(lam_v, 1)

            def norm_lo(k):
                dve.wait_ge(nrm_hi, k + 1)
                tt(n_lo[:, k, :], ext[:, 3 + k % 3, :], n_hi[:, k, :].bitcast(F32), ALU.subtract).then_inc(nrm_lo_v, 1)

            def add_squares(sems, k):
                if 0 < k < (KT if sems is n2 else KT - 1):
                    dve.wait_ge(sems[0], k + 1)
                    if k >= 2:
                        dve.wait_ge(sems[1], k - 1)
                    tt(nrm, nrm, sqr, ALU.add).then_inc(sems[1], 1)

            def rows(i):
                if i:
                    return
                z, ig = slot(9)[0:4, :], slot(8)[0:4, :]
                t1, t2, ln, f = slot(2)[0:4, :], slot(3)[0:4, :], slot(5)[0:4, :], slot(4)[0:4, :]
                for t in range(3):
                    dve.wait_ge(ev[t], 1)
                dve.wait_ge(y_st, (l_now[0] + 1) * (16 * KT))
                link(dve.memset(so[:], 0.0))
                link(dve.tensor_scalar(ig, ig, pc('ib')[0:4], None, ALU.add))
                dve.tensor_scalar(z, z, pc('fb')[0:4], None, ALU.add).then_inc(rows_v, 1)
                dve.wait_ge(rows_a, 1)
                dve.tensor_scalar(t2, t1, 1.0, None, ALU.add).then_inc(rows_v, 1)
                dve.wait_ge(rows_a, 2)
                link(dve.tensor_scalar(t2, t2, -1.0, 1e-30, ALU.add, ALU.max))
                link(dve.reciprocal(t2, t2))
                link(tt(t2, t2, t1, ALU.mult))
                link(tt(ln, ln, t2, ALU.mult))
                link(dve.scalar_tensor_tensor(z, z, 0.0, ln, ALU.min, ALU.subtract))
                one = flat(7)[0:4, 0:CH]
                link(dve.memset(flat(7)[0:P, 0:CH], 1.0))
                for c in range(NC):
                    last = dve.tensor_tensor_scan(f[:, c * CH:(c + 1) * CH], one, z[:, c * CH:(c + 1) * CH], 0.0,
                                                  ALU.mult, ALU.add)
                link(last)
                m = ln
                link(dve.tensor_tensor_scan(m[:, 0:SEQ], z[:, 0:SEQ], ig[:, 0:SEQ], 0.0, ALU.add, ALU.max))
                link(tt(f[:, SEQ:T], z[:, SEQ:T], pc('m0', 0, 8)[0:4], ALU.add))
                link(tt(m[:, SEQ:T], f[:, SEQ:T], ig[:, SEQ:T], ALU.max))
                link(dve.tensor_copy(oc('mp')[0:4], m[:, SEQ - 1:SEQ]))
                link(dve.tensor_copy(oc('ms', 0, 8)[0:4], m[:, SEQ:T]))
                beta = slot(6)[0:4, :]
                link(tt(beta[:, 0:SEQ], ig[:, 0:SEQ], f[:, 0:SEQ], ALU.subtract))
                link(tt(ig[:, SEQ:T], ig[:, SEQ:T], m[:, SEQ:T], ALU.subtract))
                link(tt(ig[:, 0:SEQ], f[:, 0:SEQ], m[:, 0:SEQ], ALU.subtract))
                link(tt(z[:, SEQ:T], f[:, SEQ:T], m[:, SEQ:T], ALU.subtract))
                a3 = ig[:, 0:SEQ].rearrange("p (c t) -> p c t", c=NC)
                m3 = m[:, 0:SEQ].rearrange("p (c t) -> p c t", c=NC)
                z3 = z[:, 0:SEQ].rearrange("p (c t) -> p c t", c=NC)
                link(dve.tensor_copy(z3[:, 0, :], a3[:, 0, :]))
                link(tt(z3[:, 1:, :], a3[:, 1:, :], m3[:, 0:NC - 1, CH - 1:CH].to_broadcast([4, NC - 1, CH]), ALU.add))
                link(tt(t1[:, 0:SEQ].rearrange("p (c t) -> p c t", c=NC),
                        beta[:, 0:SEQ].rearrange("p (c t) -> p c t", c=NC),
                        a3[:, :, CH - 1:CH].to_broadcast([4, NC, CH]), ALU.add))
                for n in range(3):
                    dve.sem_inc(rows_v, 1)
                dve.wait_ge(rows_a, 6)
                for n in range(4):
                    dve.sem_inc(rows_v, 1)

            def conv(_):
                for t in range(3):
                    dve.wait_ge(ev[t], 3)
                cv = pc('conv', 0, 48).rearrange("p (j w b) -> p j w b", j=2, w=3)
                for j in range(2):
                    x, o = slot(10 + j), slot(j)
                    link(dve.tensor_scalar(o, x, pc('cw', 3 * 2 + j), pc('cb', j), ALU.mult, ALU.add))
                    for w in range(3):
                        s = 3 - w
                        wc = pc('cw', w * 2 + j)
                        link(dve.scalar_tensor_tensor(o[:, s:SEQ], x[:, 0:SEQ - s], wc, o[:, s:SEQ], ALU.mult, ALU.add))
                        link(dve.scalar_tensor_tensor(o[:, S0:T], cv[:, j, w, :], wc, o[:, S0:T], ALU.mult, ALU.add))
                    link(dve.tensor_copy(oc('convp', 3 * j, 3), x[:, SEQ - 3:SEQ]))
                    cs = oc('convs', 24 * j, 24).rearrange("p (w b) -> p w b", w=3)
                    link(dve.tensor_copy(cs[:, 0:2, :], cv[:, j, 1:3, :]))
                    link(dve.tensor_copy(cs[:, 2, :], x[:, S0:T]))
                dve.sem_inc(conv_v, 1)

            def lru(_):
                dve.wait_ge(mix_ev, 30)
                dve.wait_ge(conv_v, 1)
                for j in range(2):
                    tt(slot(4 + j), slot(4 + j), slot(j), ALU.mult)
                for j in range(2):
                    dve.wait_ge(lru_a, 5 + j)
                    link(dve.scalar_tensor_tensor(slot(6 + j), slot(2 + j), 1.0, slot(6 + j), ALU.add, ALU.mult))
                for j in range(2):
                    last = tt(slot(4 + j), slot(4 + j), slot(6 + j), ALU.mult)
                link(last)
                for j in range(2):
                    xc, i, a = slot(j), slot(4 + j), slot(2 + j)
                    dve.tensor_tensor_scan(xc[:, 0:SEQ], a[:, 0:SEQ], i[:, 0:SEQ], 0.0, ALU.mult, ALU.add)
                    link(tt(xc[:, S0:T], a[:, S0:T], pc('h0', 8 * j, 8), ALU.mult))
                    link(tt(xc[:, S0:T], xc[:, S0:T], i[:, S0:T], ALU.add))
                    dve.tensor_copy(oc('hp', j), xc[:, SEQ - 1:SEQ])
                    dve.tensor_copy(oc('hs', 8 * j, 8), xc[:, S0:T])
                    dve.wait_ge(lru_a, 7 + j)
                    tt(slot(12 + j), slot(12 + j), xc, ALU.mult).then_inc(lru_v, 1)
                dve.wait_ge(lru_v, 2)

            def rope(part):
                for n in range(3):
                    if part == 0:
                        dve.wait_ge(rope_r, n + 1)
                        dve.scalar_tensor_tensor(slot(14 + n), slot(14 + n), pc('kg' if n == 2 else 'qg'), rp_rs[n],
                                                 ALU.mult, ALU.mult).then_inc(rope_v, 1)
                        continue
                    dve.wait_ge(rope_ld, 16)
                    dve.wait_ge(rope_v, 3 + n)
                    for t in range(3):
                        cols = slice(t * TT, (t + 1) * TT)
                        dve.wait_ge(mix_mm, 3 * (3 + n) + t + 1)
                        tt(rp_sq[n][:, cols], pm[:, t, 0:TT], slot(19)[:, cols], ALU.mult).then_inc(mix_ev, 1)
                    link(tt(slot(14 + n), slot(14 + n), slot(18), ALU.mult))
                    dve.wait_ge(mix_ev, 3 * (4 + n))
                    tt(slot(14 + n), slot(14 + n), rp_sq[n], ALU.add).then_inc(rope_v, 1)

            def attn(step):
                c = step - 1
                if 0 <= c < NC:
                    sc = flat(c % 2)[:, 0:1024].rearrange("p (i s) -> p i s", i=4)
                    lo_k, b = (0 if c else CH), 12 * (c % 2)
                    dve.wait_ge(at_e, c + 1)
                    link(tt(tiny[:, 28:32], tiny[:, b + 4:b + 8], tiny[:, b + 8:b + 12], ALU.add))
                    link(dve.reciprocal(tiny[:, 28:32], tiny[:, 28:32]))
                    tt(sc[:, :, lo_k:], sc[:, :, lo_k:], tiny[:, 28:32].unsqueeze(2).to_broadcast([P, 4, 256 - lo_k]),
                       ALU.mult).then_inc(at_p, 1)
                    dve.wait_ge(at_p, c + 1)
                c = step
                if c < NC:
                    sc = flat(c % 2)[:, 0:1024].rearrange("p (i s) -> p i s", i=4)
                    lo_k, b = (0 if c else CH), 12 * (c % 2)
                    dve.wait_ge(at_s, c + 1)
                    if c >= 2:
                        dve.wait_ge(at_t, c - 1)
                    mask = cst[:, C_MP + lo_k:C_MP + 256].unsqueeze(1).to_broadcast([P, 4, 256 - lo_k])
                    ps = pm[:, 0:2, :].rearrange("p a (j s) -> p (a j) s", j=2)[:, :, lo_k:]
                    link(dve.scalar_tensor_tensor(sc[:, :, lo_k:], ps, 0.125, mask, ALU.mult, ALU.add))
                    mx = tiny[:, 24:28]
                    link(dve.tensor_reduce(mx, sc[:, :, lo_k:], AX_X, ALU.max))
                    link(tt(mx, mx, pc('sink', 0, 4), ALU.max))
                    link(tt(tiny[:, b + 8:b + 12], pc('sink', 0, 4), mx, ALU.subtract))
                    dve.tensor_scalar(tiny[:, b:b + 4], mx, -1.0, None, ALU.mult).then_inc(at_m, 1)
                    dve.wait_ge(at_m, c + 1)

            def sattn(part):
                if part:
                    return
                dve.wait_ge(at_t, NC)
                dve.wait_ge(at_o, NC)
                dve.wait_ge(smp_ld, 32)
                qb = flat(0)[:, 0:32].rearrange("p (b i) -> p b i", b=DEC)
                link(dve.memset(flat(0)[:, 0:32], 0.0))
                for j in range(2):
                    link(dve.tensor_copy(qb[0:64, :, j], slot(14 + j)[0:64, S0:T]))
                    link(dve.tensor_copy(qb[64:P, :, 2 + j], slot(14 + j)[64:P, S0:T]))
                kc = flat(6)[:, 0:1024].rearrange("p (b s) -> p b s", b=DEC)
                dve.tensor_copy(kc[:, :, 0], slot(16)[:, S0:T]).then_inc(sa_v, 1)
                dve.wait_ge(sa_t, 2)
                s = flat(2)[0:4, 0:1024]
                s3 = s.rearrange("p (b s) -> p b s", b=DEC)
                link(dve.tensor_scalar(s.rearrange("p (a s) -> p a s", a=2), pm[0:4, 2:4, :], 0.125, None, ALU.mult))
                mx = tiny[0:4, 0:8]
                link(dve.tensor_reduce(mx, s3, AX_X, ALU.max))
                link(dve.tensor_scalar(mx, mx, pc('sinkc')[0:4], None, ALU.max))
                link(tt(s3, s3, mx.unsqueeze(2).to_broadcast([4, DEC, CH]), ALU.subtract))
                link(dve.tensor_scalar(tiny[0:4, 8:16], mx, -1.0, pc('sinkc')[0:4], ALU.mult, ALU.add))
                dve.sem_inc(sa_x, 1)
                dve.wait_ge(sa_a, 3)
                link(dve.tensor_reduce(mx, s3, AX_X, ALU.add))
                link(tt(mx, mx, tiny[0:4, 8:16], ALU.add))
                link(dve.reciprocal(mx, mx))
                tt(s3, s3, mx.unsqueeze(2).to_broadcast([4, DEC, CH]), ALU.mult).then_inc(sa_v, 1)
                dve.wait_ge(sa_t, 3)
                dve.tensor_copy(flat(3)[:, 0:32], pm[:, 4, 0:32]).then_inc(sa_v, 1)
                dve.wait_ge(sa_t, 4)
                o = pm[:, 4, 64:96].rearrange("p (b i) -> p b i", b=DEC)
                for j in range(2):
                    link(dve.tensor_copy(slot(14 + j)[0:64, S0:T], o[0:64, :, j]))
                    link(dve.tensor_copy(slot(14 + j)[64:P, S0:T], o[64:P, :, 2 + j]))
                dve.sem_inc(sa_v, 1)

            def hprep(_):
                for t in range(3):
                    dve.wait_ge(ev[t], JOB['cf1'] + 1)
                dve.wait_ge(vt_c, 10)
                dve.wait_ge(hp_a, 4)
                for j in range(2):
                    f = slot(2 + j)
                    link(dve.tensor_scalar(f, f, tiny[:, 38 + j:39 + j], tiny[:, 36 + j:37 + j], ALU.mult, ALU.add))
                    link(dve.tensor_scalar(slot(4 + j), f, -1.0, 1.0, ALU.mult, ALU.add))
                link(dve.memset(att[:, 0, :], 1.0))
                link(dve.memset(h_st[:], 0.0))
                dve.wait_ge(rows_a, 6)
                link(dve.memset(slot(9), 0.0))
                dve.sem_inc(hp_v, 1)
                dve.wait_ge(hp_a, 6)
                for j in range(2):
                    f = slot(2 + j)
                    for c in range(NC):
                        cc = slice(c * CH, (c + 1) * CH)
                        last = dve.tensor_tensor_scan(f[:, cc], att[:, 0, :], f[:, cc], 0.0, ALU.mult, ALU.add)
                link(last)
                dve.sem_inc(hp_v, 1)

            def hsub(c, g):
                b = slot(2, 2)[:, :, c * CH:(c + 1) * CH]
                for lev in GROUPS[g]:
                    b0, b1 = halves(b, lev)
                    n, half = CH >> (lev + 1), 1 << lev
                    ref = b0[:, :, :, half - 1:half].to_broadcast([P, 2, n, half])
                    last = tt(halves(level(lev), lev)[1], b1, ref, ALU.subtract)
                if g == 2:
                    last = dve.tensor_copy(ex2[:, 0], b)
                last.then_inc(hc_sub, 1)

            def hchunk(c):
                q = slot(0, 2)[:, :, c * CH:(c + 1) * CH]
                if c == 0:
                    for t in range(3):
                        dve.wait_ge(ev[t], JOB['cq1'] + 1)
                def diagonal(lev, q):
                    for hh in range(2):
                        r = slice(64 * hh, 64 * hh + 64)
                        last = tt(q_diag[r, lev % 4, :, hh, :].rearrange("p j (n b) -> p j n b", b=1 << lev),
                                  halves(level(lev)[r], lev)[1], halves(q[r], lev)[1], ALU.mult)
                    return last

                def first(c):
                    dve.wait_ge(hc_exp, 3 * c + 1)
                    for lev in GROUPS[0]:
                        last = diagonal(lev, slot(0, 2)[:, :, c * CH:(c + 1) * CH])
                    last.then_inc(hc_kq, 1)

                if c == 0:
                    first(0)
                for g, levels in enumerate(GROUPS):
                    if g == 0:
                        continue
                    dve.wait_ge(hc_exp, 3 * c + g + 1)
                    for lev in levels:
                        e1 = halves(level(lev), lev)[1]
                        if lev < 4:
                            last = diagonal(lev, q)
                        elif lev == 6:
                            last = tt(e1, e1, halves(q, lev)[1], ALU.mult)
                    if g == 1:
                        last.then_inc(hc_kq, 1)
                        dve.wait_ge(hc_lt, 3 * c + 1)
                        diagonal(4, q)
                        diagonal(5, q).then_inc(hc_kq2, 1)
                        continue
                    if g == 2:
                        dve.tensor_copy(tiny[:, 40 + 2 * (c % 2):42 + 2 * (c % 2)], ex2[:, 0, :, CH - 1])
                        if c:
                            dve.wait_ge(hc_ot, 2 * c - 1)
                        last = tt(qe[:], ex2[:, 0], q, ALU.mult)
                    last.then_inc(hc_kq, 1)
                dve.wait_ge(hc_kq, 3 * c + 3)
                dve.wait_ge(hc_lt, 3 * c + 1)
                if c:
                    dve.wait_ge(hc_ot, 2 * c - 1)
                if c == 0:
                    dve.wait_ge(sm_c, 1)
                tt(att.rearrange("p (j h) t -> p j h t", j=2), same[:, :, c, :].unsqueeze(3).to_broadcast([P, 2, 2, CH]),
                   ident.unsqueeze(1).unsqueeze(1).to_broadcast([P, 2, 2, CH]), ALU.mult).then_inc(hc_lv, 1)
                for g, levels in enumerate(GROUPS):
                    dve.wait_ge(hc_lt, 3 * c + g + 1)
                    for lev in levels:
                        dve.wait_ge(hc_lv, 8 * c + 1 + lev)
                        half, n = 1 << lev, CH >> (lev + 1)
                        out = att[:].rearrange("p i (n two b) -> p i n two b", two=2, b=half)[:, :, :, 1, :]
                        mk = cst[:, C_LEV + 64 * lev:C_LEV + 64 * lev + 64].bitcast(U32)
                        if lev < 6:
                            mk = mk.rearrange("p (n b) -> p n b", b=half)
                        bank, col = LEV_AT[lev]
                        if lev == 6:
                            out = att.rearrange("p (j h) t -> p j h t", j=2)[:, :, :, half:]
                            dat = pm[:, 0:2, :].rearrange("p h (j s) -> p j h s", j=2)[:, :, :, 0:half]
                            mk = mk.unsqueeze(1).unsqueeze(1).to_broadcast([P, 2, 2, half])
                        else:
                            dat = pm[:, bank:bank + 2, :].rearrange("p a (h s) -> p (a h) s", h=2)[:, :, col:col + 64]
                            dat, mk = dat.rearrange("p i (n b) -> p i n b", b=half), mk.unsqueeze(1).to_broadcast([P, 4, n, half])
                        dve.copy_predicated(out, mk, dat).then_inc(hc_lv, 1)
                    if c + 1 < NC:
                        hsub(c + 1, g)
                if c + 1 < NC:
                    first(c + 1)
                dve.wait_ge(hc_ot, 2 * c + 2)
                for j in range(2):
                    for hh in range(2):
                        r = slice(64 * hh, 64 * hh + 64)
                        last = dve.scalar_tensor_tensor(h_st[r, j, r], h_st[r, j, r],
                                                        tiny[r, 40 + 2 * (c % 2) + j:41 + 2 * (c % 2) + j],
                                                        pm[r, 3, j * P + 64 * hh:j * P + 64 * hh + 64], ALU.mult, ALU.add)
                link(last)
                dve.sem_inc(hc_sv, 1)

            wide = [P, DEC // 2, 2, 64]

            def each(x):
                return x.rearrange("p (c b) -> p c b", b=2).unsqueeze(3).to_broadcast(wide)

            def full(x):
                return x.rearrange("p (c b e) -> p c b e", b=2, e=64)

            eb = eye.unsqueeze(1).unsqueeze(1).to_broadcast(wide)

            def s_values(v):
                tt(full(sm_half(0)), each(v_smp[:, v, :]), eb, ALU.mult).then_inc(ss_v, 1)

            def s_update(j, bank, t, dec, kk):
                st, w1 = full(sm_state(j)), full(sm_half(1))
                dve.wait_ge(ss_t, t)
                link(tt(w1, full(pm[:, bank, :]), each(kk[:, j, :]), ALU.mult))
                link(tt(st, st, each(dec[:, j, :]), ALU.mult))
                link(tt(st, st, w1, ALU.add))

            def s_product(j, q, half):
                tt(full(sm_half(half)), full(sm_state(j)), each(q[:, j, :]), ALU.mult).then_inc(ss_v, 1)

            def s_output(j, bank, t, o, half):
                w = full(sm_half(half))
                dve.wait_ge(ss_t, t)
                link(tt(w, full(pm[:, bank, :]), eb, ALU.mult))
                link(dve.tensor_reduce(o[:, j, :].rearrange("p (c b) -> p c b", b=2), w, AX_X, ALU.add))

            def hsample(part):
                q, k = slot(0, 2)[:, :, S0:T], slot(4, 2)[:, :, S0:T]
                if part == 0:
                    dve.wait_ge(smp_st, 32)
                    s_values(0)
                    dve.wait_ge(ss_t, 1)
                    s_values(1)
                    dve.wait_ge(ss_a, 1)
                    dve.wait_ge(st_ld, 16)
                    for j in range(2):
                        s_update(j, j, j + 1, tiny[:, 0:16].rearrange("p (j b) -> p j b", j=2), k)
                    hsub(0, 0)
                    hsub(0, 1)
                    hsub(0, 2)
                else:
                    for t in range(3):
                        dve.wait_ge(ev[t], JOB['cq1'] + 1)
                    s_product(0, q, 1)
                    s_product(1, q, 0)
                    for j in range(2):
                        s_output(j, 2 + j, 3 + j, q, 1 - j)
                    dve.sem_inc(ss_v, 1)

            def gnorm(g, o, gain, gate0):
                for t in range(3):
                    dve.wait_ge(ev[t], (JOB['cg1'] if g == 0 else JOB['do1']) + 1)
                for j in range(2):
                    dve.wait_ge(nm_r, 2 * g + j + 1)
                    last = dve.scalar_tensor_tensor(slot(o + j), slot(o + j), pc(gain), slot(4 + j), ALU.mult, ALU.mult)
                    if g == 0:
                        last.then_inc(nm_g, 1)
                        continue
                    link(last)
                    tt(slot(o + j), slot(o + j), slot(gate0 + j), ALU.mult).then_inc(nm_v, 1)
                if g:
                    dve.wait_ge(y_hi, KT)
                    tt(n_lo[:, 7, :], slot(Y_SLOT[7]), n_hi[:, 7, :].bitcast(F32), ALU.subtract).then_inc(y_lo7, 1)

            def mchunk(step):
                c = step
                if c < NC:
                    cc = slice(c * CH, (c + 1) * CH)
                    if c == 0:
                        link(dve.memset(mc_st, 0.0))
                    if c >= 2:
                        dve.wait_ge(mc_nt, 2 * (c - 1))
                    dve.wait_ge(mc_t, 2 * c + 2)
                    dve.wait_ge(mc_w, c + 1)
                    tt(mc_att[c % 2].rearrange("p (a j) t -> p a (j t)", a=2), pj[:, 1:3, 0:256],
                       ex2[:].rearrange("p a j t -> p a (j t)"), ALU.mult).then_inc(mc_s, 1)
                    dve.wait_ge(mc_tt, c + 1)
                    tt(mc_kt[c % 2].rearrange("p j (h d) -> p j h d", h=2),
                       pm[:, 2, 0:256].rearrange("p (j h d) -> p j h d", j=2, h=2),
                       bw[:, c, 1, :].rearrange("p (j h) -> p j h", j=2).unsqueeze(3).to_broadcast([P, 2, 2, 64]),
                       ALU.mult).then_inc(mc_k, 1)
                c = step - 1
                if c < 0:
                    return
                cc = slice(c * CH, (c + 1) * CH)
                dve.wait_ge(mc_nt, 2 * c + 2)
                end = (c + 1) * CH - 1
                sums = pm[:, 3, :].rearrange("p (j s e) -> p j s e", j=2, s=2)
                for j in range(2):
                    for hh in range(2):
                        r = slice(64 * hh, 64 * hh + 64)
                        last = dve.scalar_tensor_tensor(mc_st[r, j, :, r], mc_st[r, j, :, r], inter[r, j, end:end + 1],
                                                        sums[r, j, :, r], ALU.mult, ALU.add)
                last.then_inc(mc_sv, 1)
                dve.wait_ge(mc_d, c + 1)
                den = early[:, 0:2, :]
                link(tt(den, den, em[:, :, cc], ALU.max))
                link(dve.reciprocal(den, den))
                tt(slot(10, 2)[:, :, cc], pm[:, c % 2, 0:256].rearrange("p (j t) -> p j t", j=2), den,
                   ALU.mult).then_inc(mc_h, 1)
                msample_part(step)

            def msample_part(step):
                dec, w = inter[:, :, S0:T], tiny[:, 0:16].rearrange("p (j b) -> p j b", j=2)
                q, k = slot(10, 2)[:, :, S0:T], slot(16, 2)[:, :, S0:T]
                if step == 2:
                    link(tt(w, w, k, ALU.mult))
                    ns = oc('ns', 0, 16).rearrange("p (j b) -> p j b", j=2)
                    link(tt(ns, pc('n0', 0, 16).rearrange("p (j b) -> p j b", j=2), dec, ALU.mult))
                    link(tt(ns, ns, w, ALU.add))
                    link(tt(tiny[:, 16:32].rearrange("p (j b) -> p j b", j=2), ns, q, ALU.mult))
                    dve.wait_ge(nm_v, 1)
                    s_values(2)
                elif step == 3:
                    dve.wait_ge(st_ld, 32)
                    s_update(0, 4, 5, dec, w)
                    s_values(3)
                elif step == 4:
                    s_update(1, 4, 6, dec, w)
                    s_product(0, q, 1)
                elif step == 5:
                    s_output(0, 4, 7, q, 1)
                    s_product(1, q, 1)
                elif step == 6:
                    s_output(1, 4, 8, q, 1)
                    dve.sem_inc(ss_v, 1)

            def msample(_):
                q = slot(10, 2)[:, :, S0:T]
                dve.wait_ge(mc_nt, 2 * NC)
                dve.wait_ge(ss_a, 2)
                d = tiny[:, 32:48].rearrange("p (j b) -> p j b", j=2)
                link(tt(d, d, em[:, :, S0:T], ALU.max))
                link(dve.reciprocal(d, d))
                tt(q, q, d, ALU.mult).then_inc(ss_v, 1)
                for j in range(2):
                    for hh in range(2):
                        dve.tensor_copy(oc('np', j)[64 * hh:64 * hh + 64],
                                        mc_st[64 * hh:64 * hh + 64, j, 1, 64 * hh:64 * hh + 1])
                dve.wait_ge(ss_v, 11)

            steps = dict(job=lambda _: None, rows=rows, conv=conv, gate=lambda _: None, lru=lru, rope=rope,
                         vt=lambda _: None, attn=attn, sattn=sattn, hprep=hprep, hdiag=lambda _: None, hchunk=hchunk, hsample=hsample,
                         hnorm=lambda part: gnorm(0, 0, 'hg', None) if part else None, mprep=lambda _: None,
                         mchunk=mchunk, msample=msample, mnorm=lambda _: gnorm(1, 10, 'mg', 18))

            def ff_step(i):
                U0 = N_WIN + N_OUT
                for q in range(4):
                    if q >= 2:
                        dve.wait_ge(ff_h, i * 4 + (q - 1))
                    for t in range(3):
                        cols = slice(t * TT, (t + 1) * TT)
                        dve.wait_ge(mm[t], i * 12 + (U0 + q + 1))
                        dve.scalar_tensor_tensor(relu[:, q % 2, cols], pj[:, t, 0:TT], 0.0, nrm[:, cols],
                                                 ALU.max, ALU.mult).then_inc(ev[t], 1)
                dve.wait_ge(ff_h, i * 4 + 4)
                tt(hid_lo[:, 3, :], hsq[:, 1, :], hid_hi[:, 3, :].bitcast(F32), ALU.subtract).then_inc(ff_l3, 1)
                for n in range(KT):
                    for t in range(3):
                        cols = slice(t * TT, (t + 1) * TT)
                        dve.wait_ge(mm[t], i * 12 + (U0 + 4 + n + 1))
                        tt(res[:, n, cols], res[:, n, cols], pj[:, t, 0:TT], ALU.add).then_inc(ev[t], 1)

            for k in range(KT):
                add_squares(n0, k)
            dve.wait_ge(cst_ld, 64)
            dve.wait_ge(n0[3], 2)
            l_now = [None]
            with dve.Fori(0, LAYERS) as l:
                l_now[0] = l
                for k in range(KT):
                    if k >= 3:
                        dve.wait_ge(*NORM_LO(k - 3))
                    dve.scalar_tensor_tensor(ext[:, 3 + k % 3, :], res[:, k, :], pc('g1', k), nrm,
                                             ALU.mult, ALU.mult).then_inc(nrm_n, 1)
                    if k - 1 in DVE_LO:
                        norm_lo(k - 1)
                if KT - 1 in DVE_LO:
                    norm_lo(KT - 1)
                lam()
                for what, i in ORDER:
                    steps[what](i)
                for n in range(N_OUT):
                    dve.wait_ge(h_ld[0 if n < 2 else 1], 16)
                    for t in range(3):
                        cols = slice(t * TT, (t + 1) * TT)
                        dve.wait_ge(mm[t], N_WIN + n + 1)
                        tt(res[:, n, cols], res[:, n, cols], pj[:, t, 0:TT], ALU.add).then_inc(ev[t], 1)
                    dve.wait_ge(m_h, n + 1)
                    dve.scalar_tensor_tensor(m_lo[:, n, :], res[:, n, :], pc('g2', n), m_hi[:, n, :].bitcast(F32),
                                             ALU.mult, ALU.subtract).then_inc(m_l, 1)
                    add_squares(n2, n)
                dve.wait_ge(n2[3], 2)
                with dve.Fori(0, FF_STEPS) as i:
                    ff_step(i)
                u = N_WIN + N_OUT + 12 * FF_STEPS
                for half in range(2):
                    u += 4
                    for m in range(4):
                        u += 1
                        for t in range(3):
                            cols = slice(t * TT, (t + 1) * TT)
                            dve.wait_ge(ev[t], u)
                            link(tt(ple_sig[:, cols], ple_sig[:, cols], ple_proj[:, m, cols], ALU.mult))
                            last = tt(res[:, 4 * half + m, cols], res[:, 4 * half + m, cols], ple_sig[:, cols], ALU.add)
                        last.then_inc(pv, 1)
                        if 4 * half + m:
                            add_squares(n1, 4 * half + m - 1)
                add_squares(n1, KT - 1)
                layer_end(dve)


def _tiles(w, k0, n):
    K, M = w.shape
    return w.reshape(K // P, P, M // P, P).transpose(1, 2, 0, 3).reshape(P, -1)


def _weights(w_in, w_out, w_up, w_down, w_gate, w_proj):
    W = np.zeros((LAYERS * N_JOBS + 2, P, KT * P), np.float32)
    off = dict(ax=0, ag=256, q=512, k=768, bv=896, cq=1024, cf=1280, ci=1536, cg=1792, dq=2048, dk=2304,
               dv=2560, do=2816, gates=3072)
    h = np.arange(64)
    pair = [np.concatenate([h + 64 * g, h + 128 + 64 * g]) for g in range(2)]
    for l in range(LAYERS):
        for name, j in JOB.items():
            if name == 'gates':
                w = np.zeros((D, P), np.float32)
                w[:, 0:4] = w_in[l][:, 3072:3076]
                w[:, 32:36] = w_in[l][:, 3076:3080]
            elif name in ('q0', 'q1'):
                w = w_in[l][:, 512 + pair[int(name[1])]]
            elif name in off:
                w = w_in[l][:, off[name]:off[name] + P]
            else:
                a = off[name[:-1]] + P * int(name[-1])
                w = w_in[l][:, a:a + P]
            W[l * N_JOBS + j] = _tiles(w, 0, 1)
        rows = np.arange(D)
        rows[256:512] = 256 + np.concatenate(pair)
        for m in range(KT):
            W[l * N_JOBS + N_WIN + m] = _tiles(w_out[l][rows][:, m * P:(m + 1) * P], 0, 1)
        j = N_WIN + N_OUT
        for f in range(FF_STEPS):
            for q in range(4):
                a = (4 * f + q) * P
                W[l * N_JOBS + j] = _tiles(w_up[l][:, a:a + P], 0, 1)
                j += 1
            for q in range(4):
                W[l * N_JOBS + j] = _tiles(w_down[l][f * 512:(f + 1) * 512, q * 256:(q + 1) * 256], 0, 2)
                j += 1
        for half in range(2):
            W[l * N_JOBS + j] = _tiles(w_proj[l][:, half * 512:(half + 1) * 512], 0, 4)
            j += 1
            for m in range(4):
                a = (4 * half + m) * P
                W[l * N_JOBS + j] = _tiles(w_gate[l][:, a:a + P], 0, 1)
                j += 1
    return W


def _cols(x, s):
    a = np.concatenate([x, s], axis=-2)
    a = a.reshape(a.shape[:-1] + (a.shape[-1] // P, P))
    return np.ascontiguousarray(np.moveaxis(a, -3, -1).swapaxes(-3, -2))


def _constants():
    c = np.zeros((P, N_CONST), np.float32)
    p, f = np.arange(P)[:, None], np.arange(P)[None, :]
    c[:, 0:P] = p == f
    c[:, C_ONE:C_ONE + P] = 1.0
    c[:, C_BLK:C_BLK + P] = p // 64 == f // 64
    same = p // 64 == f // 64
    c[:, C_ROT:C_ROT + P] = np.where(same & (f % 64 < 8) & (p == f + 8), -1.0, 0.0) + \
        np.where(same & (f % 64 >= 8) & (f % 64 < 16) & (p == f - 8), 1.0, 0.0)
    c[:, C_MD:C_MD + P] = np.where(p <= f, 0.0, NEG)
    c[:, C_MP:C_MP + P] = np.where(f > p, 0.0, NEG)
    c[:, C_MC:C_MC + P] = np.where(f <= p, 0.0, NEG)
    c[:, C_EYE:C_EYE + 64] = p % 64 == np.arange(64)[None, :]
    for j in range(2):
        c[:, C_SEL + j * P:C_SEL + (j + 1) * P] = p % 32 == 2 * j + f // 64
    for l in range(NLEV):
        b = 1 << l
        t = np.arange(P)[(np.arange(P) // b) % 2 == 1][None, :]
        c[:, C_LEV + 64 * l:C_LEV + 64 * l + 64] = ((p // b) % 2 == 0) & (p // (2 * b) == t // (2 * b))
    return c


def _rope_table():
    inv = np.power(np.float32(500000.0), -np.arange(8, dtype=np.float32) * np.float32(2.0 / 16))
    pos = np.concatenate([np.arange(SEQ), np.full(DEC, 1024)]).astype(np.float32)
    ang = (pos[:, None] * inv[None, :]).astype(np.float32)
    r = np.zeros((P, 2, T), np.float32)
    r[:, 0] = 1.0
    for d in range(P):
        if d % 64 < 16:
            r[d, 0] = np.cos(ang[:, d % 8])
            r[d, 1] = np.sin(ang[:, d % 8])
    return r


def _layout(i):
    L = LAYERS

    def chan(a):
        return a.reshape((L, -1, P) + a.shape[2:]).swapaxes(1, 2)

    par = np.zeros((L + 1, P, N_PAR), np.float32)

    def put(name, a):
        a = a.reshape(L, a.shape[1], -1)
        par[:L, :a.shape[1], PC[name]:PC[name] + a.shape[2]] = a

    put('g1', chan(i['norm1_g']))
    put('g2', chan(i['norm2_g']))
    put('cw', chan(i['conv_w'].transpose(0, 2, 1)).transpose(0, 1, 3, 2))
    for n, k in (('cb', 'conv_b'), ('br', 'lru_br'), ('bi', 'lru_bi'), ('lam', 'lru_lam')):
        put(n, chan(i[k]))
    for n, k in (('qg', 'q_norm_g'), ('kg', 'k_norm_g'), ('hg', 'hgrn_norm_g'), ('mg', 'mlstm_norm_g')):
        put(n, np.tile(i[k], (1, 2))[:, :, None])
    gam = chan(i['hgrn_gamma'])
    for l in range(L):
        par[l, :, PC['gam']:PC['gam'] + 4] = gam.transpose(1, 0, 2).reshape(P, 4)
        par[l, :, PC['lm']] = float(l > 0)
        par[l, :, PC['sink']:PC['sink'] + 4] = i['attn_sinks'][l][None, :]
    put('sinkc', i['attn_sinks'][:, :, None])
    put('ib', i['mlstm_ib'][:, :, None])
    put('fb', i['mlstm_fb'][:, :, None])
    for n, k in (('wr', 'lru_wr'), ('wi', 'lru_wi')):
        for j in range(2):
            for h in range(2):
                a = PC[n] + j * P + 64 * h
                par[:L, 64 * h:64 * h + 64, a:a + 64] = i[k][:, 2 * j + h]
    put('conv', chan(i['state_rglru_conv'].transpose(0, 3, 2, 1)))
    put('h0', chan(i['state_rglru_h'].transpose(0, 2, 1)))
    put('n0', chan(i['state_mlstm_n'].reshape(L, DEC, 256).transpose(0, 2, 1)))
    put('m0', i['state_mlstm_m'].transpose(0, 2, 1))

    def state(a):
        return np.ascontiguousarray(chan(a.transpose(0, 2, 3, 1, 4).reshape(L, 256, DEC, 64)).reshape(L, P, 1024))

    kc = i['cache_swa_k'].reshape(L, DEC, P, P)[:, :, 1:]
    vc = i['cache_swa_v'].reshape(L, DEC, P, P)[:, :, 1:]
    return dict(
        x=_cols(i['x_prompt'][0], i['x_sample'][:, 0]),
        consts=_constants(), rope=_rope_table(), par=par,
        w=_weights(i['w_in'], i['w_out'], i['w_up'], i['w_down'], i['w_ple_gate'], i['w_ple_proj']),
        p=_cols(i['p_prompt'][:, 0], i['p_sample'][:, :, 0]),
        kc=np.ascontiguousarray(kc.transpose(0, 3, 1, 2)), vc=np.ascontiguousarray(vc.transpose(0, 2, 1, 3)),
        hs=state(i['state_hgrn_s']), cs=state(i['state_mlstm_c']))


_OUTS = dict(y=(LAYERS + 1, P, KT, T), so=(LAYERS, P, N_SO), kv=(LAYERS, P, 2, CH), kc=(LAYERS, P, DEC, P), vc=(LAYERS, P, DEC, P),
             hp=(LAYERS, P, 2, P), cp=(LAYERS, P, 2, P), hs=(LAYERS, P, 1024), cs=(LAYERS, P, 1024))


def _results(r):
    L = LAYERS
    y = r['y'][L].transpose(2, 1, 0).reshape(T, D)
    so = r['so']

    def part(name, *shape):
        n = int(np.prod(shape))
        return so[:, :, OC[name]:OC[name] + n].reshape((L, P) + shape)

    def unchan(a):
        return a.swapaxes(1, 2).reshape((L, 256) + a.shape[3:])

    def blocks(a):
        o = np.stack([a[:, 64 * h:64 * h + 64, j, 64 * h:64 * h + 64] for j in range(2) for h in range(2)], axis=1)
        return o[:, None]

    def states(a):
        return unchan(a.reshape(L, P, 2, DEC, 64)).reshape(L, 4, 64, DEC, 64).transpose(0, 3, 1, 2, 4)

    def cache(a):
        return np.roll(a, -1, axis=1).transpose(0, 2, 1, 3).reshape(L, DEC, P, 2, 64)

    kv = r['kv'].transpose(0, 2, 3, 1).reshape(L, 2, 1, CH, 2, 64)
    outs = (
        y[:SEQ].reshape(1, SEQ, D), y[SEQ:].reshape(DEC, 1, D),
        unchan(part('hp', 2)).reshape(L, 1, 256),
        unchan(part('convp', 2, 3)).transpose(0, 2, 1).reshape(L, 1, 3, 256),
        kv[:, 0], kv[:, 1], blocks(r['hp']), blocks(r['cp']),
        unchan(part('np', 2)).reshape(L, 1, 4, 64), part('mp', 1)[:, 0:4, 0].reshape(L, 1, 4),
        unchan(part('hs', 2, DEC)).transpose(0, 2, 1),
        unchan(part('convs', 2, 3, DEC)).transpose(0, 3, 2, 1),
        cache(r['kc'].transpose(0, 3, 2, 1)), cache(r['vc']), states(r['hs']), states(r['cs']),
        unchan(part('ns', 2, DEC)).transpose(0, 2, 1).reshape(L, DEC, 4, 64),
        part('ms', DEC)[:, 0:4].transpose(0, 2, 1))
    return tuple(np.ascontiguousarray(o) for o in outs)


def kernel(**inputs):
    import concourse.bacc as bacc
    from concourse.bass_utils import run_bass_kernel_spmd

    nc = bacc.Bacc("TRN2", target_bir_lowering=False, num_devices=1)
    arrays = {f"in_{k}": v for k, v in _layout({k: np.asarray(v) for k, v in inputs.items()}).items()}
    ins = {k: nc.dram_tensor(k, v.shape, mybir.dt.from_np(v.dtype), kind="ExternalInput").ap() for k, v in arrays.items()}
    outs = {k: nc.dram_tensor(f"out_{k}", s, F32, kind="ExternalOutput").ap() for k, s in _OUTS.items()}
    build(nc, ins['in_x'], ins['in_consts'], ins['in_rope'], ins['in_par'], ins['in_w'], ins['in_p'], ins['in_kc'],
          ins['in_vc'], ins['in_hs'], ins['in_cs'], outs['y'], outs['so'], outs['kv'], outs['kc'], outs['vc'],
          outs['hp'], outs['cp'], outs['hs'], outs['cs'])
    r = run_bass_kernel_spmd(nc, [arrays], core_ids=[0])
    return _results({k: r.results[0][f"out_{k}"] for k in _OUTS})
```
